# Optimizing a Trainium2 kernel written in Bass

```python
import numpy as np
import jax, jax.numpy as jnp
from jax import lax

D_MODEL = 1024
BATCH = 1
SEQ = 256
DEPTH = 2

HEAD_DIM = 64
MOBA_HEADS = D_MODEL // (2 * HEAD_DIM)
NSA_HEADS = D_MODEL // (2 * HEAD_DIM)
NSA_KV_GROUPS = 2
NSA_HPG = NSA_HEADS // NSA_KV_GROUPS
MOBA_BLOCK = 256
MOBA_TOPK = 3
CMP_LEN = 32
CMP_STRIDE = 16
SLC_BLOCK = 64
SLC_TOPN = 16
WINDOW = 512
Q_CHUNK = 128
RMS_EPS = 1e-6
NEG = -1e9
FORCE_BONUS = 1e4

MOBA_W = MOBA_HEADS * HEAD_DIM
NSA_W = NSA_HEADS * HEAD_DIM
KV_W = NSA_KV_GROUPS * HEAD_DIM
SPLITS = [MOBA_W] * 4 + [NSA_W] + [KV_W] * 6 + [3 * NSA_HEADS] + [NSA_W]
D_IN = sum(SPLITS)


def rmsnorm(x, g):
    xf = x.astype(jnp.float32)
    y = xf * lax.rsqrt(jnp.mean(xf * xf, axis=-1, keepdims=True) + RMS_EPS)
    return (y * g.astype(jnp.float32)).astype(x.dtype)

def alibi_slopes(n):
    return jnp.asarray(2.0 ** (-8.0 * np.arange(1, n + 1) / n), dtype=jnp.float32)

def cmp_to_slc_matrix(n_cmp, n_slc):
    i = np.arange(n_cmp)[:, None]
    j = np.arange(n_slc)[None, :]
    start = i * CMP_STRIDE
    end = start + CMP_LEN
    ov = (start < (j + 1) * SLC_BLOCK) & (end > j * SLC_BLOCK)
    return jnp.asarray(ov.astype(np.float32))

def compress_blocks(k, pe, w1, w2):
    B, S, G, dh = k.shape
    T = (S - CMP_LEN) // CMP_STRIDE + 1
    idx = np.arange(T)[:, None] * CMP_STRIDE + np.arange(CMP_LEN)[None, :]
    win = k[:, idx] + pe[:, None, :]
    win = win.transpose(0, 3, 1, 2, 4).reshape(B, G, T, CMP_LEN * dh)
    return jax.nn.gelu(win @ w1) @ w2

def hybrid_mixer(h, w_in, w_out, pe_k, pe_v, w_ck1, w_ck2, w_cv1, w_cv2):
    B, S, _ = h.shape
    dh = HEAD_DIM
    NC = S // Q_CHUNK
    NB = -(-S // MOBA_BLOCK)
    KM = min(MOBA_TOPK, NB)
    NBS = S // SLC_BLOCK
    NS = min(SLC_TOPN, NBS)
    T = (S - CMP_LEN) // CMP_STRIDE + 1
    scale = dh ** -0.5

    u = h @ w_in
    offs = np.cumsum(SPLITS)[:-1].tolist()
    (qm, km, vm, zm, qn, kc, vc, ks, vs, kw, vw, gl, zn) = jnp.split(u, offs, axis=-1)

    def heads(a, n):
        return a.reshape(B, S, n, dh).transpose(0, 2, 1, 3)

    pad = NB * MOBA_BLOCK - S
    qm = heads(qm, MOBA_HEADS) * scale
    km = jnp.pad(heads(km, MOBA_HEADS), ((0, 0), (0, 0), (0, pad), (0, 0))).reshape(B, MOBA_HEADS, NB, MOBA_BLOCK, dh)
    vm = jnp.pad(heads(vm, MOBA_HEADS), ((0, 0), (0, 0), (0, pad), (0, 0))).reshape(B, MOBA_HEADS, NB, MOBA_BLOCK, dh)
    kmean = jnp.mean(km, axis=3)

    G = NSA_KV_GROUPS
    qn = qn.reshape(B, S, G, NSA_HPG, dh).transpose(0, 2, 3, 1, 4) * scale
    kc = compress_blocks(kc.reshape(B, S, G, dh), pe_k, w_ck1, w_ck2)
    vc = compress_blocks(vc.reshape(B, S, G, dh), pe_v, w_cv1, w_cv2)
    ks = heads(ks, G).reshape(B, G, NBS, SLC_BLOCK, dh)
    vs = heads(vs, G).reshape(B, G, NBS, SLC_BLOCK, dh)
    kw = jnp.pad(heads(kw, G), ((0, 0), (0, 0), (WINDOW, 0), (0, 0)))
    vw = jnp.pad(heads(vw, G), ((0, 0), (0, 0), (WINDOW, 0), (0, 0)))
    gates = jax.nn.sigmoid(gl.astype(jnp.float32)).reshape(B, S, G, NSA_HPG, 3)

    slope_m = alibi_slopes(MOBA_HEADS)
    slope_n = alibi_slopes(NSA_HEADS).reshape(G, NSA_HPG)
    M = cmp_to_slc_matrix(T, NBS)
    hidx = jnp.arange(MOBA_HEADS)[:, None, None]
    gidx = jnp.arange(G)[:, None, None]

    def chunk(i):
        b = i // NC
        s0 = (i % NC) * Q_CHUNK
        t = s0 + jnp.arange(Q_CHUNK)
        take = lambda a: lax.dynamic_index_in_dim(a, b, 0, keepdims=False)

        q = lax.dynamic_slice_in_dim(take(qm), s0, Q_CHUNK, axis=1)
        Kb, Vb, Kmean = take(km), take(vm), take(kmean)
        cur = s0 // MOBA_BLOCK
        gsc = jnp.einsum('hqd,hnd->hqn', q, Kmean).astype(jnp.float32)
        gsc = jnp.where(jnp.arange(NB) < cur, gsc, NEG)
        _, sel = lax.top_k(gsc, KM)
        sel_ok = jnp.arange(KM) < cur
        k_sel = Kb[hidx, sel]
        v_sel = Vb[hidx, sel]
        s_sel = jnp.einsum('hqd,hqkbd->hqkb', q, k_sel).astype(jnp.float32)
        pos_sel = sel[..., None] * MOBA_BLOCK + jnp.arange(MOBA_BLOCK)
        d_sel = (t[None, :, None, None] - pos_sel).astype(jnp.float32)
        s_sel = jnp.where(sel_ok[None, None, :, None], s_sel - slope_m[:, None, None, None] * d_sel, NEG)
        k_own = lax.dynamic_index_in_dim(Kb, cur, 1, keepdims=False)
        v_own = lax.dynamic_index_in_dim(Vb, cur, 1, keepdims=False)
        s_own = jnp.einsum('hqd,hkd->hqk', q, k_own).astype(jnp.float32)
        d_own = t[:, None] - (cur * MOBA_BLOCK + jnp.arange(MOBA_BLOCK))[None, :]
        s_own = jnp.where(d_own >= 0, s_own - slope_m[:, None, None] * d_own.astype(jnp.float32), NEG)
        logits = jnp.concatenate([s_sel.reshape(MOBA_HEADS, Q_CHUNK, KM * MOBA_BLOCK), s_own], axis=-1)
        p = jax.nn.softmax(logits, axis=-1).astype(v_own.dtype)
        p_sel = p[..., :KM * MOBA_BLOCK].reshape(MOBA_HEADS, Q_CHUNK, KM, MOBA_BLOCK)
        o_m = (jnp.einsum('hqkb,hqkbd->hqd', p_sel, v_sel)
               + jnp.einsum('hqb,hbd->hqd', p[..., KM * MOBA_BLOCK:], v_own))
        o_m = o_m.transpose(1, 0, 2).reshape(Q_CHUNK, MOBA_W)

        qg = lax.dynamic_slice_in_dim(take(qn), s0, Q_CHUNK, axis=2)
        kcb, vcb = take(kc), take(vc)
        s_c = jnp.einsum('gjqd,gtd->gjqt', qg, kcb).astype(jnp.float32)
        d_c = t[:, None] - (jnp.arange(T) * CMP_STRIDE + CMP_LEN - 1)[None, :]
        ok_c = d_c >= 0
        s_c = jnp.where(ok_c, s_c - slope_n[:, :, None, None] * d_c.astype(jnp.float32), NEG)
        p_c = jax.nn.softmax(s_c, axis=-1) * ok_c
        o_c = jnp.einsum('gjqt,gtd->gjqd', p_c.astype(vcb.dtype), vcb)
        imp = jnp.einsum('gjqt,tn->gqn', p_c, M)
        blk = t // SLC_BLOCK
        jn = jnp.arange(NBS)[None, :]
        forced = (jn == 0) | (jn == blk[:, None]) | (jn == blk[:, None] - 1)
        imp = jnp.where(forced, FORCE_BONUS, imp)
        imp = jnp.where(jn <= blk[:, None], imp, NEG)
        _, sidx = lax.top_k(imp, NS)
        s_valid = sidx <= blk[None, :, None]
        ksb = take(ks)[gidx, sidx]
        vsb = take(vs)[gidx, sidx]
        s_s = jnp.einsum('gjqd,gqnbd->gjqnb', qg, ksb).astype(jnp.float32)
        d_s = t[None, :, None, None] - (sidx[..., None] * SLC_BLOCK + jnp.arange(SLC_BLOCK))
        ok_s = (d_s >= 0) & s_valid[..., None]
        s_s = jnp.where(ok_s[:, None], s_s - slope_n[:, :, None, None, None] * d_s[:, None].astype(jnp.float32), NEG)
        p_s = jax.nn.softmax(s_s.reshape(G, NSA_HPG, Q_CHUNK, NS * SLC_BLOCK), axis=-1)
        p_s = p_s.reshape(G, NSA_HPG, Q_CHUNK, NS, SLC_BLOCK).astype(vsb.dtype)
        o_s = jnp.einsum('gjqnb,gqnbd->gjqd', p_s, vsb)
        kwb = lax.dynamic_slice_in_dim(take(kw), s0, WINDOW + Q_CHUNK, axis=1)
        vwb = lax.dynamic_slice_in_dim(take(vw), s0, WINDOW + Q_CHUNK, axis=1)
        s_w = jnp.einsum('gjqd,gkd->gjqk', qg, kwb).astype(jnp.float32)
        pos_w = s0 - WINDOW + jnp.arange(WINDOW + Q_CHUNK)
        d_w = t[:, None] - pos_w[None, :]
        ok_w = (d_w >= 0) & (d_w < WINDOW) & (pos_w >= 0)[None, :]
        s_w = jnp.where(ok_w, s_w - slope_n[:, :, None, None] * d_w.astype(jnp.float32), NEG)
        p_w = jax.nn.softmax(s_w, axis=-1).astype(vwb.dtype)
        o_w = jnp.einsum('gjqk,gkd->gjqd', p_w, vwb)
        g = lax.dynamic_slice_in_dim(take(gates), s0, Q_CHUNK, axis=0).transpose(1, 2, 0, 3)
        g = g.astype(o_c.dtype)
        o_n = g[..., 0:1] * o_c + g[..., 1:2] * o_s + g[..., 2:3] * o_w
        o_n = o_n.transpose(2, 0, 1, 3).reshape(Q_CHUNK, NSA_W)
        return o_m, o_n

    o_m, o_n = lax.map(chunk, jnp.arange(B * NC))
    o_m = o_m.reshape(B, S, MOBA_W)
    o_n = o_n.reshape(B, S, NSA_W)
    y = jnp.concatenate([o_m * jax.nn.silu(zm), o_n * jax.nn.silu(zn)], axis=-1)
    return y @ w_out

def first_inputs(seed: int = 0) -> dict:
    key = jax.random.key(seed)
    ks = jax.random.split(key, 16)
    L, D, dh = DEPTH, D_MODEL, HEAD_DIM
    nrm = lambda k, shape, s: jax.random.normal(k, shape, jnp.float32) * s
    return {
        "x": nrm(ks[0], (BATCH, SEQ, D), 1.0),
        "c": nrm(ks[1], (BATCH, D), 1.0),
        "w_ada": nrm(ks[2], (L, D, 3 * D), D ** -0.5),
        "b_ada": nrm(ks[3], (L, 3 * D), 0.01),
        "g_pre": 1.0 + nrm(ks[4], (L, D), 0.1),
        "g_post": 1.0 + nrm(ks[5], (L, D), 0.1),
        "w_in": nrm(ks[6], (L, D, D_IN), D ** -0.5),
        "w_out": nrm(ks[7], (L, D, D), D ** -0.5),
        "pe_k": nrm(ks[8], (L, CMP_LEN, dh), 0.1),
        "pe_v": nrm(ks[9], (L, CMP_LEN, dh), 0.1),
        "w_ck1": nrm(ks[10], (L, CMP_LEN * dh, dh), (CMP_LEN * dh) ** -0.5),
        "w_ck2": nrm(ks[11], (L, dh, dh), dh ** -0.5),
        "w_cv1": nrm(ks[12], (L, CMP_LEN * dh, dh), (CMP_LEN * dh) ** -0.5),
        "w_cv2": nrm(ks[13], (L, dh, dh), dh ** -0.5),
    }

def first_block(x, c, w_ada, b_ada, g_pre, g_post, w_in, w_out, pe_k, pe_v, w_ck1, w_ck2, w_cv1, w_cv2):
    D = x.shape[-1]
    cs = jax.nn.silu(c)
    for l in range(DEPTH):
        mod = cs @ w_ada[l] + b_ada[l]
        shift, scale, gate = mod[:, None, :D], mod[:, None, D:2 * D], mod[:, None, 2 * D:]
        h = rmsnorm(x, g_pre[l]) * (1.0 + scale) + shift
        y = hybrid_mixer(h, w_in[l], w_out[l], pe_k[l], pe_v[l], w_ck1[l], w_ck2[l], w_cv1[l], w_cv2[l])
        x = x + gate * rmsnorm(y, g_post[l])
    return x


GRID_W = 64
NA_HEADS = 16
NA_HEAD_DIM = D_MODEL // NA_HEADS
NA_WIN_H = 8
NA_WIN_W = 16
MLA_HEADS = 16
MLA_Q_LORA = D_MODEL // 4
MLA_KV_LORA = D_MODEL // 8
MLA_NOPE = 64
MLA_ROPE = 32
MLA_V = 64
ROPE_THETA = 10000.0
Q_BLOCK = 128
FFN_DIM = 2816
N_EXPERTS = 8
TOP_K = 2
EXPERT_DIM = 1792
NORM_EPS = 1e-6


def _rmsnorm(x):
    xf = x.astype(jnp.float32)
    y = xf * lax.rsqrt(jnp.mean(xf * xf, axis=-1, keepdims=True) + NORM_EPS)
    return y.astype(x.dtype)

def _modulate(x, shift, scale):
    return _rmsnorm(x) * (1 + scale[:, None, :]) + shift[:, None, :]

def _swiglu(h, w_gu, w_down):
    gate, up = jnp.split(h @ w_gu, 2, axis=-1)
    return (jax.nn.silu(gate) * up) @ w_down

def _rope_2d_tables(seq_len):
    t = jnp.arange(seq_len)
    row = (t // GRID_W).astype(jnp.float32)
    col = (t % GRID_W).astype(jnp.float32)
    n = MLA_ROPE // 4
    inv = ROPE_THETA ** (-jnp.arange(n, dtype=jnp.float32) / n)
    ang = jnp.concatenate([row[:, None] * inv, col[:, None] * inv], axis=-1)
    return jnp.cos(ang), jnp.sin(ang)

def _apply_rope(x, cos, sin):
    x1 = x[..., 0::2].astype(jnp.float32)
    x2 = x[..., 1::2].astype(jnp.float32)
    out = jnp.stack([x1 * cos - x2 * sin, x1 * sin + x2 * cos], axis=-1)
    return out.reshape(x.shape).astype(x.dtype)

def _neighborhood_attention(h, w_qkv, rpb, w_o):
    B, S, D = h.shape
    rows = S // GRID_W
    kh = min(NA_WIN_H, rows)
    kw = min(NA_WIN_W, GRID_W)
    qkv = (h @ w_qkv).reshape(B, rows, GRID_W, 3, NA_HEADS, NA_HEAD_DIM)
    q = qkv[:, :, :, 0] * (NA_HEAD_DIM ** -0.5)
    k = qkv[:, :, :, 1]
    v = qkv[:, :, :, 2]
    cols = jnp.arange(GRID_W)
    col_idx = jnp.clip(cols - kw // 2, 0, GRID_W - kw)[:, None] + jnp.arange(kw)[None, :]
    dc_idx = col_idx - cols[:, None] + NA_WIN_W - 1

    def row_block(r):
        rs = jnp.clip(r - kh // 2, 0, rows - kh)
        q_r = lax.dynamic_index_in_dim(q, r, axis=1, keepdims=False)
        k_g = lax.dynamic_slice_in_dim(k, rs, kh, axis=1)[:, :, col_idx]
        v_g = lax.dynamic_slice_in_dim(v, rs, kh, axis=1)[:, :, col_idx]
        dr_idx = rs + jnp.arange(kh) - r + NA_WIN_H - 1
        bias = rpb[:, dr_idx[None, :, None], dc_idx[:, None, :]]
        s = jnp.einsum('bqhd,bkqjhd->bhqkj', q_r, k_g).astype(jnp.float32) + bias.astype(jnp.float32)
        p = jax.nn.softmax(s.reshape(B, NA_HEADS, GRID_W, kh * kw), axis=-1)
        p = p.reshape(s.shape).astype(v.dtype)
        return jnp.einsum('bhqkj,bkqjhd->bqhd', p, v_g)

    o = lax.map(row_block, jnp.arange(rows))
    o = jnp.moveaxis(o, 0, 1).reshape(B, S, D)
    return o @ w_o

def _mla(h, w_down, q_norm, w_uq, kv_norm, w_ukv, w_o):
    B, S, D = h.shape
    down = h @ w_down
    c_q = _rmsnorm(down[..., :MLA_Q_LORA]) * q_norm
    c_kv = _rmsnorm(down[..., MLA_Q_LORA:MLA_Q_LORA + MLA_KV_LORA]) * kv_norm
    k_rope = down[..., MLA_Q_LORA + MLA_KV_LORA:]
    q = (c_q @ w_uq).reshape(B, S, MLA_HEADS, MLA_NOPE + MLA_ROPE)
    kv = (c_kv @ w_ukv).reshape(B, S, MLA_HEADS, MLA_NOPE + MLA_V)
    k_nope, v = kv[..., :MLA_NOPE], kv[..., MLA_NOPE:]
    cos, sin = _rope_2d_tables(S)
    q_nope = q[..., :MLA_NOPE]
    q_rope = _apply_rope(q[..., MLA_NOPE:], cos[:, None, :], sin[:, None, :])
    k_rope = _apply_rope(k_rope, cos, sin)
    scale = (MLA_NOPE + MLA_ROPE) ** -0.5
    nb = S // Q_BLOCK

    def to_blocks(t):
        return jnp.moveaxis(t.reshape(B, nb, Q_BLOCK, *t.shape[2:]), 1, 0)

    def q_block(blk):
        qn, qr = blk
        s = (jnp.einsum('bqhd,bkhd->bhqk', qn, k_nope)
             + jnp.einsum('bqhr,bkr->bhqk', qr, k_rope)).astype(jnp.float32) * scale
        p = jax.nn.softmax(s, axis=-1).astype(v.dtype)
        return jnp.einsum('bhqk,bkhd->bqhd', p, v)

    o = lax.map(q_block, (to_blocks(q_nope), to_blocks(q_rope)))
    o = jnp.moveaxis(o, 0, 1).reshape(B, S, MLA_HEADS * MLA_V)
    return o @ w_o

def _moe(h, w_router, w_gu, w_down):
    B, S, D = h.shape
    hf = h.reshape(B * S, D)
    probs = jax.nn.softmax((hf @ w_router).astype(jnp.float32), axis=-1)
    vals, idx = lax.top_k(probs, TOP_K)
    wts = vals / jnp.sum(vals, axis=-1, keepdims=True)
    combine = jnp.sum(jax.nn.one_hot(idx, N_EXPERTS, dtype=jnp.float32) * wts[..., None], axis=1)
    combine = combine.astype(h.dtype)
    y = jnp.zeros_like(hf)
    for e in range(N_EXPERTS):
        y = y + combine[:, e:e + 1] * _swiglu(hf, w_gu[e], w_down[e])
    return y.reshape(B, S, D)

def second_inputs(seed: int = 0) -> dict:
    key = jax.random.key(seed)
    ks = iter(jax.random.split(key, 32))
    n_even = (DEPTH + 1) // 2
    n_odd = DEPTH // 2
    D = D_MODEL

    def nrm(shape, fan_in, mult=1.0):
        return jax.random.normal(next(ks), shape, jnp.float32) * (mult * fan_in ** -0.5)

    return {
        "x": jax.random.normal(next(ks), (BATCH, SEQ, D), jnp.float32),
        "c": jax.random.normal(next(ks), (BATCH, D), jnp.float32),
        "w_ada": nrm((DEPTH, D, 6 * D), D, 0.5),
        "b_ada": 0.02 * jax.random.normal(next(ks), (DEPTH, 6 * D), jnp.float32),
        "na_w_qkv": nrm((n_even, D, 3 * D), D),
        "na_rpb": 0.1 * jax.random.normal(next(ks), (n_even, NA_HEADS, 2 * NA_WIN_H - 1, 2 * NA_WIN_W - 1), jnp.float32),
        "na_w_o": nrm((n_even, D, D), D),
        "ffn_w_gu": nrm((n_even, D, 2 * FFN_DIM), D),
        "ffn_w_down": nrm((n_even, FFN_DIM, D), FFN_DIM),
        "mla_w_down": nrm((n_odd, D, MLA_Q_LORA + MLA_KV_LORA + MLA_ROPE), D),
        "mla_q_norm": 1.0 + 0.01 * jax.random.normal(next(ks), (n_odd, MLA_Q_LORA), jnp.float32),
        "mla_w_uq": nrm((n_odd, MLA_Q_LORA, MLA_HEADS * (MLA_NOPE + MLA_ROPE)), MLA_Q_LORA),
        "mla_kv_norm": 1.0 + 0.01 * jax.random.normal(next(ks), (n_odd, MLA_KV_LORA), jnp.float32),
        "mla_w_ukv": nrm((n_odd, MLA_KV_LORA, MLA_HEADS * (MLA_NOPE + MLA_V)), MLA_KV_LORA),
        "mla_w_o": nrm((n_odd, MLA_HEADS * MLA_V, D), MLA_HEADS * MLA_V),
        "moe_w_router": nrm((n_odd, D, N_EXPERTS), D),
        "moe_w_gu": nrm((n_odd, N_EXPERTS, D, 2 * EXPERT_DIM), D),
        "moe_w_down": nrm((n_odd, N_EXPERTS, EXPERT_DIM, D), EXPERT_DIM),
        "final_norm": 1.0 + 0.01 * jax.random.normal(next(ks), (D,), jnp.float32),
    }

def second_block(x, c, w_ada, b_ada, na_w_qkv, na_rpb, na_w_o, ffn_w_gu, ffn_w_down,
              mla_w_down, mla_q_norm, mla_w_uq, mla_kv_norm, mla_w_ukv, mla_w_o,
              moe_w_router, moe_w_gu, moe_w_down, final_norm):
    c_act = jax.nn.silu(c)
    for i in range(DEPTH):
        j = i // 2
        mod = c_act @ w_ada[i] + b_ada[i]
        sh_a, sc_a, g_a, sh_f, sc_f, g_f = jnp.split(mod, 6, axis=-1)
        h = _modulate(x, sh_a, sc_a)
        if i % 2 == 0:
            m = _neighborhood_attention(h, na_w_qkv[j], na_rpb[j], na_w_o[j])
        else:
            m = _mla(h, mla_w_down[j], mla_q_norm[j], mla_w_uq[j], mla_kv_norm[j], mla_w_ukv[j], mla_w_o[j])
        x = x + g_a[:, None, :] * m
        h = _modulate(x, sh_f, sc_f)
        if i % 2 == 0:
            f = _swiglu(h, ffn_w_gu[j], ffn_w_down[j])
        else:
            f = _moe(h, moe_w_router[j], moe_w_gu[j], moe_w_down[j])
        x = x + g_f[:, None, :] * f
    return _rmsnorm(x) * final_norm


def setup_inputs(seed=0):
    out = dict(first_inputs(seed))
    for name, value in second_inputs(seed + 1).items():
        if name != "x":
            out[name + "_2"] = value
    return out


def reference(
    x, c, w_ada, b_ada, g_pre, g_post, w_in, w_out, pe_k, pe_v, w_ck1, w_ck2, w_cv1, w_cv2, c_2,
    w_ada_2, b_ada_2, na_w_qkv_2, na_rpb_2, na_w_o_2, ffn_w_gu_2, ffn_w_down_2, mla_w_down_2,
    mla_q_norm_2, mla_w_uq_2, mla_kv_norm_2, mla_w_ukv_2, mla_w_o_2, moe_w_router_2, moe_w_gu_2,
    moe_w_down_2, final_norm_2,
):
    x = first_block(
        x, c, w_ada, b_ada, g_pre, g_post, w_in, w_out, pe_k, pe_v, w_ck1, w_ck2, w_cv1, w_cv2,
    )
    return second_block(
        x, c_2, w_ada_2, b_ada_2, na_w_qkv_2, na_rpb_2, na_w_o_2, ffn_w_gu_2, ffn_w_down_2,
        mla_w_down_2, mla_q_norm_2, mla_w_uq_2, mla_kv_norm_2, mla_w_ukv_2, mla_w_o_2,
        moe_w_router_2, moe_w_gu_2, moe_w_down_2, final_norm_2,
    )


_drawn_inputs = setup_inputs


def setup_inputs(seed=0):
    import zlib

    import numpy as np

    out = dict(_drawn_inputs(seed))
    spreads = {}
    factors = {'pe_k': 8.0,
     'na_rpb_2': 8.0,
     'mla_q_norm_2': 8.0,
     'mla_kv_norm_2': 8.0,
     'final_norm_2': 5.639}
    for name, (base, spread) in spreads.items():
        noise = np.random.default_rng([zlib.crc32(name.encode()), seed]).standard_normal(out[name].shape)
        drawn = base * np.exp(spread * noise) if base else spread * noise
        out[name] = __import__('jax').numpy.asarray(drawn.astype(out[name].dtype))
    for name, factor in factors.items():
        out[name] = (out[name] * factor).astype(out[name].dtype)
    return out
```

```python
from contextlib import ExitStack

import numpy as np
import concourse.bass as bass
from concourse import mybir

F32 = mybir.dt.float32
F32R = mybir.dt.float32r
ALU = mybir.AluOpType
ACT = mybir.ActivationFunctionType
AX_X = mybir.AxisListType.X

P = 128
D = 1024
S = 256
MT = S // P
KT = D // P
HD = 64
STEP = 2048
RAW = 6
SPL = 3
EPS = 1e-6
FAR = 1e12
QS = HD ** -0.5
MS = 96 ** -0.5
NEXP = 8
FFN_SLOTS = 11
MOE_SLOTS = 7
T_CMP = 15

PHASES = ["pre", "lay", "na", "ffn", "mla", "rt", "moe", "end"]
REPS = {"lay": 2, "moe": NEXP}


def ada_steps(j):
    return [("ada", j, 0), ("ada", j, 1)]


def layer_steps():
    out, n = [], 0
    for s in range(8):
        out += [("w", n), ("w", n + 1)]
        n += 2
        if s < 6:
            out += ada_steps(s)
    out.append(("ck",))
    return out + [("w", n + i) for i in range(4)]


def na_steps():
    out = []
    for s in range(6):
        out += [("w", 2 * s), ("w", 2 * s + 1)] + ada_steps(s)
    return out + [("w", 12 + i) for i in range(4)]


def mlp_steps(slots, ada):
    out, n = [], 0
    for s in range(slots):
        out += [("w", n), ("w", n + 1)]
        n += 2
        if ada:
            out += ada_steps(s)
        if s >= 1:
            out.append(("w", n))
            n += 1
    if ada:
        out += ada_steps(slots)
    out.append(("w", n))
    return out


STEPS = {
    "pre": [x for j in range(6) for x in ada_steps(j)],
    "lay": layer_steps(),
    "na": na_steps(),
    "ffn": mlp_steps(FFN_SLOTS, True),
    "mla": [("w", i) for i in range(9)],
    "rt": [],
    "moe": mlp_steps(MOE_SLOTS, False),
    "end": [],
}
SPLITS = {p: sum(x[0] == "w" for x in STEPS[p]) for p in PHASES}
NSTEPS = sum(len(STEPS[p]) * REPS.get(p, 1) for p in PHASES)


def up_proj_split(s):
    return 0 if s == 0 else 3 * s - 1


def down_split(s, slots):
    return 3 * s + 4 if s < slots - 1 else 3 * slots - 1


def ring_plan(size, lengths):
    place, need, start = {}, {}, 0
    owner = [None] * size
    total = 0
    for p in PHASES:
        n, reps = lengths[p], REPS.get(p, 1)
        pad = -n % size if reps > 1 else 0
        place[p] = [(start + i) % size for i in range(n)]
        need[p] = [None] * n
        for _ in range(reps):
            for i in range(n):
                last = owner[place[p][i]]
                if last is not None:
                    k = last + 1 - total
                    need[p][i] = k if need[p][i] is None else max(need[p][i], k)
                owner[place[p][i]] = total + i
            total += n
        start = (start + n + pad) % size
    return place, need


RAW_AT, RAW_NEED = ring_plan(RAW, {p: len(STEPS[p]) for p in PHASES})
SPL_AT, SPL_NEED = ring_plan(SPL, SPLITS)
STEP_OF_SPLIT = {p: [i for i, x in enumerate(STEPS[p]) if x[0] == "w"] for p in PHASES}

COUNTS = {
    "act": {"ffn": 22, "moe": 14},
    "act_hi": {"ffn": 22, "moe": 14},
    "ada_sum": {"pre": 6, "lay": 6, "na": 6, "ffn": 12},
    "bank0": {"lay": 6, "na": 4, "ffn": 8, "moe": 5},
    "bank1": {"lay": 5, "na": 4, "ffn": 7, "moe": 5},
    "bank2": {"lay": 5, "na": 4, "ffn": 7, "moe": 4},
    "bank3": {"pre": 6, "lay": 6, "na": 6, "ffn": 12},
    "brow": {"pre": 1, "lay": 1, "na": 1, "ffn": 2},
    "c": {"mla": 2},
    "c_f": {"mla": 1},
    "c_hi": {"mla": 1},
    "c_t": {"mla": 1},
    "cexp": {"lay": 2},
    "clogits": {"lay": 2},
    "cmp1": {"lay": 1},
    "cmp2": {"lay": 1},
    "cmp3": {"lay": 1},
    "cmp_act": {"lay": 1},
    "cmp_kv": {"lay": 2},
    "cmp_tanh": {"lay": 1},
    "cmp_u": {"lay": 1},
    "cn": {"mla": 4},
    "consts": {"pre": 2},
    "cout": {"lay": 2},
    "cout_used": {"lay": 2},
    "cprobs": {"lay": 2},
    "cprobs_t": {"lay": 2},
    "cpt": {"lay": 2},
    "cs_tanh": {"pre": 1},
    "cscores": {"lay": 2},
    "down_used": {"mla": 2},
    "dve": {"pre": 39, "lay": 84, "na": 50, "ffn": 103, "mla": 28, "rt": 32, "moe": 14, "end": 2},
    "final": {"end": 2},
    "fnorm": {"rt": 1},
    "g_tanh": {"lay": 1},
    "gg": {"lay": 1},
    "gpost": {"lay": 1},
    "h": {"lay": 8, "na": 8, "ffn": 4, "mla": 8, "rt": 4},
    "h_hi": {"lay": 8, "na": 8, "ffn": 4, "mla": 8, "rt": 4},
    "hb": {"lay": 4, "na": 4, "ffn": 4, "mla": 4, "rt": 4},
    "hi": {"lay": 20, "na": 16, "ffn": 33, "mla": 9, "moe": 21},
    "kk": {"lay": 7},
    "lc_in": {"pre": 1},
    "logits": {"lay": 48, "na": 32, "mla": 32},
    "lp": {"lay": 1},
    "mean_sq": {"lay": 2, "na": 1, "ffn": 1, "mla": 3, "rt": 1, "end": 1},
    "mk_sum": {"mla": 1},
    "mkv": {"mla": 5},
    "mq": {"mla": 4},
    "mr": {"mla": 2},
    "o_used": {"lay": 6, "na": 4, "mla": 4},
    "par_in": {"pre": 1},
    "probs": {"lay": 48, "na": 32, "mla": 32},
    "probs_t": {"lay": 48, "na": 32, "mla": 32},
    "pt": {"lay": 48, "na": 32, "mla": 32},
    "pv": {"lay": 48, "na": 32, "mla": 32},
    "raw_in0": {"pre": 2, "lay": 6, "na": 5, "ffn": 10, "mla": 1, "moe": 4},
    "raw_in1": {"pre": 2, "lay": 6, "na": 5, "ffn": 9, "mla": 2, "moe": 3},
    "raw_in2": {"pre": 2, "lay": 6, "na": 5, "ffn": 9, "mla": 2, "moe": 3},
    "raw_in3": {"pre": 2, "lay": 5, "na": 5, "ffn": 9, "mla": 2, "moe": 3},
    "raw_in4": {"pre": 2, "lay": 5, "na": 4, "ffn": 10, "mla": 1, "moe": 4},
    "raw_in5": {"pre": 2, "lay": 5, "na": 4, "ffn": 10, "mla": 1, "moe": 4},
    "raw_used": {"pre": 12, "lay": 33, "na": 28, "ffn": 57, "mla": 9, "moe": 21},
    "rexp": {"rt": 2},
    "rmax": {"rt": 2},
    "route_read": {"rt": 2},
    "router": {"rt": 2},
    "rp_in": {"na": 1},
    "rstd": {"lay": 2, "na": 1, "ffn": 1, "mla": 2, "rt": 1, "end": 1},
    "scores": {"lay": 48, "na": 32, "mla": 32},
    "split_used": {"pre": 3, "lay": 20, "na": 16, "ffn": 33, "mla": 9, "moe": 21},
    "sq": {"lay": 3, "na": 2, "ffn": 2, "mla": 6, "rt": 2, "end": 2},
    "stored": {"end": 2},
    "tanh": {"ffn": 22, "moe": 14},
    "turned": {"lay": 8, "na": 8, "ffn": 4, "mla": 8, "rt": 4},
    "vb": {"lay": 1},
    "x": {"pre": 1, "lay": 2, "na": 2, "ffn": 2, "mla": 2},
    "x_in": {"pre": 1},
    "x_last": {"end": 2},
    "xn": {"lay": 2, "na": 2, "ffn": 2, "mla": 2, "rt": 2},
    "y": {"pre": 1, "lay": 4},
    "y_used": {"moe": 2},
    "ysq": {"lay": 4},
    "z_tanh": {"lay": 4},
}


class Signals:

    def __init__(self, nc, ctx):
        self.nc, self.ctx, self.sems, self.made = nc, ctx, {}, {}

    def sem(self, name):
        if name not in self.sems:
            self.sems[name] = self.ctx.enter_context(self.nc.semaphore(name))
        return self.sems[name]

    def value(self, name, phase, rep, k):
        c = COUNTS.get(name, {})
        base = 0
        for p in PHASES:
            if p == phase:
                break
            base += c.get(p, 0) * REPS.get(p, 1)
        per = c.get(phase, 0)
        return base + k + (rep * per if per and not isinstance(rep, int) else 0)


class Count:

    def __init__(self, signals):
        self.sg = signals
        self.phase, self.rep = "pre", 0
        self.own = {}

    def enter(self, phase, rep=0):
        self.phase, self.rep, self.own = phase, rep, {}

    def at(self, name, k, unit=1):
        v = self.sg.value(name, self.phase, self.rep, k)
        assert not isinstance(v, int) or v > 0, (name, self.phase, k, v)
        return self.sg.sem(name), v * unit

    def inc(self, name, unit=1):
        d = self.sg.made.setdefault(name, {})
        d[self.phase] = d.get(self.phase, 0) + 1
        self.own[name] = self.own.get(name, 0) + 1
        return self.sg.sem(name), unit

    def last(self, name):
        return self.at(name, self.own[name])


def build(nc, dram):
    ctx = ExitStack()
    with ctx:
        at = [nc.sbuf_base + (-nc.sbuf_base) % 64]

        def sb(name, shape, dt=F32, offset=None):
            size = int(np.prod(shape[1:])) * 4
            size += -size % 32
            if offset is None:
                offset = at[0]
                at[0] += size
            return nc.alloc_sbuf_tensor_at(name, shape, dt, offset=offset)

        raw = sb("raw", [P, RAW, STEP])
        wh = sb("w_hi", [P, SPL, STEP], F32R)
        wl = sb("w_lo", [P, SPL, STEP], F32R)
        hh = sb("h_hi", [P, KT, S], F32R)
        hl = sb("h_lo", [P, KT, S], F32R)
        x = sb("x", [P, MT, D])
        gate = [sb("gate0", [P, D]), sb("gate1", [P, D])]
        acc = sb("acc", [P, 2, 512])
        brow = sb("brow", [1, D])
        par = sb("par", [P, dram["par"].shape[1]])
        cs = sb("cs", [P, 2, KT])
        csc = sb("cs_cur", [P, KT])
        modc = sb("modc", [P, 3, 16])
        ab = sb("ab", [P, 2, KT])
        st = sb("st", [P, 256])
        ones = sb("ones", [P, P])
        spare = sb("spare", [P, 8])
        work = at[0]
        hb = sb("hb", [P, 4, S])
        pt = sb("pt", [P, 2, S])
        lg = sb("lg", [P, 2, S], offset=work)
        pr = sb("pr", [P, 2, S], offset=work + 2048)
        gate2_at = at[0]
        gate.append(sb("gate2", [P, D]))
        arena = at[0]
        top = nc.sbuf_top

        def region(start):
            pos = [start]

            def take(name, shape, dt=F32):
                off = pos[0]
                size = int(np.prod(shape[1:])) * 4
                pos[0] += size + (-size % 32)
                assert pos[0] <= top, (name, pos[0] - top)
                return nc.alloc_sbuf_tensor_at(name, shape, dt, offset=off)
            return take, pos

        take, pos = region(gate2_at)
        lc = take("lc", [P, dram["lc"].shape[1]])
        y_at = pos[0]
        y = take("y", [P, MT, D])
        qm = take("qm", [P, 4, S])
        km = take("km", [P, 4, S])
        vm = take("vm", [P, MT, 512])
        zm = take("zm", [P, MT, 512])
        qn = take("qn", [P, 4, S])
        ksw = take("ksw", [P, 2, S])
        vsw = take("vsw", [P, MT, 280])
        zn_at = pos[0]
        zn = take("zn", [P, MT, 512])
        lpc = take("lpc", [P, 184])
        cw = take("cw", [P, 512])
        kk_at = pos[0]
        kk = take("kk", [P, 2, 2, S])
        xn_l = nc.alloc_sbuf_tensor_at("xn_l", [P, MT, D], F32, offset=y_at)
        gpost = nc.alloc_sbuf_tensor_at("gpost", [P, D], F32, offset=zn_at)
        vb = nc.alloc_sbuf_tensor_at("vb", [P, 512], F32, offset=kk_at)
        tmpo = nc.alloc_sbuf_tensor_at("tmpo", [P, 512], F32, offset=kk_at + 2048)
        take, pos = region(gate2_at)
        rp = take("rp", [P, 16 * 6, 64])
        naq = take("naq", [P, 8, S])
        nak = take("nak", [P, 8, S])
        nav = take("nav", [P, MT, D])
        o_at = pos[0]
        nao = take("nao", [P, MT, D])
        xn_n = nc.alloc_sbuf_tensor_at("xn_n", [P, MT, D], F32, offset=o_at)
        take, pos = region(arena)
        ysum = take("ysum", [P, MT, D])
        xn_f = take("xn_f", [P, MT, D])
        ah = take("a_hi", [P, 2, 2, S], F32R)
        al = take("a_lo", [P, 2, 2, S], F32R)
        fnorm = take("fnorm", [P, D])
        rw = take("rw", [P, 320])
        take, pos = region(arena)
        dsb = take("dsb", [P, MT, 416])
        cn = take("cn", [P, MT, 512])
        mq = take("mq", [P, 8, S])
        mr = take("mr", [P, 4, S])
        mt2 = take("mt2", [P, 4, S])
        kr = take("kr", [P, S])
        mk = take("mk", [P, 8, S])
        mv = take("mv", [P, MT, D])
        mo = take("mo", [P, MT, D])
        xn_m = nc.alloc_sbuf_tensor_at("xn_m", [P, MT, D], F32, offset=arena)

        PS = ctx.enter_context(nc.psum_tensor("PS", [P, 8, 512], F32))

        pc = {}
        o = 0
        for name, n in dram["par_cols"]:
            pc[name] = (o, n)
            o += n

        def pcol(name, a=0, b=None):
            s0, n = pc[name]
            return par[:, s0 + a:s0 + (n if b is None else b)]

        lcc = {}
        o = 0
        for name, n in dram["lc_cols"]:
            lcc[name] = (o, n)
            o += n

        def lcol(name):
            s0, n = lcc[name]
            return lc[:, s0:s0 + n]

        ident = pcol("ident")
        alibi = lcol("alibi").rearrange("p (h k) -> p h k", h=8)
        alibi_c = lcol("alibi_c").rearrange("p (m h t) -> p m h t", m=2, h=8)
        ok_c = lcol("ok_c").rearrange("p (m t) -> p m t", m=2)
        rep_sel = lcol("rep_sel").rearrange("p (g q) -> p g q", g=2)
        mask8 = lcol("mask8")
        LP = {}
        o = 0
        for name, n in (("gpre", 8), ("bcol", 16), ("pek", 16), ("pev", 16), ("ck2", 64), ("cv2", 64)):
            LP[name] = lpc[:, o:o + n]
            o += n
        lpall = pcol("lpall").rearrange("p (l n) -> p l n", l=2)

        SQ = slice(0, 8)
        s_sq, s_ms, s_rs, s_half = 0, 8, 16, 24
        mn = lambda u: st[:, 32 + u:33 + u]
        sm = lambda u: st[:, 96 + u:97 + u]
        rinv = lambda a, b: st[:, 160 + a:160 + b]
        wgt = lambda: st[:, 224:232]

        sg = Signals(nc, ctx)
        settled = sg.sem("settled")

        def attention_units(kind):
            out = []
            groups = {"lay": [(b, m) for b in ("moba", "sel", "win") for m in range(2)],
                      "na": [(b, m) for b in (0, 1) for m in range(2)],
                      "mla": [(b, m) for b in (0, 1) for m in range(2)]}[kind]
            for gi, (b, m) in enumerate(groups):
                for h in range(8):
                    u = dict(group=gi, branch=b, m=m, col=h, nk=S)
                    tok = slice(m * P, (m + 1) * P)
                    if kind == "lay":
                        u["nk"] = nk = (m + 1) * P
                        u["bias"] = alibi[:, h, m * P:m * P + nk]
                        if b == "moba":
                            r = slice((h % 2) * HD, (h % 2) * HD + HD)
                            u["s"] = [(qm[r, h // 2, tok], km[r, h // 2, 0:nk])]
                            u["v"] = [vm[:, t, h * HD:(h + 1) * HD] for t in range(m + 1)]
                        else:
                            w, g, j = (0 if b == "sel" else 1), h // 4, h % 4
                            r = slice(g * HD, g * HD + HD)
                            u["s"] = [(qn[r, j, tok], ksw[r, w, 0:nk])]
                            u["v"] = [vsw[:, t, w * P + g * HD:w * P + (g + 1) * HD] for t in range(m + 1)]
                    elif kind == "na":
                        hh_ = b * 8 + h
                        r = slice((hh_ % 2) * HD, (hh_ % 2) * HD + HD)
                        u["s"] = [(naq[r, hh_ // 2, tok], nak[r, hh_ // 2, :])]
                        u["v"] = [nav[:, t, hh_ * HD:(hh_ + 1) * HD] for t in range(2)]
                        first = 2 if m == 0 else 0
                        u["bias"] = rp[:, hh_ * 6 + first:hh_ * 6 + first + 4, :].rearrange("p a b -> p (a b)")
                    else:
                        hh_ = b * 8 + h
                        r = slice((hh_ % 2) * HD, (hh_ % 2) * HD + HD)
                        rr = slice((hh_ % 4) * 32, (hh_ % 4) * 32 + 32)
                        u["s"] = [(mq[r, hh_ // 2, tok], mk[r, hh_ // 2, :]),
                                  (mr[rr, hh_ // 4, tok], kr[rr, :])]
                        u["v"] = [mv[:, t, hh_ * HD:(hh_ + 1) * HD] for t in range(2)]
                        u["bias"] = pcol("zeros")
                    out.append(u)
            return out

        UNITS = {k: attention_units(k) for k in ("lay", "na", "mla")}
        S_BANK, PT_BANK, O_BANK = (4, 5), (0, 1), (2, 3)

        def gbank(use):
            return use % 3

        def uses_to(use):
            return sum(gbank(q) == gbank(use) for q in range(use + 1))

        block = ctx.enter_context(nc.Block())

        @block.sync
        def _(sp):
            e = Count(sg)

            def stream(phase, rep, base):
                for i in range(len(STEPS[phase])):
                    if RAW_NEED[phase][i] is not None:
                        sp.wait_ge(*e.at("raw_used", RAW_NEED[phase][i]))
                    r = RAW_AT[phase][i]
                    src = rep * len(STEPS[phase]) + base + i if not isinstance(rep, int) else base + i
                    sp.dma_start(raw[:, r, :], dram["ws"][src]).then_inc(*e.inc(f"raw_in{r}", 16))

            base = 0
            for p in PHASES:
                if p == "lay":
                    sp.dma_start(x[:], dram["x"]).then_inc(*e.inc("x_in", 16))
                    sp.dma_start(lc[:], dram["lc"]).then_inc(*e.inc("lc_in", 16))
                if p == "pre":
                    e.enter(p)
                    sp.dma_start(par[:], dram["par"]).then_inc(*e.inc("par_in", 16))
                if p in REPS:
                    with sp.Fori(0, REPS[p]) as rep:
                        e.enter(p, rep)
                        stream(p, rep, base)
                else:
                    if p != "pre":
                        e.enter(p)
                    stream(p, 0, base)
                base += len(STEPS[p]) * REPS.get(p, 1)
            e.enter("end")
            for m in range(MT):
                sp.wait_ge(*e.at("final", m + 1))
                sp.dma_start(dram["out"][:, m, :], xn_f[:, m, :]).then_inc(*e.inc("stored", 16))
            sp.wait_ge(*e.at("stored", MT, 16))

        @block.gpsimd
        def _(pool):
            g = nc.gpsimd
            e = Count(sg)
            e.enter("pre")
            g.memset(ones[:], 1.0).then_inc(*e.inc("consts"))
            g.memset(st[:], -0.5).then_inc(*e.inc("consts"))

            def rstd(sq_wait, spans):
                pool.wait_ge(*e.at("sq", sq_wait))
                pool.sem_inc(settled)
                for a, b, n in spans:
                    g.tensor_scalar(st[:, s_ms + a:s_ms + b], st[:, s_sq + a:s_sq + b],
                                    1.0 / n, EPS, ALU.mult, ALU.add).then_inc(*e.inc("mean_sq"))
                    pool.wait_ge(*e.last("mean_sq"))
                    pool.sem_inc(settled)
                a, b = spans[0][0], spans[-1][1]
                g.tensor_tensor(st[:, s_rs + a:s_rs + b], st[:, s_ms + a:s_ms + b],
                                st[:, s_half:s_half + b - a], ALU.pow).then_inc(*e.inc("rstd"))

            for name, n in (("x", 1), ("y", 1), ("split_used", SPL)):
                for _ in range(n):
                    g.memset(spare[:], 0.0).then_inc(*e.inc(name))
                    pool.wait_ge(*e.at(name, e.own[name]))
            pool.wait_ge(*e.at("consts", 2))
            with pool.Fori(0, 2) as rep:
                e.enter("lay", rep)
                rstd(2, [(0, 2, D)])
                rstd(3, [(2, 4, D)])
            e.enter("na")
            rstd(2, [(0, 2, D)])
            e.enter("ffn")
            rstd(2, [(0, 2, D)])
            e.enter("mla")
            rstd(2, [(0, 2, D)])
            rstd(6, [(2, 4, 256), (4, 6, 128)])
            e.enter("rt")
            rstd(2, [(0, 2, D)])
            e.enter("end")
            rstd(2, [(0, 2, D)])

        @block.tensor
        def _(pe):
            t = nc.tensor
            e = Count(sg)

            def mm3(out, lhs, rhs, start, stop):
                t.matmul(out, lhs[0], rhs[0], start=start, stop=False, skip_group_check=True)
                t.matmul(out, lhs[0], rhs[1], start=False, stop=False, skip_group_check=True)
                return t.matmul(out, lhs[1], rhs[0], start=False, stop=stop, skip_group_check=True)

            def arrived(n):
                pe.wait_ge(*e.at("raw_used", STEP_OF_SPLIT[e.phase][n] + 1))
                r = SPL_AT[e.phase][n]
                return wh[:, r, :], wl[:, r, :]

            used = {}

            def bank_free(b):
                if used.get(b, 0) or e.phase == "moe":
                    pe.wait_ge(*e.at(f"bank{b}", used.get(b, 0)))
                used[b] = used.get(b, 0) + 1

            def tok_slot(n, banks, width, first=True):
                for kh in range(2):
                    w = arrived(n + kh)
                    for m in range(MT):
                        if kh == 0 and first:
                            bank_free(banks[m])
                        for k in range(4):
                            kt = kh * 4 + k
                            lhs = [a[:, kt, m * P:(m + 1) * P] for a in (hh, hl)]
                            rhs = [a[:, k * width:(k + 1) * width] for a in w]
                            last = mm3(PS[:, banks[m], 0:width], lhs, rhs, kt == 0, kt == KT - 1)
                    last.then_inc(*e.inc("split_used"))

            def feat_slot(n, banks, order=(0, 1, 2, 3)):
                for kh in range(2):
                    w = arrived(n + kh)
                    for i, f in enumerate(order):
                        b = banks[i // 2]
                        if kh == 0 and i % 2 == 0:
                            bank_free(b)
                        for k in range(4):
                            kt = kh * 4 + k
                            lhs = [a[:, k * 512 + f * P:k * 512 + (f + 1) * P] for a in w]
                            last = mm3(PS[:, b, (i % 2) * S:(i % 2 + 1) * S], lhs, (hh[:, kt, :], hl[:, kt, :]),
                                       kt == 0 and i % 2 == 0, kt == KT - 1)
                    last.then_inc(*e.inc("split_used"))

            def ada(j):
                pe.wait_ge(*e.at("raw_used", [i for i, s in enumerate(STEPS[e.phase]) if s == ("ada", j, 1)][0] + 1))
                bank_free(3)
                a = acc[:, j % 2, :]
                if j % 6 < 4:
                    for c in range(4):
                        last = t.matmul(PS[:, 3, c:c + 1], a[:, c * P:(c + 1) * P], ones[:, 0:1],
                                        start=True, stop=True)
                else:
                    if j % 6 == 4:
                        pe.wait_ge(*e.at("brow", j // 6 + 1, 16))
                    t.matmul(PS[:, 3, :], ones[:], a, start=True, stop=False)
                    c = (j % 6 - 4) * 512
                    last = t.matmul(PS[:, 3, :], ones[0:1, :], brow[0:1, c:c + 512], start=False, stop=True)
                last.then_inc(*e.inc("ada_sum"))

            def turn(src, stage):
                for b in range(4):
                    for k in range(2):
                        for m in range(MT):
                            kt = 2 * b + k
                            c = (k * 2 + m) * P
                            last = t.transpose(PS[:, 4 + b, c:c + P], src[:, m, kt * P:(kt + 1) * P], ident)
                    last.then_inc(*e.inc("turned"))

            def attention(units):
                banks = range(4)
                for b in banks:
                    if used.get(b, 0) > 0:
                        pe.wait_ge(*e.at(f"bank{b}", used.get(b, 0)))

                def scores(i):
                    u = units[i]
                    if i >= 2:
                        pe.wait_ge(*e.at("logits", i - 1))
                    for j, (q, k) in enumerate(u["s"]):
                        last = t.matmul(PS[:, S_BANK[i % 2], 0:u["nk"]], q, k,
                                        start=j == 0, stop=j == len(u["s"]) - 1)
                    last.then_inc(*e.inc("scores"))

                def turn_probs(i):
                    u = units[i]
                    pe.wait_ge(*e.at("probs", i + 1))
                    if i >= 2:
                        pe.wait_ge(*e.at("pt", i - 1))
                    for c in range(u["nk"] // P):
                        last = t.transpose(PS[:, PT_BANK[i % 2], c * P:(c + 1) * P],
                                           pr[:, i % 2, c * P:(c + 1) * P], ident)
                    last.then_inc(*e.inc("probs_t"))

                def values(i):
                    u = units[i]
                    pe.wait_ge(*e.at("pt", i + 1))
                    if u["col"] == 0 and u["group"] >= 2:
                        pe.wait_ge(*e.at("o_used", u["group"] - 1))
                    nkt = u["nk"] // P
                    for c in range(nkt):
                        last = t.matmul(PS[:, O_BANK[u["group"] % 2], u["col"] * HD:(u["col"] + 1) * HD],
                                        pt[:, i % 2, c * P:(c + 1) * P], u["v"][c],
                                        start=c == 0, stop=c == nkt - 1)
                    last.then_inc(*e.inc("pv"))

                n = len(units)
                scores(0)
                for i in range(n + 1):
                    if i + 1 < n:
                        scores(i + 1)
                    if i < n:
                        turn_probs(i)
                    if i >= 1:
                        values(i - 1)

            def out_proj(n):
                pe.wait_ge(*e.at("h", 8))
                for s in range(2):
                    tok_slot(n + 2 * s, (4 + s, 6 + s), 512, first=False)

            def mlp(slots, adas):
                up = lambda s: feat_slot(up_proj_split(s), (gbank(2 * s), gbank(2 * s + 1)), (0, 2, 1, 3))

                def down(s):
                    w = arrived(down_split(s, slots))
                    pe.wait_ge(*e.at("act", 2 * (s + 1)))
                    if s == 0 and e.phase == "moe":
                        pe.wait_ge(*e.at("y_used", 0))
                    for k in range(2):
                        for m in range(MT):
                            lhs = [a[:, s % 2, k, m * P:(m + 1) * P] for a in (ah, al)]
                            for c in range(2):
                                rhs = [a[:, k * D + c * 512:k * D + (c + 1) * 512] for a in w]
                                last = mm3(PS[:, 4 + 2 * m + c, :], lhs, rhs,
                                           s == 0 and k == 0, s == slots - 1 and k == 1)
                    last.then_inc(*e.inc("split_used"))

                for s in range(slots):
                    up(s)
                    if adas and s >= 1:
                        ada(s - 1)
                    if s >= 1:
                        down(s - 1)
                if adas:
                    ada(slots - 1)
                down(slots - 1)
                if adas:
                    ada(slots)

            e.enter("pre")
            pe.wait_ge(*e.at("par_in", 1, 16))
            pe.wait_ge(*e.at("consts", 2))
            for j in range(6):
                ada(j)

            with pe.Fori(0, 2) as rep:
                e.enter("lay", rep)
                used.clear()
                pe.wait_ge(*e.at("xn", 2))
                turn(xn_l, 0)
                pe.wait_ge(*e.at("h", 4))
                for s in range(8):
                    b = (gbank(2 * s), gbank(2 * s + 1))
                    if s in (0, 1, 4, 5):
                        feat_slot(2 * s, b)
                    else:
                        tok_slot(2 * s, b, 280 if s == 6 else 512)
                    if 1 <= s <= 6:
                        ada(s - 1)
                for b in range(4):
                    pe.wait_ge(*e.at(f"bank{b}", used.get(b, 0)))
                pe.wait_ge(*e.at("kk", 7))
                ck = STEPS["lay"].index(("ck",))
                rk = RAW_AT["lay"][ck]
                fills = sum(r == rk for r in RAW_AT["lay"][:ck + 1])
                pe.wait_ge(*e.at(f"raw_in{rk}", fills, 16))
                pe.wait_ge(*e.at("lp", 1))
                for v in range(2):
                    for n, (lo, rhs_n) in enumerate(((v * 32, 30), (64 + v, 1))):
                        for a in range(16):
                            c = v * 1024 + a * 64
                            if n == 0:
                                rhs = kk[:, v, :, 2 * a:2 * a + 16 * (T_CMP - 1) + 1:16]
                                out = PS[0:HD, 4 + v, 0:30].rearrange("p (g t) -> p g t", g=2)
                            else:
                                rhs = LP["pek" if v == 0 else "pev"][:, a:a + 1]
                                out = PS[0:HD, 6 + v, 0:1]
                            last = t.matmul(out, raw[:, rk, c:c + 64], rhs, start=a == 0, stop=a == 15)
                last.then_inc(*e.inc("cmp1"))
                pe.wait_ge(*e.at("cmp_act", 1))
                pe.sem_inc(settled)
                for g in range(2):
                    t.matmul(PS[g * HD:(g + 1) * HD, 4, 0:T_CMP], LP["ck2"][0:HD, :],
                             cw[0:HD, 64 + g * 15:64 + g * 15 + 15], start=True, stop=True)
                for g in range(2):
                    last = t.matmul(PS[0:T_CMP, 5, g * HD:(g + 1) * HD],
                                    cw[0:HD, 96 + g * 15:96 + g * 15 + 15], LP["cv2"][0:HD, :],
                                    start=True, stop=True)
                last.then_inc(*e.inc("cmp2"))
                pe.wait_ge(*e.at("cmp_kv", 2))
                pe.wait_ge(*e.at("lc_in", 0, 16))
                for g in range(2):
                    last = t.matmul(PS[:, 6, g * HD:(g + 1) * HD], rep_sel[0:T_CMP, g, :],
                                    cw[0:T_CMP, 160 + g * HD:160 + (g + 1) * HD], start=True, stop=True)
                last.then_inc(*e.inc("cmp3"))
                for m in range(MT):
                    for g in range(2):
                        for j in range(4):
                            last = t.matmul(PS[:, 2 * m + g, j * 16:j * 16 + T_CMP],
                                            qn[g * HD:(g + 1) * HD, j, m * P:(m + 1) * P],
                                            cw[g * HD:(g + 1) * HD, 128:128 + T_CMP], start=True, stop=True)
                    last.then_inc(*e.inc("cscores"))
                for m in range(MT):
                    pe.wait_ge(*e.at("cprobs", m + 1))
                    t.transpose(PS[:, 4 + m, 0:P], cw[:, 288 + 0:288 + P] if m == 0 else pt[:, 1, 0:P],
                                ident).then_inc(*e.inc("cprobs_t"))
                pe.wait_ge(*e.at("vb", 1))
                for m in range(MT):
                    pe.wait_ge(*e.at("cpt", m + 1))
                    t.matmul(PS[:, 6 + m, :], pt[:, 0, m * P:(m + 1) * P], vb[:], start=True,
                             stop=True).then_inc(*e.inc("cout"))
                pe.wait_ge(*e.at("cout_used", 2))
                attention(UNITS["lay"])
                pe.wait_ge(*e.at("y", 4))
                turn(y, 1)
                out_proj(16)

            e.enter("na")
            used.clear()
            pe.wait_ge(*e.at("xn", 2))
            turn(xn_n, 0)
            pe.wait_ge(*e.at("h", 4))
            for s in range(6):
                b = (gbank(2 * s), gbank(2 * s + 1))
                if s < 4:
                    feat_slot(2 * s, b)
                else:
                    tok_slot(2 * s, b, 512)
                if s >= 1:
                    ada(s - 1)
            ada(5)
            attention(UNITS["na"])
            pe.wait_ge(*e.at("o_used", 4))
            turn(nao, 1)
            out_proj(12)

            e.enter("ffn")
            used.clear()
            pe.wait_ge(*e.at("xn", 2))
            turn(xn_f, 0)
            pe.wait_ge(*e.at("h", 4))
            mlp(FFN_SLOTS, True)

            e.enter("mla")
            used.clear()
            pe.wait_ge(*e.at("xn", 2))
            turn(xn_m, 0)
            pe.wait_ge(*e.at("h", 4))
            tok_slot(0, (0, 1), 416, first=False)
            pe.wait_ge(*e.at("cn", 4))
            for k in range(4):
                for m in range(MT):
                    last = t.transpose(PS[:, 4 + k // 2, ((k % 2) * 2 + m) * P:((k % 2) * 2 + m + 1) * P],
                                       cn[:, m, k * P:(k + 1) * P], ident)
            last.then_inc(*e.inc("c_t"))
            pe.wait_ge(*e.at("c", 2))
            for half in range(2):
                w = arrived(2 + half)
                if half == 0:
                    pe.wait_ge(*e.at("down_used", 2))
                for f in range(8):
                    b = 4 * half + f // 2
                    for k in range(2):
                        lhs = [a[:, k * D + f * P:k * D + (f + 1) * P] for a in w]
                        last = mm3(PS[:, b, (f % 2) * S:(f % 2 + 1) * S], lhs, (hh[:, k, :], hl[:, k, :]),
                                   k == 0 and f % 2 == 0, k == 1)
                last.then_inc(*e.inc("split_used"))
            w = arrived(4)
            pe.wait_ge(*e.at("mq", 4))
            for f in range(8):
                lhs = [a[:, f * P:(f + 1) * P] for a in w]
                last = mm3(PS[:, f // 2, (f % 2) * S:(f % 2 + 1) * S], lhs, (hh[:, 2, :], hl[:, 2, :]),
                           f % 2 == 0, True)
            last.then_inc(*e.inc("mk_sum"))
            pe.wait_ge(*e.at("mr", 2))
            for m in range(MT):
                lhs = [a[:, 2, m * P:(m + 1) * P] for a in (hh, hl)]
                for c in range(2):
                    rhs = [a[:, D + c * 512:D + (c + 1) * 512] for a in w]
                    last = mm3(PS[:, 4 + 2 * m + c, :], lhs, rhs, True, True)
            last.then_inc(*e.inc("split_used"))
            pe.wait_ge(*e.at("mkv", 5))
            attention(UNITS["mla"])
            pe.wait_ge(*e.at("o_used", 4))
            turn(mo, 1)
            out_proj(5)

            e.enter("rt")
            used.clear()
            pe.wait_ge(*e.at("xn", 2))
            turn(xn_f, 0)
            pe.wait_ge(*e.at("h", 4))
            for m in range(MT):
                for i, a in enumerate((hh, hl)):
                    for kt in range(KT):
                        last = t.matmul(PS[:, m, 0:NEXP], a[:, kt, m * P:(m + 1) * P].bitcast(F32),
                                        pcol("router", kt * NEXP, (kt + 1) * NEXP),
                                        start=i == 0 and kt == 0, stop=i == 1 and kt == KT - 1)
                last.then_inc(*e.inc("router"))
            pe.wait_ge(*e.at("route_read", 2))

            with pe.Fori(0, NEXP) as rep:
                e.enter("moe", rep)
                used.clear()
                mlp(MOE_SLOTS, False)

        @block.scalar
        def _(act):
            a = nc.scalar
            e = Count(sg)
            done = [0]

            def hi_to(n):
                for i in range(done[0], min(n, SPLITS[e.phase])):
                    step = STEP_OF_SPLIT[e.phase][i]
                    r = RAW_AT[e.phase][step]
                    act.wait_ge(*e.at(f"raw_in{r}", sum(q == r for q in RAW_AT[e.phase][:step + 1]), 16))
                    if SPL_NEED[e.phase][i] is not None:
                        act.wait_ge(*e.at("split_used", SPL_NEED[e.phase][i]))
                    a.activation(wh[:, SPL_AT[e.phase][i], :], raw[:, r, :], ACT.Copy).then_inc(*e.inc("hi"))
                done[0] = max(done[0], min(n, SPLITS[e.phase]))

            def start(phase, rep=0):
                e.enter(phase, rep)
                done[0] = 0
                hi_to(SPL)

            def squares(xn):
                if e.phase == "end":
                    act.wait_ge(*e.at("x_last", MT))
                else:
                    act.wait_ge(*e.at("x", 0))
                for m in range(MT):
                    a.activation(xn[:, m, :], x[:, m, :], ACT.Square,
                                 accum_out=st[:, s_sq + m:s_sq + m + 1]).then_inc(*e.inc("sq"))

            def h_hi(stage):
                for b in range(4):
                    dst = hh[:, 2 * b:2 * b + 2, :]
                    if stage == 0:
                        act.wait_ge(*e.at("hb", b + 1))
                        src = hb[:, (2 * b) % 4:(2 * b) % 4 + 2, :]
                    else:
                        act.wait_ge(*e.at("turned", 5 + b))
                        src = PS[:, 4 + b, :].rearrange("p (k s) -> p k s", k=2)
                    a.activation(dst, src, ACT.Copy).then_inc(*e.inc("h_hi"))

            def get_brow(unit):
                act.dma_start(brow[:], dram["brow"][unit]).then_inc(*e.inc("brow", 16))

            def ada_out(j, buf):
                act.wait_ge(*e.at("ada_sum", j + 1))
                j6 = j % 6
                if j6 < 4:
                    ins = a.activation(modc[:, buf, j6 * 4:j6 * 4 + 4], PS[:, 3, 0:4], ACT.Copy)
                else:
                    ins = a.activation(gate[buf][:, (j6 - 4) * 512:(j6 - 3) * 512], PS[:, 3, :], ACT.Copy)
                ins.then_inc(*e.inc("bank3"))

            def summed(n):
                act.wait_ge(*e.at("split_used", n + 2))

            def out_feat(s, dst, scale):
                summed(2 * s)
                for i in range(2):
                    b = gbank(2 * s + i)
                    src = PS[:, b, :].rearrange("p (k s) -> p k s", k=2)
                    a.activation(dst[:, 2 * i:2 * i + 2, :], src, ACT.Copy,
                                 scale=scale).then_inc(*e.inc(f"bank{b}"))

            def out_tok(s, dst):
                summed(2 * s)
                for m in range(MT):
                    b = gbank(2 * s + m)
                    w = dst.shape[2]
                    a.activation(dst[:, m, :], PS[:, b, 0:w], ACT.Copy).then_inc(*e.inc(f"bank{b}"))

            def exps(units):
                for i, u in enumerate(units):
                    act.wait_ge(*e.at("logits", i + 1))
                    if i >= 2:
                        act.wait_ge(*e.at("probs_t", i - 1))
                    c = i % 48
                    a.activation(pr[:, i % 2, 0:u["nk"]], lg[:, i % 2, 0:u["nk"]], ACT.Exp,
                                 bias=mn(c), scale=-1.0, accum_out=sm(c)).then_inc(*e.inc("probs"))

            def mlp(slots, adas):
                for s in range(slots):
                    n = up_proj_split(s)
                    hi_to(n + 2 + SPL)
                    summed(n)
                    for f in range(2):
                        q = 2 * s + f
                        if q >= 4 or e.phase == "moe":
                            act.wait_ge(*e.at("act", max(q - 3, 0)))
                        a.activation(hb[:, q % 4, :], PS[:, gbank(q), 0:S], ACT.Tanh,
                                     scale=0.5).then_inc(*e.inc("tanh"))
                    for f in range(2):
                        q = 2 * s + f
                        b = gbank(q)
                        act.wait_ge(*e.at(f"bank{b}", sum(gbank(r) == b for r in range(q + 1))))
                        if s >= 2:
                            act.wait_ge(*e.at("split_used", down_split(s - 2, slots) + 1))
                        else:
                            act.wait_ge(*e.at("split_used", 0))
                        a.activation(ah[:, s % 2, f, :], hb[:, q % 4, :], ACT.Copy).then_inc(*e.inc("act_hi"))
                    if adas and s >= 1:
                        if s == 7:
                            get_brow(5)
                        ada_out(s - 1, 1 if s - 1 < 6 else 2)
                    if s >= 1:
                        hi_to(down_split(s - 1, slots) + 1 + SPL)
                hi_to(SPLITS[e.phase])
                if adas:
                    ada_out(slots - 1, 2)
                    ada_out(slots, 2)

            e.enter("pre")
            get_brow(0)
            act.wait_ge(*e.at("par_in", 1, 16))
            act.wait_ge(*e.at("consts", 2))
            c2 = pcol("cc").rearrange("p (c k) -> p c k", c=2)
            a.activation(cs[:], c2, ACT.Tanh, scale=0.5).then_inc(*e.inc("cs_tanh"))
            for j in range(6):
                ada_out(j, 1)

            with act.Fori(0, 2) as rep:
                start("lay", rep)
                act.wait_ge(*e.at("x_in", 0, 16))
                squares(xn_l)
                act.wait_ge(*e.at("y", 0))
                act.dma_start(gpost[:], dram["gpost"][rep]).then_inc(*e.inc("gpost", 16))
                act.dma_start(brow[:], dram["brow"][rep + 1]).then_inc(*e.inc("brow", 16))
                h_hi(0)
                for s in range(8):
                    hi_to(2 * s + 2 + SPL)
                    if s == 0:
                        out_feat(s, qm, -QS)
                    if s == 1:
                        out_feat(s, km, 1.0)
                    if s == 2:
                        out_tok(s, vm)
                    if s in (3, 7):
                        if s == 7:
                            act.wait_ge(*e.at("gg", 1))
                        z = zm if s == 3 else zn
                        summed(2 * s)
                        for m in range(MT):
                            a.activation(z[:, m, :], PS[:, gbank(2 * s + m), :], ACT.Tanh,
                                         scale=0.5).then_inc(*e.inc("z_tanh"))
                    if s == 4:
                        out_feat(s, qn, -QS)
                    if s == 5:
                        summed(2 * s)
                        b = gbank(2 * s + 1)
                        a.activation(ksw[:], PS[:, b, :].rearrange("p (k s) -> p k s", k=2),
                                     ACT.Copy).then_inc(*e.inc(f"bank{b}"))
                    if s == 6:
                        out_tok(s, vsw)
                    if 1 <= s <= 6:
                        ada_out(s - 1, 1)
                gl = vsw[:, :, 256:280]
                for b in range(3):
                    act.wait_ge(*e.at(f"bank{b}", sum(gbank(q) == b for q in range(16))))
                a.activation(gl, gl, ACT.Tanh, scale=0.5).then_inc(*e.inc("g_tanh"))
                act.wait_ge(*e.at("cmp_u", 1))
                a.activation(cw[0:HD, 64:128], cw[0:HD, 0:64], ACT.Tanh,
                             scale=0.7978845608028654).then_inc(*e.inc("cmp_tanh"))
                act.wait_ge(*e.at("cmp2", 1))
                a.activation(cw[:, 128:128 + T_CMP], PS[:, 4, 0:T_CMP], ACT.Copy,
                             scale=0.5).then_inc(*e.inc("cmp_kv"))
                a.activation(cw[0:T_CMP, 160:288], PS[0:T_CMP, 5, 0:P], ACT.Copy,
                             scale=0.5).then_inc(*e.inc("cmp_kv"))
                for m in range(MT):
                    act.wait_ge(*e.at("clogits", m + 1))
                    dst = (cw[:, 288:416] if m == 0 else pt[:, 1, 0:P]).rearrange("p (h t) -> p h t", h=8)
                    src = hb[:, m, 0:P].rearrange("p (h t) -> p h t", h=8)
                    a.activation(dst[:, :, 0:T_CMP], src[:, :, 0:T_CMP], ACT.Exp,
                                 scale=-1.0).then_inc(*e.inc("cexp"))
                exps(UNITS["lay"])
                h_hi(1)
                hi_to(20)
                act.wait_ge(*e.at("split_used", 20))
                for i in range(4):
                    a.activation(xn_l[:, i // 2, (i % 2) * 512:(i % 2 + 1) * 512], PS[:, 4 + i, :], ACT.Square,
                                 accum_out=st[:, 240 + i:241 + i]).then_inc(*e.inc("ysq"))

            start("na")
            squares(xn_n)
            act.dma_start(rp[:], dram["rp"]).then_inc(*e.inc("rp_in", 16))
            get_brow(3)
            h_hi(0)
            for s in range(6):
                hi_to(2 * s + 2 + SPL)
                if s < 2:
                    out_feat(s, naq[:, 4 * s:4 * s + 4, :], -QS)
                elif s < 4:
                    out_feat(s, nak[:, 4 * (s - 2):4 * (s - 2) + 4, :], 1.0)
                else:
                    out_tok(s, nav[:, :, (s - 4) * 512:(s - 3) * 512])
                if s >= 1:
                    ada_out(s - 1, 0)
            ada_out(5, 0)
            exps(UNITS["na"])
            h_hi(1)
            hi_to(16)

            start("ffn")
            squares(xn_f)
            get_brow(4)
            h_hi(0)
            mlp(FFN_SLOTS, True)

            start("mla")
            squares(xn_m)
            h_hi(0)
            summed(0)
            for m in range(MT):
                a.activation(dsb[:, m, :], PS[:, m, 0:416], ACT.Copy).then_inc(*e.inc("down_used"))
            act.wait_ge(*e.at("down_used", 2))
            for m in range(MT):
                for i, (c0, c1) in enumerate(((0, 256), (256, 384))):
                    a.activation(cn[:, m, c0:c1], dsb[:, m, c0:c1], ACT.Square,
                                 accum_out=st[:,
                                              s_sq + 2 + 2 * i + m:s_sq + 3 + 2 * i + m]).then_inc(*e.inc("sq"))
            act.wait_ge(*e.at("c_f", 1))
            a.activation(hh[:, 0:3, :], hb[:, 0:3, :], ACT.Copy).then_inc(*e.inc("c_hi"))
            hi_to(5)
            act.wait_ge(*e.at("split_used", 3))
            for i in range(4):
                src = PS[:, i, :].rearrange("p (k s) -> p k s", k=2)
                a.activation(mq[:, 2 * i:2 * i + 2, :], src, ACT.Copy, scale=-MS).then_inc(*e.inc("mq"))
            act.wait_ge(*e.at("mk_sum", 1))
            for i in range(4):
                src = PS[:, i, :].rearrange("p (k s) -> p k s", k=2)
                a.activation(mk[:, 2 * i:2 * i + 2, :], src, ACT.Copy).then_inc(*e.inc("mkv"))
            hi_to(8)
            exps(UNITS["mla"])
            h_hi(1)
            hi_to(9)

            e.enter("rt")
            squares(xn_f)
            act.dma_start(fnorm[:], dram["fnorm"]).then_inc(*e.inc("fnorm", 16))
            h_hi(0)
            for m in range(MT):
                act.wait_ge(*e.at("rmax", m + 1))
                a.activation(rw[:, m * 8:m * 8 + 8], rw[:, m * 8:m * 8 + 8], ACT.Exp,
                             bias=rw[:, 16 + m:17 + m], accum_out=rw[:, 18 + m:19 + m]).then_inc(*e.inc("rexp"))

            with act.Fori(0, NEXP) as rep:
                start("moe", rep)
                mlp(MOE_SLOTS, False)

            e.enter("end")
            squares(xn_f)

        @block.vector
        def _(dve):
            v = nc.vector
            e = Count(sg)
            done = [0]

            def link(ins):
                ins.then_inc(*e.inc("dve"))
                dve.wait_ge(*e.last("dve"))

            def raw_to(n):
                ph = e.phase
                for i in range(done[0], min(n, len(STEPS[ph]))):
                    step, r = STEPS[ph][i], RAW_AT[ph][i]
                    if step[0] == "w":
                        s = SPL_AT[ph][step[1]]
                        dve.wait_ge(*e.at("hi", step[1] + 1))
                        v.tensor_tensor(wl[:, s, :], raw[:, r, :], wh[:, s, :].bitcast(F32),
                                        ALU.subtract).then_inc(*e.inc("raw_used"))
                        dve.wait_ge(*e.last("raw_used"))
                    elif step[0] == "ada":
                        _, j, kh = step
                        dve.wait_ge(*e.at(f"raw_in{r}", sum(q == r for q in RAW_AT[ph][:i + 1]), 16))
                        dst = acc[:, j % 2, :]
                        if kh == 0:
                            if j >= 2:
                                dve.wait_ge(*e.at("ada_sum", j - 1))
                        c = cs[:, 1, :] if ph == "ffn" or ph == "na" else csc[:]
                        for k in range(4):
                            kt = kh * 4 + k
                            w = raw[:, r, k * 512:(k + 1) * 512]
                            if kt == 0:
                                ins = v.tensor_scalar(dst, w, c[:, kt:kt + 1], None, ALU.mult)
                            else:
                                ins = v.scalar_tensor_tensor(out=dst, in0=w, scalar=c[:, kt:kt + 1], in1=dst,
                                                             op0=ALU.mult, op1=ALU.add)
                            if k < 3:
                                link(ins)
                            else:
                                ins.then_inc(*e.inc("raw_used"))
                                dve.wait_ge(*e.last("raw_used"))
                    else:
                        return i
                    done[0] = i + 1

            def split_to(n):
                ph = e.phase
                n = min(n, SPLITS[ph])
                raw_to(STEP_OF_SPLIT[ph][n - 1] + 1)

            def start(phase, rep=0):
                e.enter(phase, rep)
                done[0] = 0

            def norm(xn, wa, wb):
                dve.wait_ge(*e.at("rstd", 1))
                for m in range(MT):
                    v.tensor_scalar(xn[:, m, :], x[:, m, :], st[:, s_rs + m:s_rs + m + 1], None,
                                    ALU.mult).then_inc(*e.inc("xn"))
                    dve.wait_ge(*e.last("xn"))

                def lo(b):
                    dve.wait_ge(*e.at("h_hi", b + 1))
                    v.tensor_tensor(hl[:, 2 * b:2 * b + 2, :], hb[:, (2 * b) % 4:(2 * b) % 4 + 2, :],
                                    hh[:, 2 * b:2 * b + 2, :].bitcast(F32), ALU.subtract).then_inc(*e.inc("h"))
                    dve.wait_ge(*e.last("h"))

                for b in range(4):
                    dve.wait_ge(*e.at("turned", b + 1))
                    for k in range(2):
                        kt = 2 * b + k
                        ins = v.tensor_scalar(hb[:, kt % 4, :], PS[:, 4 + b, k * S:(k + 1) * S],
                                              wa[:, kt:kt + 1], wb[:, kt:kt + 1], ALU.mult, ALU.add)
                        if k == 0:
                            link(ins)
                        else:
                            ins.then_inc(*e.inc("hb"))
                            dve.wait_ge(*e.last("hb"))
                    if b >= 1:
                        lo(b - 1)
                lo(3)

            def make_ab(buf, bcol, gpre=None):
                dve.wait_ge(*e.at("bank3", 0))
                link(v.tensor_tensor(modc[:, buf, :], modc[:, buf, :], bcol, ALU.add))
                if gpre is not None:
                    link(v.scalar_tensor_tensor(out=ab[:, 0, :], in0=modc[:, buf, 8:16], scalar=1.0, in1=gpre,
                                                op0=ALU.add, op1=ALU.mult))
                else:
                    link(v.tensor_scalar(ab[:, 0, :], modc[:, buf, 8:16], 1.0, None, ALU.add))
                link(v.tensor_copy(ab[:, 1, :], modc[:, buf, 0:8]))

            def h_lo_psum():
                for b in range(4):
                    dve.wait_ge(*e.at("h_hi", 5 + b))
                    v.tensor_tensor(hl[:, 2 * b:2 * b + 2, :],
                                    PS[:, 4 + b, :].rearrange("p (k s) -> p k s", k=2),
                                    hh[:, 2 * b:2 * b + 2, :].bitcast(F32), ALU.subtract).then_inc(*e.inc("h"))
                    dve.wait_ge(*e.last("h"))

            def attention(units, finish):
                def logits(i):
                    u = units[i]
                    dve.wait_ge(*e.at("scores", i + 1))
                    if i >= 2:
                        dve.wait_ge(*e.at("probs", i - 1))
                    n = u["nk"]
                    dve.sem_inc(settled)
                    v.tensor_tensor_reduce(lg[:, i % 2, 0:n], u["bias"], PS[:, S_BANK[i % 2], 0:n],
                                           1.0, 3e38, ALU.add, ALU.min, mn(i % 48)).then_inc(*e.inc("logits"))
                    dve.wait_ge(*e.last("logits"))

                def copy_pt(i):
                    n = units[i]["nk"]
                    dve.wait_ge(*e.at("probs_t", i + 1))
                    if i >= 2:
                        dve.wait_ge(*e.at("pv", i - 1))
                    v.tensor_copy(pt[:, i % 2, 0:n], PS[:, PT_BANK[i % 2], 0:n]).then_inc(*e.inc("pt"))
                    dve.wait_ge(*e.last("pt"))

                n = len(units)
                logits(0)
                for i in range(n):
                    if i + 1 < n:
                        logits(i + 1)
                    copy_pt(i)
                    if i % 8 == 2 and i > 8:
                        out_group(i // 8 - 1, units, finish)
                out_group(n // 8 - 1, units, finish)

            def out_group(g, units, finish):
                dve.wait_ge(*e.at("probs", 8 * g + 8))
                c = (8 * g) % 48
                link(v.reciprocal(rinv(0, 8), st[:, 96 + c:104 + c]))
                dve.wait_ge(*e.at("pv", 8 * g + 8))
                o = PS[:, O_BANK[g % 2], :].rearrange("p (h d) -> p h d", h=8)
                finish(units[8 * g], o, rinv(0, 8))

            def bc(w):
                return w.unsqueeze(2).broadcast_to([P, 8, HD])

            def update_x(g, n_wait):
                dve.wait_ge(*e.at("split_used", n_wait))
                for m in range(MT):
                    tmp = hb[:].rearrange("p a b -> p (a b)")
                    src = PS[:, 4 + 2 * m:6 + 2 * m, :].rearrange("p a b -> p (a b)")
                    link(v.tensor_tensor(tmp, src, g[:], ALU.mult))
                    v.tensor_tensor(x[:, m, :], x[:, m, :], tmp, ALU.add).then_inc(*e.inc("x"))
                    dve.wait_ge(*e.last("x"))

            def mlp(slots, adas):
                for s in range(slots):
                    n = up_proj_split(s)
                    split_to(n + 2 + SPL)
                    dve.wait_ge(*e.at("split_used", n + 2))
                    for f in range(2):
                        q = 2 * s + f
                        b = gbank(q)
                        t_ = hb[:, q % 4, :]
                        dve.wait_ge(*e.at("tanh", q + 1))
                        link(v.scalar_tensor_tensor(out=t_, in0=t_, scalar=1.0, in1=PS[:, b, 0:S],
                                                    op0=ALU.add, op1=ALU.mult))
                        v.scalar_tensor_tensor(out=t_, in0=t_, scalar=0.5, in1=PS[:, b, S:2 * S],
                                               op0=ALU.mult, op1=ALU.mult).then_inc(*e.inc(f"bank{b}"))
                        dve.wait_ge(*e.at(f"bank{b}", uses_to(q)))
                    for f in range(2):
                        q = 2 * s + f
                        dve.wait_ge(*e.at("act_hi", q + 1))
                        v.tensor_tensor(al[:, s % 2, f, :], hb[:, q % 4, :],
                                        ah[:, s % 2, f, :].bitcast(F32), ALU.subtract).then_inc(*e.inc("act"))
                        dve.wait_ge(*e.last("act"))
                    if s >= 1:
                        split_to(down_split(s - 1, slots) + 1 + SPL)
                raw_to(999)

            e.enter("pre")
            c2 = pcol("cc").rearrange("p (c k) -> p c k", c=2)
            dve.wait_ge(*e.at("cs_tanh", 1))
            dve.wait_ge(*e.at("consts", 2))
            link(v.scalar_tensor_tensor(out=cs[:], in0=cs[:], scalar=1.0, in1=c2, op0=ALU.add, op1=ALU.mult))
            link(v.tensor_scalar(cs[:], cs[:], 0.5, None, ALU.mult))
            link(v.tensor_copy(csc[:], cs[:, 0, :]))
            raw_to(99)

            with dve.Fori(0, 2) as rep:
                start("lay", rep)
                dve.wait_ge(*e.at("par_in", 0, 16))
                dve.wait_ge(*e.at("x_in", 0, 16))
                link(v.tensor_copy(csc[:], cs[:, bass.ds(rep, 1), :].rearrange("p a b -> p (a b)")))
                v.tensor_copy(lpc[:],
                              lpall[:, bass.ds(rep, 1), :].rearrange("p a b -> p (a b)")).then_inc(*e.inc("lp"))
                dve.wait_ge(*e.last("lp"))
                make_ab(1, LP["bcol"], LP["gpre"])
                split_to(2)
                norm(xn_l, ab[:, 0, :], ab[:, 1, :])
                dve.wait_ge(*e.at("gpost", 1, 16))
                v.tensor_tensor(gate[0][:], gate[1][:], gpost[:], ALU.mult).then_inc(*e.inc("gg"))
                dve.wait_ge(*e.last("gg"))
                for s in range(8):
                    if s < 6:
                        split_to(2 * s + 2 + SPL)
                    if s in (3, 7):
                        z = zm if s == 3 else zn
                        for m in range(MT):
                            b = gbank(2 * s + m)
                            dve.wait_ge(*e.at("z_tanh", (2 if s == 7 else 0) + m + 1))
                            v.scalar_tensor_tensor(out=z[:, m, :], in0=z[:, m, :], scalar=1.0,
                                                   in1=PS[:, b,
                                                          :], op0=ALU.add, op1=ALU.mult).then_inc(*e.inc(f"bank{b}"))
                            dve.wait_ge(*e.at(f"bank{b}", uses_to(2 * s + m)))
                    if s == 5:
                        dve.wait_ge(*e.at("split_used", 12))
                        b = gbank(10)
                        for w in range(2):
                            for g in range(2):
                                src = PS[g * HD:(g + 1) * HD, b, w * S:(w + 1) * S]
                                v.tensor_copy(kk[0:HD, w, g, :], src).then_inc(*e.inc("kk"))
                                dve.wait_ge(*e.last("kk"))
                                ins = v.tensor_copy(kk[HD:P, w, g, 0:S - 1], src[:, 1:S])
                                if (w, g) == (1, 1):
                                    ins.then_inc(*e.inc(f"bank{b}"))
                                    dve.wait_ge(*e.at(f"bank{b}", uses_to(10)))
                                else:
                                    ins.then_inc(*e.inc("kk"))
                                    dve.wait_ge(*e.last("kk"))
                    if s == 5:
                        split_to(16)
                raw_to(999)
                dve.wait_ge(*e.at("g_tanh", 1))
                gl = vsw[:, :, 256:280]
                link(v.tensor_scalar(gl, gl, 0.5, 0.5, ALU.mult, ALU.add))
                dve.wait_ge(*e.at("cmp1", 1))
                xc, u_ = cw[0:HD, 0:64], cw[0:HD, 416:480]
                link(v.memset(cw[0:HD, 0:128], 0.0))
                bias = st[0:HD, 232:234]
                link(v.tensor_copy(bias, PS[0:HD, 6:8, 0:1].rearrange("p a b -> p (a b)")))
                for w in range(2):
                    link(v.tensor_scalar(xc[:, w * 32:w * 32 + 30], PS[0:HD, 4 + w, 0:30], bias[:, w:w + 1], None,
                                         ALU.add))
                link(v.tensor_tensor(u_, xc, xc, ALU.mult))
                link(v.tensor_scalar(u_, u_, 0.044715, 1.0, ALU.mult, ALU.add))
                link(v.tensor_copy(hb[0:HD, 0, 0:64], xc))
                v.tensor_tensor(xc, u_, xc, ALU.mult).then_inc(*e.inc("cmp_u"))
                dve.wait_ge(*e.last("cmp_u"))
                dve.wait_ge(*e.at("cmp_tanh", 1))
                v.scalar_tensor_tensor(out=cw[0:HD, 64:128], in0=cw[0:HD, 64:128], scalar=1.0,
                                       in1=hb[0:HD, 0,
                                              0:64], op0=ALU.add, op1=ALU.mult).then_inc(*e.inc("cmp_act"))
                dve.wait_ge(*e.last("cmp_act"))
                dve.wait_ge(*e.at("cmp_act", 1))
                v.memset(st[:, 236:237], 0.0).then_inc(*e.inc("raw_used"))
                dve.wait_ge(*e.last("raw_used"))
                done[0] = STEPS["lay"].index(("ck",)) + 1
                split_to(19)
                dve.wait_ge(*e.at("cmp3", 1))
                dve.wait_ge(*e.at("lc_in", 0, 16))
                link(v.memset(cw[:, 288:416], 0.0))
                link(v.memset(pt[:, 1, 0:P], 0.0))
                for g in range(2):
                    ins = v.tensor_tensor(
                        vb[:].rearrange("p (h d) -> p h d", h=8)[:, 4 * g:4 * g + 4, :],
                        PS[:, 6, g * HD:(g + 1) * HD].unsqueeze(1).broadcast_to([P, 4, HD]),
                        mask8[:, 4 * g:4 * g + 4].unsqueeze(2).broadcast_to([P, 4, HD]), ALU.mult)
                    if g == 0:
                        link(ins)
                ins.then_inc(*e.inc("vb"))
                dve.wait_ge(*e.last("vb"))
                for m in range(MT):
                    dve.wait_ge(*e.at("cscores", m + 1))
                    l8 = hb[:, m, 0:P].rearrange("p (h t) -> p h t", h=8)[:, :, 0:T_CMP]
                    for g in range(2):
                        link(v.tensor_tensor(l8[:, 4 * g:4 * g + 4, :],
                                             PS[:, 2 * m + g, 0:64].rearrange("p (j t) -> p j t", j=4)[:, :, 0:T_CMP],
                                             alibi_c[:, m, 4 * g:4 * g + 4, 0:T_CMP], ALU.add))
                    link(v.tensor_reduce(rinv(0, 8), l8, AX_X, ALU.min))
                    v.tensor_tensor(l8, l8, rinv(0, 8).unsqueeze(2).broadcast_to([P, 8, T_CMP]),
                                    ALU.subtract).then_inc(*e.inc("clogits"))
                    dve.wait_ge(*e.last("clogits"))
                for m in range(MT):
                    dve.wait_ge(*e.at("cexp", m + 1))
                    ex = (cw[:, 288:416] if m == 0 else pt[:, 1, 0:P]).rearrange("p (h t) -> p h t", h=8)[:, :, 0:T_CMP]
                    link(v.tensor_reduce(st[:, 240 + 8 * m:248 + 8 * m], ex, AX_X, ALU.add))
                    v.tensor_tensor(ex, ex, ok_c[:, m, 0:T_CMP].unsqueeze(1).broadcast_to([P, 8, T_CMP]),
                                    ALU.mult).then_inc(*e.inc("cprobs"))
                    dve.wait_ge(*e.last("cprobs"))
                for m in range(MT):
                    dve.wait_ge(*e.at("cprobs_t", m + 1))
                    v.tensor_copy(pt[:, 0, m * P:(m + 1) * P], PS[:, 4 + m, 0:P]).then_inc(*e.inc("cpt"))
                    dve.wait_ge(*e.last("cpt"))

                def gate_of(m, c):
                    return vsw[:, m, 256:280].rearrange("p (h c) -> p h c", c=3)[:, :, c:c + 1].rearrange("p h c -> p (h c)")

                for m in range(MT):
                    link(v.reciprocal(rinv(0, 8), st[:, 240 + 8 * m:248 + 8 * m]))
                    link(v.tensor_tensor(wgt(), rinv(0, 8), gate_of(m, 0), ALU.mult))
                    dve.wait_ge(*e.at("cout", m + 1))
                    v.tensor_tensor(y[:, m, 512:1024].rearrange("p (h d) -> p h d", h=8),
                                    PS[:, 6 + m, :].rearrange("p (h d) -> p h d", h=8), bc(wgt()),
                                    ALU.mult).then_inc(*e.inc("cout_used"))
                    dve.wait_ge(*e.last("cout_used"))

                def finish(u, o, ri):
                    m = u["m"]
                    t3 = tmpo[:].rearrange("p (h d) -> p h d", h=8)
                    if u["branch"] == "moba":
                        v.scalar_tensor_tensor(out=t3, in0=o, scalar=0.5, in1=bc(ri), op0=ALU.mult,
                                               op1=ALU.mult).then_inc(*e.inc("o_used"))
                        dve.wait_ge(*e.last("o_used"))
                        v.tensor_tensor(y[:, m, 0:512], tmpo[:], zm[:, m, :], ALU.mult).then_inc(*e.inc("y"))
                        dve.wait_ge(*e.last("y"))
                        return
                    c = 1 if u["branch"] == "sel" else 2
                    link(v.tensor_tensor(wgt(), ri, gate_of(m, c), ALU.mult))
                    v.tensor_tensor(t3, o, bc(wgt()), ALU.mult).then_inc(*e.inc("o_used"))
                    dve.wait_ge(*e.last("o_used"))
                    link(v.tensor_tensor(y[:, m, 512:1024], y[:, m, 512:1024], tmpo[:], ALU.add))
                    if c == 2:
                        v.scalar_tensor_tensor(out=y[:, m, 512:1024], in0=y[:, m, 512:1024], scalar=0.5,
                                               in1=zn[:, m,
                                                      :], op0=ALU.mult, op1=ALU.mult).then_inc(*e.inc("y"))
                        dve.wait_ge(*e.last("y"))

                attention(UNITS["lay"], finish)
                h_lo_psum()
                raw_to(999)
                dve.wait_ge(*e.at("ysq", 4))
                link(v.tensor_tensor(st[:, s_sq + 2:s_sq + 3], st[:, 240:241], st[:, 241:242], ALU.add))
                v.tensor_tensor(st[:, s_sq + 3:s_sq + 4], st[:, 242:243], st[:, 243:244],
                                ALU.add).then_inc(*e.inc("sq"))
                dve.wait_ge(*e.at("sq", 3))
                dve.wait_ge(*e.at("rstd", 2))
                for m in range(MT):
                    tmp = hb[:].rearrange("p a b -> p (a b)")
                    src = PS[:, 4 + 2 * m:6 + 2 * m, :].rearrange("p a b -> p (a b)")
                    link(v.scalar_tensor_tensor(out=tmp, in0=src, scalar=st[:, s_rs + 2 + m:s_rs + 3 + m],
                                                in1=gate[0][:], op0=ALU.mult, op1=ALU.mult))
                    v.tensor_tensor(x[:, m, :], x[:, m, :], tmp, ALU.add).then_inc(*e.inc("x"))
                    dve.wait_ge(*e.last("x"))

            start("na")
            make_ab(1, pcol("bcol", 0, 16))
            split_to(2)
            norm(xn_n, ab[:, 0, :], ab[:, 1, :])
            for s in range(6):
                split_to(min(2 * s + 2 + SPL, 15))
            dve.wait_ge(*e.at("rp_in", 1, 16))
            link(v.tensor_tensor(rp[:], pcol("namask").unsqueeze(1).broadcast_to([P, 96, 64]), rp[:], ALU.subtract))

            def finish_plain(dst):
                def finish(u, o, ri):
                    m, b = u["m"], u["branch"]
                    v.tensor_tensor(dst[:, m, b * 512:(b + 1) * 512].rearrange("p (h d) -> p h d", h=8),
                                    o, bc(ri), ALU.mult).then_inc(*e.inc("o_used"))
                    dve.wait_ge(*e.last("o_used"))
                return finish

            attention(UNITS["na"], finish_plain(nao))
            h_lo_psum()
            raw_to(999)
            update_x(gate[1], 16)

            start("ffn")
            make_ab(0, pcol("bcol", 16, 32))
            split_to(2)
            norm(xn_f, ab[:, 0, :], ab[:, 1, :])
            mlp(FFN_SLOTS, True)
            update_x(gate[0], SPLITS["ffn"])

            start("mla")
            make_ab(1, pcol("bcol", 32, 48))
            split_to(3)
            norm(xn_m, ab[:, 0, :], ab[:, 1, :])
            dve.wait_ge(*e.at("rstd", 2))
            dve.wait_ge(*e.at("down_used", 2))
            kt4 = hb[:, 3, 0:128]
            for m in range(MT):
                v.tensor_scalar(cn[:, m, 0:256], dsb[:, m, 0:256], st[:, s_rs + 2 + m:s_rs + 3 + m], None,
                                ALU.mult).then_inc(*e.inc("cn"))
                dve.wait_ge(*e.last("cn"))
                link(v.tensor_scalar(cn[:, m, 256:384], dsb[:, m, 256:384], st[:, s_rs + 4 + m:s_rs + 5 + m], None,
                                     ALU.mult))
                x1, x2 = dsb[:, m, 384:400], dsb[:, m, 400:416]
                cc, ss = pcol("kcos", m * 16, m * 16 + 16), pcol("ksin", m * 16, m * 16 + 16)
                q = [kt4[:, i * 16:(i + 1) * 16] for i in range(4)]
                for dst, p0, p1 in ((q[0], x1, cc), (q[1], x2, ss), (q[2], x1, ss), (q[3], x2, cc)):
                    link(v.tensor_tensor(dst, p0, p1, ALU.mult))
                k0 = cn[:, m, 384:512].rearrange("p (r i) -> p r i", r=4)
                link(v.tensor_tensor(k0[:, :, 0:16], q[0].unsqueeze(1).broadcast_to([P, 4, 16]),
                                     q[1].unsqueeze(1).broadcast_to([P, 4, 16]), ALU.subtract))
                v.tensor_tensor(k0[:, :, 16:32], q[2].unsqueeze(1).broadcast_to([P, 4, 16]),
                                q[3].unsqueeze(1).broadcast_to([P, 4, 16]), ALU.add).then_inc(*e.inc("cn"))
                dve.wait_ge(*e.last("cn"))
            dve.wait_ge(*e.at("c_t", 1))
            for k in range(3):
                ins = v.tensor_scalar(hb[:, k, :], PS[:, 4 + k // 2, (k % 2) * S:(k % 2 + 1) * S],
                                      pcol("lnorm", k, k + 1), None, ALU.mult)
                if k < 2:
                    link(ins)
            ins.then_inc(*e.inc("c_f"))
            dve.wait_ge(*e.last("c_f"))
            v.tensor_copy(kr[:], PS[:, 5, S:2 * S]).then_inc(*e.inc("c"))
            dve.wait_ge(*e.last("c"))
            dve.wait_ge(*e.at("c_hi", 1))
            v.tensor_tensor(hl[:, 0:3, :], hb[:, 0:3, :], hh[:, 0:3, :].bitcast(F32),
                            ALU.subtract).then_inc(*e.inc("c"))
            dve.wait_ge(*e.last("c"))
            split_to(5)
            dve.wait_ge(*e.at("split_used", 4))
            tab = lambda n: pcol(n).unsqueeze(1).broadcast_to([P, 4, S])
            link(v.tensor_tensor(mt2[:], PS[:, 6:8, :].rearrange("p a b -> p (a b)").rearrange("p (k s) -> p k s", s=S),
                                 tab("qsin"), ALU.mult))
            v.tensor_tensor(mr[:], PS[:, 4:6, :].rearrange("p a b -> p (a b)").rearrange("p (k s) -> p k s", s=S),
                            tab("qcos"), ALU.mult).then_inc(*e.inc("mr"))
            dve.wait_ge(*e.last("mr"))
            v.tensor_tensor(mr[:], mr[:], mt2[:], ALU.add).then_inc(*e.inc("mr"))
            dve.wait_ge(*e.last("mr"))
            dve.wait_ge(*e.at("split_used", 5))
            v.tensor_copy(mv[:].rearrange("p m d -> p (m d)"),
                          PS[:, 4:8, :].rearrange("p a b -> p (a b)")).then_inc(*e.inc("mkv"))
            split_to(8)
            attention(UNITS["mla"], finish_plain(mo))
            h_lo_psum()
            raw_to(999)
            update_x(gate[1], 9)

            e.enter("rt")
            make_ab(2, pcol("bcol", 48, 64))
            norm(xn_f, ab[:, 0, :], ab[:, 1, :])
            for m in range(MT):
                r8 = rw[:, m * 8:m * 8 + 8]
                dve.wait_ge(*e.at("router", m + 1))
                v.tensor_copy(r8, PS[:, m, 0:NEXP]).then_inc(*e.inc("route_read"))
                dve.wait_ge(*e.last("route_read"))
                link(v.tensor_reduce(rw[:, 16 + m:17 + m], r8, AX_X, ALU.max))
                v.tensor_scalar(rw[:, 16 + m:17 + m], rw[:, 16 + m:17 + m], -1.0, None,
                                ALU.mult).then_inc(*e.inc("rmax"))
                dve.wait_ge(*e.last("rmax"))
            for m in range(MT):
                r8 = rw[:, m * 8:m * 8 + 8]
                dve.wait_ge(*e.at("rexp", m + 1))
                link(v.reciprocal(rw[:, 20:21], rw[:, 18 + m:19 + m]))
                link(v.tensor_scalar(r8, r8, rw[:, 20:21], None, ALU.mult))
                other = r8.unsqueeze(1).broadcast_to([P, 8, 8])
                own = r8.unsqueeze(2).broadcast_to([P, 8, 8])
                gt = rw[:, 64:128].rearrange("p (a b) -> p a b", a=8)
                eq = rw[:, 128:192].rearrange("p (a b) -> p a b", a=8)
                link(v.tensor_tensor(gt, other, own, ALU.is_gt))
                link(v.tensor_tensor(eq, other, own, ALU.is_equal))
                link(v.tensor_tensor(rw[:, 128:192], rw[:, 128:192], pcol("lower"), ALU.mult))
                link(v.tensor_tensor(rw[:, 64:128], rw[:, 64:128], rw[:, 128:192], ALU.add))
                link(v.tensor_reduce(rw[:, 24:32], gt, AX_X, ALU.add))
                link(v.scalar_tensor_tensor(out=r8, in0=rw[:, 24:32], scalar=1.5, in1=r8, op0=ALU.is_lt,
                                            op1=ALU.mult))
                link(v.tensor_reduce(rw[:, 21:22], r8, AX_X, ALU.add))
                link(v.reciprocal(rw[:, 22:23], rw[:, 21:22]))
                link(v.tensor_scalar(r8, r8, rw[:, 22:23], None, ALU.mult))
            link(v.memset(ysum[:], 0.0))

            with dve.Fori(0, NEXP) as rep:
                start("moe", rep)
                mlp(MOE_SLOTS, False)
                dve.wait_ge(*e.at("split_used", SPLITS["moe"]))
                for m in range(MT):
                    w = rw[:, m * 8:m * 8 + 8][:, bass.ds(rep, 1)]
                    v.scalar_tensor_tensor(out=ysum[:, m, :],
                                           in0=PS[:, 4 + 2 * m:6 + 2 * m, :].rearrange("p a b -> p (a b)"),
                                           scalar=w, in1=ysum[:, m,
                                                              :], op0=ALU.mult, op1=ALU.add).then_inc(*e.inc("y_used"))
                    dve.wait_ge(*e.last("y_used"))

            e.enter("end")
            dve.wait_ge(*e.at("y_used", 0))
            dve.wait_ge(*e.at("bank3", 0))
            for m in range(MT):
                tmp = hb[:].rearrange("p a b -> p (a b)")
                link(v.tensor_tensor(tmp, ysum[:, m, :], gate[2][:], ALU.mult))
                v.tensor_tensor(x[:, m, :], x[:, m, :], tmp, ALU.add).then_inc(*e.inc("x_last"))
                dve.wait_ge(*e.last("x_last"))
            dve.wait_ge(*e.at("rstd", 1))
            dve.wait_ge(*e.at("fnorm", 0, 16))
            for m in range(MT):
                v.scalar_tensor_tensor(out=xn_f[:, m, :], in0=x[:, m, :],
                                       scalar=st[:, s_rs + m:s_rs + m + 1], in1=fnorm[:],
                                       op0=ALU.mult, op1=ALU.mult).then_inc(*e.inc("final"))
                dve.wait_ge(*e.last("final"))
    return sg


def tables():
    f = np.float32
    p = np.arange(P)
    slopes = (2.0 ** (-8.0 * np.arange(1, 9) / 8)).astype(f)
    c = {}
    c["ident"] = np.eye(P, dtype=f)
    c["zeros"] = np.zeros((P, S), f)
    al = np.zeros((P, 8, 384), f)
    for m in range(MT):
        n = (m + 1) * P
        d = (m * P + p)[:, None] - np.arange(n)[None, :]
        b = slopes[None, :, None] * d[:, None, :]
        al[:, :, m * P:m * P + n] = np.where(d[:, None, :] >= 0, b, FAR)
    c["alibi"] = al.reshape(P, -1)
    ac = np.zeros((P, MT, 8, 16), f)
    ok = np.zeros((P, MT, 16), f)
    for m in range(MT):
        d = (m * P + p)[:, None] - (np.arange(16) * 16 + 31)[None, :]
        ac[:, m] = np.where(d[:, None, :] >= 0, slopes[None, :, None] * d[:, None, :], FAR)
        ok[:, m] = d >= 0
    c["alibi_c"] = ac.reshape(P, -1)
    c["ok_c"] = ok.reshape(P, -1)
    rs = np.zeros((P, 2, P), f)
    for g in range(2):
        for h in range(4 * g, 4 * g + 4):
            for t in range(T_CMP):
                rs[t, g, h * 16 + t] = 1.0
    c["rep_sel"] = rs.reshape(P, -1)
    c["mask8"] = (p[:, None] // 16 == np.arange(8)[None, :]).astype(f)
    col = p % 64
    first = np.clip(col - 8, 0, 48)[:, None]
    kc = np.arange(64)[None, :]
    c["namask"] = np.where((kc >= first) & (kc < first + 16), 0.0, FAR).astype(f)
    t = np.arange(S)
    inv = (10000.0 ** (-np.arange(8, dtype=f) / 8)).astype(f)
    ang = np.concatenate([(t // 64).astype(f)[:, None] * inv, (t % 64).astype(f)[:, None] * inv], axis=1)
    cos, sin = np.cos(ang).astype(f), np.sin(ang).astype(f)
    c["kcos"] = cos.reshape(MT, P, 16).transpose(1, 0, 2).reshape(P, 32)
    c["ksin"] = sin.reshape(MT, P, 16).transpose(1, 0, 2).reshape(P, 32)
    i = p % 32
    c["qcos"] = (-MS * cos[:, i % 16].T).astype(f)
    c["qsin"] = (np.where(i < 16, MS, -MS)[:, None] * sin[:, i % 16].T).astype(f)
    c["lower"] = np.broadcast_to(np.tril(np.ones((8, 8), f), -1).reshape(1, 64), (P, 64))
    return c


def kernel(**inputs):
    import concourse.bacc as bacc
    from concourse.bass_utils import run_bass_kernel_spmd

    a = {k: np.asarray(v) for k, v in inputs.items()}
    f = np.float32

    def cols(vec):
        return np.ascontiguousarray(vec.reshape(-1, P).T)

    def ktiles(w):
        n = w.shape[0] // P
        return w.reshape(n, P, -1).transpose(1, 0, 2).reshape(P, -1)

    ws = np.zeros((NSTEPS, P, STEP), f)
    pos = [0]

    def put(block):
        ws[pos[0], :, :block.shape[1]] = block
        pos[0] += 1

    def halves(w):
        return [ktiles(w[:512]), ktiles(w[512:])]

    def emit(phase, splits, ada, ck=None):
        for step in STEPS[phase]:
            if step[0] == "w":
                put(splits[step[1]])
            elif step[0] == "ada":
                u, j = divmod(step[1], 6)
                put(halves(ada[u][:, j * 512:(j + 1) * 512])[step[2]])
            else:
                put(ck)

    units = [a["w_ada"][0], a["w_ada"][1]]
    bias = [a["b_ada"][0], a["b_ada"][1]]
    for l in range(2):
        for h in range(2):
            units.append(a["w_ada_2"][l][:, h * 3072:(h + 1) * 3072])
            bias.append(a["b_ada_2"][l][h * 3072:(h + 1) * 3072])

    def mlp_blocks(gu, down, slots):
        n = slots * 256
        ups = [np.concatenate([gu[:, s * 256:(s + 1) * 256], gu[:, n + s * 256:n + (s + 1) * 256]], axis=1)
               for s in range(slots)]
        out = list(halves(ups[0]))
        for s in range(1, slots):
            out += halves(ups[s]) + [ktiles(down[(s - 1) * 256:s * 256])]
        return out + [ktiles(down[(slots - 1) * 256:])]

    emit("pre", [], [units[0]])
    nsa = np.concatenate([np.arange(h * HD, (h + 1) * HD) for j in range(4) for h in (j, 4 + j)])
    for l in range(2):
        w = a["w_in"][l]
        q, kvo = w[:, 2048:2560][:, nsa], 2560
        part = lambda i: w[:, kvo + i * P:kvo + (i + 1) * P]
        slots = [w[:, 0:512], w[:, 512:1024], w[:, 1024:1536], w[:, 1536:2048], q,
                 np.concatenate([part(0), part(1), part(2), part(4)], axis=1),
                 np.concatenate([part(3), part(5), w[:, 3328:3352]], axis=1), w[:, 3352:3864],
                 a["w_out"][l][:, 0:512], a["w_out"][l][:, 512:1024]]
        ck = np.concatenate([ktiles(a["w_ck1"][l]), ktiles(a["w_cv1"][l])], axis=1)
        emit("lay", [b for s in slots for b in halves(s)], [units[l + 1]], ck)
    w, wo = a["na_w_qkv_2"][0], a["na_w_o_2"][0]
    slots = [w[:, s * 512:(s + 1) * 512] for s in range(6)] + [wo[:, 0:512], wo[:, 512:1024]]
    emit("na", [b for s in slots for b in halves(s)], [units[3]])
    emit("ffn", mlp_blocks(a["ffn_w_gu_2"][0], a["ffn_w_down_2"][0], FFN_SLOTS), [units[4], units[5]])
    uq = a["mla_w_uq_2"][0].reshape(256, 16, 96)
    nope, r1, r2 = uq[:, :, :64], uq[:, :, 64::2], uq[:, :, 65::2]
    ukv = a["mla_w_ukv_2"][0].reshape(P, 16, 2, 64)
    down = a["mla_w_down_2"][0]
    down = np.concatenate([down[:, :384], down[:, 384::2], down[:, 385::2]], axis=1)
    wo = a["mla_w_o_2"][0]
    emit("mla", halves(down) + [
        ktiles(nope.reshape(256, 1024)),
        ktiles(np.concatenate([np.concatenate([r1, r2], axis=2).reshape(256, 512),
                               np.concatenate([r2, r1], axis=2).reshape(256, 512)], axis=1)),
        np.concatenate([ukv[:, :, 0].reshape(P, 1024), ukv[:, :, 1].reshape(P, 1024)], axis=1),
    ] + halves(wo[:, 0:512]) + halves(wo[:, 512:1024]), [])
    for x in range(NEXP):
        emit("moe", mlp_blocks(a["moe_w_gu_2"][0, x], a["moe_w_down_2"][0, x], MOE_SLOTS), [])
    assert pos[0] == NSTEPS

    c = tables()

    def rows64(w):
        out = np.zeros((P, w.shape[1]), f)
        out[:HD] = w
        return out

    lp = np.stack([np.concatenate([
        cols(a["g_pre"][l]), cols(bias[l][:2048]), ktiles(a["pe_k"][l].reshape(-1, 1)),
        ktiles(a["pe_v"][l].reshape(-1, 1)), rows64(a["w_ck2"][l]), rows64(a["w_cv2"][l])], axis=1)
        for l in range(2)], axis=1)
    c["lpall"] = lp.reshape(P, -1)
    c["bcol"] = np.concatenate([cols(bias[u][:2048]) for u in range(2, 6)], axis=1)
    c["cc"] = np.concatenate([cols(a["c"][0]), cols(a["c_2"][0])], axis=1)
    c["lnorm"] = np.concatenate([cols(a["mla_q_norm_2"][0]), cols(a["mla_kv_norm_2"][0])], axis=1)
    c["router"] = ktiles(a["moe_w_router_2"][0])
    par_names = ["ident", "zeros", "namask", "kcos", "ksin", "qcos", "qsin", "lower", "lpall", "bcol", "cc",
                 "lnorm", "router"]
    lc_names = ["alibi", "alibi_c", "ok_c", "rep_sel", "mask8"]
    dc = np.clip(np.arange(64)[None, :] - (np.arange(P) % 64)[:, None] + 15, 0, 30)
    dr = np.arange(6)[None, :] + 5 - (np.arange(P) // 64)[:, None]
    rp = a["na_rpb_2"][0][:, dr[:, :, None], dc[:, None, :]].transpose(1, 0, 2, 3).reshape(P, 96, 64)
    arrays = {
        "ws": ws,
        "x": a["x"][0].reshape(MT, P, D).transpose(1, 0, 2),
        "par": np.concatenate([c[n] for n in par_names], axis=1),
        "lc": np.concatenate([c[n] for n in lc_names], axis=1),
        "rp": rp,
        "brow": np.stack([b[2048:] for b in bias])[:, None, :],
        "gpost": np.ascontiguousarray(np.broadcast_to(a["g_post"][:, None, :], (2, P, D))),
        "fnorm": np.ascontiguousarray(np.broadcast_to(a["final_norm_2"][None, :], (P, D))),
    }
    arrays = {k: np.ascontiguousarray(v, dtype=f) for k, v in arrays.items()}

    nc = bacc.Bacc("TRN2", target_bir_lowering=False, num_devices=1)
    dram = {k: nc.dram_tensor(f"in_{k}", v.shape, F32, kind="ExternalInput").ap() for k, v in arrays.items()}
    dram["out"] = nc.dram_tensor("out_0", (P, MT, D), F32, kind="ExternalOutput").ap()
    dram["par_cols"] = [(n, c[n].shape[1]) for n in par_names]
    dram["lc_cols"] = [(n, c[n].shape[1]) for n in lc_names]
    build(nc, dram)
    r = run_bass_kernel_spmd(nc, [{f"in_{k}": v for k, v in arrays.items()}], core_ids=[0])
    return r.results[0]["out_0"].transpose(1, 0, 2).reshape(1, S, D)
```

```python
from contextlib import ExitStack

import numpy as np
import concourse.bass as bass
from concourse import mybir

F32 = mybir.dt.float32
F32R = mybir.dt.float32r
ALU = mybir.AluOpType
ACT = mybir.ActivationFunctionType
AX_X = mybir.AxisListType.X

P = 128
D = 1024
S = 256
MT = S // P
KT = D // P
HD = 64
STEP = 2048
RAW = 6
SPL = 3
EPS = 1e-6
FAR = 1e12
QS = HD ** -0.5
MS = 96 ** -0.5
NEXP = 8
FFN_SLOTS = 11
MOE_SLOTS = 7
T_CMP = 15

PHASES = ["pre", "lay", "na", "ffn", "mla", "rt", "go", "moe", "fin", "more", "end"]
MORE = 2 * S // (P + 1)
REPS = {"lay": 2, "moe": NEXP, "more": MORE}


def ada_steps(j):
    return [("ada", j, 0), ("ada", j, 1)]


def layer_steps():
    out, n = [], 0
    for s in range(8):
        out += [("w", n), ("w", n + 1)]
        n += 2
        if s < 6:
            out += ada_steps(s)
    out.append(("ck",))
    return out + [("w", n + i) for i in range(4)]


def na_steps():
    out = []
    for s in range(6):
        out += [("w", 2 * s), ("w", 2 * s + 1)] + ada_steps(s)
    return out + [("w", 12 + i) for i in range(4)]


def ffn_steps():
    out, n = [], 0
    for s in range(FFN_SLOTS):
        out += [("w", n), ("w", n + 1)] + ada_steps(s)
        n += 2
        if s >= 1:
            out.append(("w", n))
            n += 1
    return out + ada_steps(FFN_SLOTS) + [("w", n)]


STEPS = {
    "pre": [x for j in range(6) for x in ada_steps(j)],
    "lay": layer_steps(),
    "na": na_steps(),
    "ffn": ffn_steps(),
    "mla": [("w", i) for i in range(9)],
    "moe": [("w", i) for i in range(3 * MOE_SLOTS)],
    "more": [("w", i) for i in range(3 * MOE_SLOTS)],
}
STEPS = {p: STEPS.get(p, []) for p in PHASES}
SPLITS = {p: sum(x[0] == "w" for x in STEPS[p]) for p in PHASES}
NSTEPS = sum(len(STEPS[p]) * REPS.get(p, 1) for p in PHASES if p != "more")


def ffn_up(s):
    return 0 if s == 0 else 3 * s - 1


def ffn_down(s):
    return 3 * s + 4 if s < FFN_SLOTS - 1 else 3 * FFN_SLOTS - 1


def moe_up(s):
    return 2 * s if s < 2 else 3 * s - 2


def moe_down(s):
    return min(3 * s + 6, 2 * MOE_SLOTS + s)


def ring_plan(size, lengths):
    place, need, start = {}, {}, 0
    owner = [None] * size
    total = 0
    for p in PHASES:
        n, reps = lengths[p], REPS.get(p, 1)
        pad = -n % size if reps > 1 else 0
        place[p] = [(start + i) % size for i in range(n)]
        need[p] = [None] * n
        for _ in range(reps):
            for i in range(n):
                last = owner[place[p][i]]
                if last is not None:
                    k = last + 1 - total
                    need[p][i] = k if need[p][i] is None else max(need[p][i], k)
                owner[place[p][i]] = total + i
            total += n
        start = (start + n + pad) % size
    return place, need


RAW_AT, RAW_NEED = ring_plan(RAW, {p: len(STEPS[p]) for p in PHASES})
SPL_AT, SPL_NEED = ring_plan(SPL, SPLITS)
STEP_OF_SPLIT = {p: [i for i, x in enumerate(STEPS[p]) if x[0] == "w"] for p in PHASES}

COUNTS = {
    "act": {"ffn": 22},
    "act_hi": {"ffn": 22, "moe": 7, "more": 7},
    "act_lo": {"moe": 7, "more": 7},
    "act_tok": {"moe": 7, "more": 7},
    "act_turned": {"moe": 7, "more": 7},
    "ada_sum": {"pre": 6, "lay": 6, "na": 6, "ffn": 12},
    "bank0": {"lay": 6, "na": 4, "ffn": 8},
    "bank1": {"lay": 5, "na": 4, "ffn": 7},
    "bank2": {"lay": 5, "na": 4, "ffn": 7},
    "bank3": {"pre": 6, "lay": 6, "na": 6, "ffn": 12},
    "brow": {"pre": 1, "lay": 1, "na": 1, "ffn": 2},
    "c": {"mla": 2},
    "c_f": {"mla": 1},
    "c_hi": {"mla": 1},
    "c_t": {"mla": 1},
    "cexp": {"lay": 2},
    "chosen": {"rt": 2},
    "clogits": {"lay": 2},
    "cmp1": {"lay": 1},
    "cmp2": {"lay": 1},
    "cmp3": {"lay": 1},
    "cmp_act": {"lay": 1},
    "cmp_kv": {"lay": 2},
    "cmp_tanh": {"lay": 1},
    "cmp_u": {"lay": 1},
    "cn": {"mla": 4},
    "combined": {"moe": 4, "fin": 4, "more": 4},
    "consts": {"pre": 2},
    "cout": {"lay": 2},
    "cout_used": {"lay": 2},
    "cprobs": {"lay": 2},
    "cprobs_t": {"lay": 2},
    "cpt": {"lay": 2},
    "cs_tanh": {"pre": 1},
    "cscores": {"lay": 2},
    "down_used": {"mla": 2},
    "dve": {"pre": 39, "lay": 84, "na": 50, "ffn": 103, "mla": 28, "rt": 36, "go": 24, "moe": 14, "more": 14},
    "dve_end": {"end": 2},
    "final": {"end": 2},
    "fnorm": {"rt": 1},
    "g_tanh": {"lay": 1},
    "gathered": {"go": 2, "moe": 2, "more": 2},
    "gg": {"lay": 1},
    "gpost": {"lay": 1},
    "h": {"lay": 8, "na": 8, "ffn": 4, "mla": 8, "rt": 4},
    "h_hi": {"lay": 8, "na": 8, "ffn": 4, "mla": 8, "rt": 4},
    "hb": {"lay": 4, "na": 4, "ffn": 4, "mla": 4, "rt": 4},
    "hi": {"lay": 20, "na": 16, "ffn": 33, "mla": 9, "moe": 21, "more": 21},
    "kk": {"lay": 7},
    "lc_in": {"pre": 1},
    "logits": {"lay": 48, "na": 32, "mla": 32},
    "lp": {"lay": 1},
    "mean_sq": {"lay": 2, "na": 1, "ffn": 1, "mla": 3, "rt": 1, "end": 1},
    "mk_sum": {"mla": 1},
    "mkv": {"mla": 5},
    "mq": {"mla": 4},
    "mr": {"mla": 2},
    "o_used": {"lay": 6, "na": 4, "mla": 4},
    "over": {"go": 1},
    "par_in": {"pre": 1},
    "probs": {"lay": 48, "na": 32, "mla": 32},
    "probs_t": {"lay": 48, "na": 32, "mla": 32},
    "pt": {"lay": 48, "na": 32, "mla": 32},
    "pv": {"lay": 48, "na": 32, "mla": 32},
    "ranked": {"go": 1},
    "raw_in0": {"pre": 2, "lay": 6, "na": 5, "ffn": 10, "mla": 1, "moe": 4, "more": 4},
    "raw_in1": {"pre": 2, "lay": 6, "na": 5, "ffn": 9, "mla": 2, "moe": 3, "more": 3},
    "raw_in2": {"pre": 2, "lay": 6, "na": 5, "ffn": 9, "mla": 2, "moe": 3, "more": 3},
    "raw_in3": {"pre": 2, "lay": 5, "na": 5, "ffn": 9, "mla": 2, "moe": 3, "more": 3},
    "raw_in4": {"pre": 2, "lay": 5, "na": 4, "ffn": 10, "mla": 1, "moe": 4, "more": 4},
    "raw_in5": {"pre": 2, "lay": 5, "na": 4, "ffn": 10, "mla": 1, "moe": 4, "more": 4},
    "raw_used": {"pre": 12, "lay": 33, "na": 28, "ffn": 57, "mla": 9, "moe": 21, "more": 21},
    "rc": {"rt": 1},
    "rexp": {"rt": 2},
    "rmax": {"rt": 2},
    "route_read": {"rt": 2},
    "router": {"rt": 2},
    "rp_in": {"na": 1},
    "rstd": {"lay": 2, "na": 1, "ffn": 1, "mla": 2, "rt": 1, "end": 1},
    "scores": {"lay": 48, "na": 32, "mla": 32},
    "sel": {"go": 1, "moe": 1, "more": 1},
    "sel_t": {"go": 1, "moe": 1, "more": 1},
    "sel_turned": {"moe": 1, "more": 1},
    "split_used": {"pre": 3, "lay": 20, "na": 16, "ffn": 33, "mla": 9, "moe": 21, "more": 21},
    "sq": {"lay": 3, "na": 2, "ffn": 2, "mla": 6, "rt": 2, "end": 2},
    "stored": {"end": 2},
    "tanh": {"ffn": 22, "moe": 7, "more": 7},
    "turned": {"lay": 8, "na": 8, "ffn": 4, "mla": 8, "rt": 4},
    "vb": {"lay": 1},
    "x": {"pre": 1, "lay": 2, "na": 2, "ffn": 2, "mla": 2},
    "x_f": {"go": 2, "moe": 2, "more": 2},
    "x_hi": {"go": 2, "moe": 2, "more": 2},
    "x_in": {"pre": 1},
    "x_last": {"end": 2},
    "x_lo": {"go": 2, "moe": 2, "more": 2},
    "xn": {"lay": 2, "na": 2, "ffn": 2, "mla": 2, "rt": 2},
    "y": {"pre": 1, "lay": 4},
    "y_sb": {"moe": 2, "fin": 2, "more": 2},
    "y_used": {"moe": 4, "fin": 4, "more": 4},
    "ysq": {"lay": 4},
    "z_tanh": {"lay": 4},
}


class Signals:

    def __init__(self, nc, ctx):
        self.nc, self.ctx, self.sems, self.made = nc, ctx, {}, {}

    def sem(self, name):
        if name not in self.sems:
            self.sems[name] = self.ctx.enter_context(self.nc.semaphore(name))
        return self.sems[name]

    def value(self, name, phase, rep, k):
        c = COUNTS.get(name, {})
        base = 0
        for p in PHASES:
            if p == phase:
                break
            base += c.get(p, 0) * REPS.get(p, 1)
        per = c.get(phase, 0)
        return base + k + (rep * per if per and not isinstance(rep, int) else 0)


class Count:

    def __init__(self, signals):
        self.sg = signals
        self.phase, self.rep = "pre", 0
        self.own = {}

    def enter(self, phase, rep=0):
        self.phase, self.rep, self.own = phase, rep, {}

    def at(self, name, k, unit=1):
        v = self.sg.value(name, self.phase, self.rep, k)
        assert not isinstance(v, int) or v > 0, (name, self.phase, k, v)
        return self.sg.sem(name), v * unit

    def inc(self, name, unit=1):
        d = self.sg.made.setdefault(name, {})
        d[self.phase] = d.get(self.phase, 0) + 1
        self.own[name] = self.own.get(name, 0) + 1
        return self.sg.sem(name), unit

    def last(self, name):
        return self.at(name, self.own[name])


def build(nc, dram):
    ctx = ExitStack()
    with ctx:
        at = [nc.sbuf_base + (-nc.sbuf_base) % 64]

        def sb(name, shape, dt=F32, offset=None):
            size = int(np.prod(shape[1:])) * 4
            size += -size % 32
            if offset is None:
                offset = at[0]
                at[0] += size
            return nc.alloc_sbuf_tensor_at(name, shape, dt, offset=offset)

        raw = sb("raw", [P, RAW, STEP])
        wh = sb("w_hi", [P, SPL, STEP], F32R)
        wl = sb("w_lo", [P, SPL, STEP], F32R)
        hh = sb("h_hi", [P, KT, S], F32R)
        hl = sb("h_lo", [P, KT, S], F32R)
        x = sb("x", [P, MT, D])
        gate = [sb("gate0", [P, D]), sb("gate1", [P, D])]
        acc = sb("acc", [P, 2, 512])
        brow = sb("brow", [1, D])
        par = sb("par", [P, dram["par"].shape[1]])
        cs = sb("cs", [P, 2, KT])
        csc = sb("cs_cur", [P, KT])
        modc = sb("modc", [P, 3, 16])
        ab = sb("ab", [P, 2, KT])
        st = sb("st", [P, 256])
        ones = sb("ones", [P, P])
        spare = sb("spare", [P, 8])
        work = at[0]
        hb = sb("hb", [P, 4, S])
        pt = sb("pt", [P, 2, S])
        lg = sb("lg", [P, 2, S], offset=work)
        pr = sb("pr", [P, 2, S], offset=work + 2048)
        gate2_at = at[0]
        gate.append(sb("gate2", [P, D]))
        arena = at[0]
        top = nc.sbuf_top

        def region(start):
            pos = [start]

            def take(name, shape, dt=F32):
                off = pos[0]
                size = int(np.prod(shape[1:])) * 4
                pos[0] += size + (-size % 32)
                assert pos[0] <= top, (name, pos[0] - top)
                return nc.alloc_sbuf_tensor_at(name, shape, dt, offset=off)
            return take, pos

        take, pos = region(gate2_at)
        lc = take("lc", [P, dram["lc"].shape[1]])
        y_at = pos[0]
        y = take("y", [P, MT, D])
        qm = take("qm", [P, 4, S])
        km = take("km", [P, 4, S])
        vm = take("vm", [P, MT, 512])
        zm = take("zm", [P, MT, 512])
        qn = take("qn", [P, 4, S])
        ksw = take("ksw", [P, 2, S])
        vsw = take("vsw", [P, MT, 280])
        zn_at = pos[0]
        zn = take("zn", [P, MT, 512])
        lpc = take("lpc", [P, 184])
        cw = take("cw", [P, 512])
        kk_at = pos[0]
        kk = take("kk", [P, 2, 2, S])
        xn_l = nc.alloc_sbuf_tensor_at("xn_l", [P, MT, D], F32, offset=y_at)
        gpost = nc.alloc_sbuf_tensor_at("gpost", [P, D], F32, offset=zn_at)
        vb = nc.alloc_sbuf_tensor_at("vb", [P, 512], F32, offset=kk_at)
        tmpo = nc.alloc_sbuf_tensor_at("tmpo", [P, 512], F32, offset=kk_at + 2048)
        take, pos = region(gate2_at)
        rp = take("rp", [P, 16 * 6, 64])
        naq = take("naq", [P, 8, S])
        nak = take("nak", [P, 8, S])
        nav = take("nav", [P, MT, D])
        o_at = pos[0]
        nao = take("nao", [P, MT, D])
        xn_n = nc.alloc_sbuf_tensor_at("xn_n", [P, MT, D], F32, offset=o_at)
        take, pos = region(arena)
        ysum = take("ysum", [P, MT, D])
        xn_f = take("xn_f", [P, MT, D])
        ah = take("a_hi", [P, 2, 2, S], F32R)
        al = take("a_lo", [P, 2, 2, S], F32R)
        fnorm = take("fnorm", [P, D])
        rw = take("rw", [P, 320])
        ysb = take("ysb", [P, D])
        xg = take("xg", [P, KT, P])
        sel = take("sel", [P, MT, P])
        selt = take("sel_t", [P, S])
        rc = take("rc", [P, dram["rc"].shape[1]])
        row_no, before = rc[:, 0:S], rc[:, S:S + P]
        wcol = take("wcol", [P, MT, NEXP + 1])
        pos_of = take("pos_of", [P, MT, NEXP + 1])
        over = nc.alloc_sbuf_tensor_at("over", [P, 1 + MORE], mybir.dt.int32, offset=pos[0])
        take, pos = region(arena)
        dsb = take("dsb", [P, MT, 416])
        cn = take("cn", [P, MT, 512])
        mq = take("mq", [P, 8, S])
        mr = take("mr", [P, 4, S])
        mt2 = take("mt2", [P, 4, S])
        kr = take("kr", [P, S])
        mk = take("mk", [P, 8, S])
        mv = take("mv", [P, MT, D])
        mo = take("mo", [P, MT, D])
        xn_m = nc.alloc_sbuf_tensor_at("xn_m", [P, MT, D], F32, offset=arena)

        PS = ctx.enter_context(nc.psum_tensor("PS", [P, 8, 512], F32))

        pc = {}
        o = 0
        for name, n in dram["par_cols"]:
            pc[name] = (o, n)
            o += n

        def pcol(name, a=0, b=None):
            s0, n = pc[name]
            return par[:, s0 + a:s0 + (n if b is None else b)]

        lcc = {}
        o = 0
        for name, n in dram["lc_cols"]:
            lcc[name] = (o, n)
            o += n

        def lcol(name):
            s0, n = lcc[name]
            return lc[:, s0:s0 + n]

        ident = pcol("ident")
        alibi = lcol("alibi").rearrange("p (h k) -> p h k", h=8)
        alibi_c = lcol("alibi_c").rearrange("p (m h t) -> p m h t", m=2, h=8)
        ok_c = lcol("ok_c").rearrange("p (m t) -> p m t", m=2)
        rep_sel = lcol("rep_sel").rearrange("p (g q) -> p g q", g=2)
        mask8 = lcol("mask8")
        LP = {}
        o = 0
        for name, n in (("gpre", 8), ("bcol", 16), ("pek", 16), ("pev", 16), ("ck2", 64), ("cv2", 64)):
            LP[name] = lpc[:, o:o + n]
            o += n
        lpall = pcol("lpall").rearrange("p (l n) -> p l n", l=2)

        SQ = slice(0, 8)
        s_sq, s_ms, s_rs, s_half = 0, 8, 16, 24
        mn = lambda u: st[:, 32 + u:33 + u]
        sm = lambda u: st[:, 96 + u:97 + u]
        rinv = lambda a, b: st[:, 160 + a:160 + b]
        wgt = lambda: st[:, 224:232]

        sg = Signals(nc, ctx)
        settled = sg.sem("settled")

        def attention_units(kind):
            out = []
            groups = {"lay": [(b, m) for b in ("moba", "sel", "win") for m in range(2)],
                      "na": [(b, m) for b in (0, 1) for m in range(2)],
                      "mla": [(b, m) for b in (0, 1) for m in range(2)]}[kind]
            for gi, (b, m) in enumerate(groups):
                for h in range(8):
                    u = dict(group=gi, branch=b, m=m, col=h, nk=S)
                    tok = slice(m * P, (m + 1) * P)
                    if kind == "lay":
                        u["nk"] = nk = (m + 1) * P
                        u["bias"] = alibi[:, h, m * P:m * P + nk]
                        if b == "moba":
                            r = slice((h % 2) * HD, (h % 2) * HD + HD)
                            u["s"] = [(qm[r, h // 2, tok], km[r, h // 2, 0:nk])]
                            u["v"] = [vm[:, t, h * HD:(h + 1) * HD] for t in range(m + 1)]
                        else:
                            w, g, j = (0 if b == "sel" else 1), h // 4, h % 4
                            r = slice(g * HD, g * HD + HD)
                            u["s"] = [(qn[r, j, tok], ksw[r, w, 0:nk])]
                            u["v"] = [vsw[:, t, w * P + g * HD:w * P + (g + 1) * HD] for t in range(m + 1)]
                    elif kind == "na":
                        hh_ = b * 8 + h
                        r = slice((hh_ % 2) * HD, (hh_ % 2) * HD + HD)
                        u["s"] = [(naq[r, hh_ // 2, tok], nak[r, hh_ // 2, :])]
                        u["v"] = [nav[:, t, hh_ * HD:(hh_ + 1) * HD] for t in range(2)]
                        first = 2 if m == 0 else 0
                        u["bias"] = rp[:, hh_ * 6 + first:hh_ * 6 + first + 4, :].rearrange("p a b -> p (a b)")
                    else:
                        hh_ = b * 8 + h
                        r = slice((hh_ % 2) * HD, (hh_ % 2) * HD + HD)
                        rr = slice((hh_ % 4) * 32, (hh_ % 4) * 32 + 32)
                        u["s"] = [(mq[r, hh_ // 2, tok], mk[r, hh_ // 2, :]),
                                  (mr[rr, hh_ // 4, tok], kr[rr, :])]
                        u["v"] = [mv[:, t, hh_ * HD:(hh_ + 1) * HD] for t in range(2)]
                        u["bias"] = pcol("zeros")
                    out.append(u)
            return out

        UNITS = {k: attention_units(k) for k in ("lay", "na", "mla")}
        S_BANK, PT_BANK, O_BANK, C_BANK = (4, 5), (0, 1), (2, 3), (6, 7, 3, 2)

        def gbank(use):
            return use % 3

        def overfull(engine):
            return engine.value_load(over[0:1, 0:1], min_val=0, max_val=MORE)

        def uses_to(use):
            return sum(gbank(q) == gbank(use) for q in range(use + 1))

        block = ctx.enter_context(nc.Block())

        @block.sync
        def _(sp):
            e = Count(sg)

            def stream(phase, rep, base):
                for i in range(len(STEPS[phase])):
                    if RAW_NEED[phase][i] is not None:
                        sp.wait_ge(*e.at("raw_used", RAW_NEED[phase][i]))
                    r = RAW_AT[phase][i]
                    src = rep * len(STEPS[phase]) + base + i if not isinstance(rep, int) else base + i
                    sp.dma_start(raw[:, r, :], dram["ws"][src]).then_inc(*e.inc(f"raw_in{r}", 16))

            base = 0
            for p in ("pre", "lay", "na", "ffn", "mla", "moe"):
                if p == "lay":
                    sp.dma_start(x[:], dram["x"]).then_inc(*e.inc("x_in", 16))
                    sp.dma_start(lc[:], dram["lc"]).then_inc(*e.inc("lc_in", 16))
                if p == "pre":
                    e.enter(p)
                    sp.dma_start(par[:], dram["par"]).then_inc(*e.inc("par_in", 16))
                if p in REPS:
                    with sp.Fori(0, REPS[p]) as rep:
                        e.enter(p, rep)
                        stream(p, rep, base)
                else:
                    if p != "pre":
                        e.enter(p)
                    stream(p, 0, base)
                if p != "moe":
                    base += len(STEPS[p]) * REPS.get(p, 1)
            sp.wait_ge(*e.at("over", 0))
            count = overfull(sp)
            with sp.Fori(0, MORE) as rep:
                e.enter("more", rep)
                with sp.If(count > rep):
                    which = sp.value_load(over[0:1, bass.ds(rep + 1, 1)], min_val=0, max_val=NEXP - 1)
                    stream("more", which, base)
            e.enter("end")
            for m in range(MT):
                sp.wait_ge(*e.at("final", m + 1))
                sp.dma_start(dram["out"][:, m, :], xn_f[:, m, :]).then_inc(*e.inc("stored", 16))
            sp.wait_ge(*e.at("stored", MT, 16))

        @block.gpsimd
        def _(pool):
            g = nc.gpsimd
            e = Count(sg)
            e.enter("pre")
            g.memset(ones[:], 1.0).then_inc(*e.inc("consts"))
            g.memset(st[:], -0.5).then_inc(*e.inc("consts"))

            def rstd(sq_wait, spans):
                pool.wait_ge(*e.at("sq", sq_wait))
                pool.sem_inc(settled)
                for a, b, n in spans:
                    g.tensor_scalar(st[:, s_ms + a:s_ms + b], st[:, s_sq + a:s_sq + b],
                                    1.0 / n, EPS, ALU.mult, ALU.add).then_inc(*e.inc("mean_sq"))
                    pool.wait_ge(*e.last("mean_sq"))
                    pool.sem_inc(settled)
                a, b = spans[0][0], spans[-1][1]
                g.tensor_tensor(st[:, s_rs + a:s_rs + b], st[:, s_ms + a:s_ms + b],
                                st[:, s_half:s_half + b - a], ALU.pow).then_inc(*e.inc("rstd"))

            for name, n in (("x", 1), ("y", 1), ("split_used", SPL)):
                for _ in range(n):
                    g.memset(spare[:], 0.0).then_inc(*e.inc(name))
                    pool.wait_ge(*e.at(name, e.own[name]))
            pool.wait_ge(*e.at("consts", 2))
            with pool.Fori(0, 2) as rep:
                e.enter("lay", rep)
                rstd(2, [(0, 2, D)])
                rstd(3, [(2, 4, D)])
            e.enter("na")
            rstd(2, [(0, 2, D)])
            e.enter("ffn")
            rstd(2, [(0, 2, D)])
            e.enter("mla")
            rstd(2, [(0, 2, D)])
            rstd(6, [(2, 4, 256), (4, 6, 128)])
            e.enter("rt")
            rstd(2, [(0, 2, D)])
            e.enter("end")
            rstd(2, [(0, 2, D)])

        @block.tensor
        def _(pe):
            t = nc.tensor
            e = Count(sg)

            def mm3(out, lhs, rhs, start, stop):
                t.matmul(out, lhs[0], rhs[0], start=start, stop=False, skip_group_check=True)
                t.matmul(out, lhs[0], rhs[1], start=False, stop=False, skip_group_check=True)
                return t.matmul(out, lhs[1], rhs[0], start=False, stop=stop, skip_group_check=True)

            def arrived(n):
                pe.wait_ge(*e.at("raw_used", STEP_OF_SPLIT[e.phase][n] + 1))
                r = SPL_AT[e.phase][n]
                return wh[:, r, :], wl[:, r, :]

            used = {}

            def bank_free(b):
                if used.get(b, 0) or e.phase == "moe":
                    pe.wait_ge(*e.at(f"bank{b}", used.get(b, 0)))
                used[b] = used.get(b, 0) + 1

            def tok_slot(n, banks, width, first=True):
                for kh in range(2):
                    w = arrived(n + kh)
                    for m in range(MT):
                        if kh == 0 and first:
                            bank_free(banks[m])
                        for k in range(4):
                            kt = kh * 4 + k
                            lhs = [a[:, kt, m * P:(m + 1) * P] for a in (hh, hl)]
                            rhs = [a[:, k * width:(k + 1) * width] for a in w]
                            last = mm3(PS[:, banks[m], 0:width], lhs, rhs, kt == 0, kt == KT - 1)
                    last.then_inc(*e.inc("split_used"))

            def feat_slot(n, banks, order=(0, 1, 2, 3)):
                for kh in range(2):
                    w = arrived(n + kh)
                    for i, f in enumerate(order):
                        b = banks[i // 2]
                        if kh == 0 and i % 2 == 0:
                            bank_free(b)
                        for k in range(4):
                            kt = kh * 4 + k
                            lhs = [a[:, k * 512 + f * P:k * 512 + (f + 1) * P] for a in w]
                            last = mm3(PS[:, b, (i % 2) * S:(i % 2 + 1) * S], lhs, (hh[:, kt, :], hl[:, kt, :]),
                                       kt == 0 and i % 2 == 0, kt == KT - 1)
                    last.then_inc(*e.inc("split_used"))

            def ada(j):
                pe.wait_ge(*e.at("raw_used", [i for i, s in enumerate(STEPS[e.phase]) if s == ("ada", j, 1)][0] + 1))
                bank_free(3)
                a = acc[:, j % 2, :]
                if j % 6 < 4:
                    for c in range(4):
                        last = t.matmul(PS[:, 3, c:c + 1], a[:, c * P:(c + 1) * P], ones[:, 0:1],
                                        start=True, stop=True)
                else:
                    if j % 6 == 4:
                        pe.wait_ge(*e.at("brow", j // 6 + 1, 16))
                    t.matmul(PS[:, 3, :], ones[:], a, start=True, stop=False)
                    c = (j % 6 - 4) * 512
                    last = t.matmul(PS[:, 3, :], ones[0:1, :], brow[0:1, c:c + 512], start=False, stop=True)
                last.then_inc(*e.inc("ada_sum"))

            def turn(src, stage):
                for b in range(4):
                    for k in range(2):
                        for m in range(MT):
                            kt = 2 * b + k
                            c = (k * 2 + m) * P
                            last = t.transpose(PS[:, 4 + b, c:c + P], src[:, m, kt * P:(kt + 1) * P], ident)
                    last.then_inc(*e.inc("turned"))

            def attention(units):
                banks = range(4)
                for b in banks:
                    if used.get(b, 0) > 0:
                        pe.wait_ge(*e.at(f"bank{b}", used.get(b, 0)))

                def scores(i):
                    u = units[i]
                    if i >= 2:
                        pe.wait_ge(*e.at("logits", i - 1))
                    for j, (q, k) in enumerate(u["s"]):
                        last = t.matmul(PS[:, S_BANK[i % 2], 0:u["nk"]], q, k,
                                        start=j == 0, stop=j == len(u["s"]) - 1)
                    last.then_inc(*e.inc("scores"))

                def turn_probs(i):
                    u = units[i]
                    pe.wait_ge(*e.at("probs", i + 1))
                    if i >= 2:
                        pe.wait_ge(*e.at("pt", i - 1))
                    for c in range(u["nk"] // P):
                        last = t.transpose(PS[:, PT_BANK[i % 2], c * P:(c + 1) * P],
                                           pr[:, i % 2, c * P:(c + 1) * P], ident)
                    last.then_inc(*e.inc("probs_t"))

                def values(i):
                    u = units[i]
                    pe.wait_ge(*e.at("pt", i + 1))
                    if u["col"] == 0 and u["group"] >= 2:
                        pe.wait_ge(*e.at("o_used", u["group"] - 1))
                    nkt = u["nk"] // P
                    for c in range(nkt):
                        last = t.matmul(PS[:, O_BANK[u["group"] % 2], u["col"] * HD:(u["col"] + 1) * HD],
                                        pt[:, i % 2, c * P:(c + 1) * P], u["v"][c],
                                        start=c == 0, stop=c == nkt - 1)
                    last.then_inc(*e.inc("pv"))

                n = len(units)
                scores(0)
                for i in range(n + 1):
                    if i + 1 < n:
                        scores(i + 1)
                    if i < n:
                        turn_probs(i)
                    if i >= 1:
                        values(i - 1)

            def out_proj(n):
                pe.wait_ge(*e.at("h", 8))
                for s in range(2):
                    tok_slot(n + 2 * s, (4 + s, 6 + s), 512, first=False)

            def ffn():
                def down(s):
                    w = arrived(ffn_down(s))
                    pe.wait_ge(*e.at("act", 2 * (s + 1)))
                    for k in range(2):
                        for m in range(MT):
                            lhs = [a[:, s % 2, k, m * P:(m + 1) * P] for a in (ah, al)]
                            for c in range(2):
                                rhs = [a[:, k * D + c * 512:k * D + (c + 1) * 512] for a in w]
                                last = mm3(PS[:, 4 + 2 * m + c, :], lhs, rhs,
                                           s == 0 and k == 0, s == FFN_SLOTS - 1 and k == 1)
                    last.then_inc(*e.inc("split_used"))

                for s in range(FFN_SLOTS):
                    feat_slot(ffn_up(s), (gbank(2 * s), gbank(2 * s + 1)), (0, 2, 1, 3))
                    if s >= 1:
                        ada(s - 1)
                        down(s - 1)
                ada(FFN_SLOTS - 1)
                down(FFN_SLOTS - 1)
                ada(FFN_SLOTS)

            def gather():
                for kt in range(KT):
                    for m in range(MT):
                        last = t.matmul(PS[:, 6 + kt // 4, (kt % 4) * P:(kt % 4 + 1) * P],
                                        xn_f[:, m, kt * P:(kt + 1) * P], sel[:, m, :],
                                        start=m == 0, stop=m == MT - 1)
                    if kt % 4 == 3:
                        last.then_inc(*e.inc("gathered"))

            def combine():
                for i, b in enumerate(C_BANK):
                    m, c = divmod(i, 2)
                    t.matmul(PS[:, b, :], selt[:, m * P:(m + 1) * P], ysb[:, c * 512:(c + 1) * 512],
                             start=True, stop=True).then_inc(*e.inc("combined"))

            def expert(alone=False):
                def up(s):
                    for kh in range(2):
                        w = arrived(moe_up(s) + kh)
                        for k in range(4):
                            kt = kh * 4 + k
                            last = mm3(PS[:, s % 2, :], (hh[:, kt, 0:P], hl[:, kt, 0:P]),
                                       [a[:, k * 512:(k + 1) * 512] for a in w], kt == 0, kt == KT - 1)
                        last.then_inc(*e.inc("split_used"))

                def turn_act(s):
                    pe.wait_ge(*e.at("act_tok", s + 1))
                    if s >= 1:
                        pe.wait_ge(*e.at("act_lo", s))
                    for f in range(2):
                        last = t.transpose(PS[:, 2, f * P:(f + 1) * P], hb[:, s % 2, f * P:(f + 1) * P], ident)
                    last.then_inc(*e.inc("act_turned"))

                def down(s):
                    w = arrived(moe_down(s))
                    pe.wait_ge(*e.at("act_lo", s + 1))
                    for k in range(2):
                        for c in range(2):
                            last = mm3(PS[:, 4 + c, :], (ah[:, s % 2, k, 0:P], al[:, s % 2, k, 0:P]),
                                       [a[:, k * D + c * 512:k * D + (c + 1) * 512] for a in w],
                                       s == 0 and k == 0, s == MOE_SLOTS - 1 and k == 1)
                    last.then_inc(*e.inc("split_used"))

                if alone:
                    pe.wait_ge(*e.at("sel", 1))
                    gather()
                pe.wait_ge(*e.at("x_lo", 2 if alone else 0))
                up(0)
                if not alone:
                    pe.wait_ge(*e.at("y_sb", 2))
                    pe.wait_ge(*e.at("sel_t", 0))
                    combine()
                    pe.wait_ge(*e.at("sel", 0))
                for m in range(MT):
                    last = t.transpose(PS[:, 4, m * P:(m + 1) * P], sel[:, m, :], ident)
                last.then_inc(*e.inc("sel_turned"))
                up(1)
                if not alone:
                    pe.wait_ge(*e.at("y_used", 4))
                pe.wait_ge(*e.at("sel_t", 1))
                turn_act(0)
                for s in range(2, MOE_SLOTS):
                    up(s)
                    turn_act(s - 1)
                    down(s - 2)
                if not alone:
                    pe.wait_ge(*e.at("sel", 1))
                    gather()
                turn_act(MOE_SLOTS - 1)
                down(MOE_SLOTS - 2)
                down(MOE_SLOTS - 1)
                if alone:
                    pe.wait_ge(*e.at("y_sb", 2))
                    combine()

            def experts():
                e.enter("go")
                pe.wait_ge(*e.at("rc", 0, 16))
                pe.wait_ge(*e.at("chosen", 0))
                ch = [rw[:, 240 + m * 8:248 + m * 8] for m in range(MT)]
                t.matmul(PS[:, 3, 0:8], before, ch[0], start=True, stop=True)
                t.matmul(PS[:, 3, 8:16], ones[:], ch[0], start=True, stop=False)
                t.matmul(PS[:, 3, 8:16], before, ch[1], start=False, stop=True)
                t.matmul(PS[:, 3, 16:24], ones[:], ch[0], start=True, stop=False)
                t.matmul(PS[:, 3, 16:24], ones[:], ch[1], start=False, stop=True).then_inc(*e.inc("ranked"))
                pe.wait_ge(*e.at("sel", 1))
                gather()
                with pe.Fori(0, NEXP) as rep:
                    e.enter("moe", rep)
                    expert()
                e.enter("fin")
                pe.wait_ge(*e.at("y_sb", 2))
                pe.wait_ge(*e.at("sel_t", 0))
                combine()
                count = overfull(pe)
                with pe.Fori(0, MORE) as rep:
                    e.enter("more", rep)
                    with pe.If(count > rep):
                        expert(alone=True)

            e.enter("pre")
            pe.wait_ge(*e.at("par_in", 1, 16))
            pe.wait_ge(*e.at("consts", 2))
            for j in range(6):
                ada(j)

            with pe.Fori(0, 2) as rep:
                e.enter("lay", rep)
                used.clear()
                pe.wait_ge(*e.at("xn", 2))
                turn(xn_l, 0)
                pe.wait_ge(*e.at("h", 4))
                for s in range(8):
                    b = (gbank(2 * s), gbank(2 * s + 1))
                    if s in (0, 1, 4, 5):
                        feat_slot(2 * s, b)
                    else:
                        tok_slot(2 * s, b, 280 if s == 6 else 512)
                    if 1 <= s <= 6:
                        ada(s - 1)
                for b in range(4):
                    pe.wait_ge(*e.at(f"bank{b}", used.get(b, 0)))
                pe.wait_ge(*e.at("kk", 7))
                ck = STEPS["lay"].index(("ck",))
                rk = RAW_AT["lay"][ck]
                fills = sum(r == rk for r in RAW_AT["lay"][:ck + 1])
                pe.wait_ge(*e.at(f"raw_in{rk}", fills, 16))
                pe.wait_ge(*e.at("lp", 1))
                for v in range(2):
                    for n, (lo, rhs_n) in enumerate(((v * 32, 30), (64 + v, 1))):
                        for a in range(16):
                            c = v * 1024 + a * 64
                            if n == 0:
                                rhs = kk[:, v, :, 2 * a:2 * a + 16 * (T_CMP - 1) + 1:16]
                                out = PS[0:HD, 4 + v, 0:30].rearrange("p (g t) -> p g t", g=2)
                            else:
                                rhs = LP["pek" if v == 0 else "pev"][:, a:a + 1]
                                out = PS[0:HD, 6 + v, 0:1]
                            last = t.matmul(out, raw[:, rk, c:c + 64], rhs, start=a == 0, stop=a == 15)
                last.then_inc(*e.inc("cmp1"))
                pe.wait_ge(*e.at("cmp_act", 1))
                pe.sem_inc(settled)
                for g in range(2):
                    t.matmul(PS[g * HD:(g + 1) * HD, 4, 0:T_CMP], LP["ck2"][0:HD, :],
                             cw[0:HD, 64 + g * 15:64 + g * 15 + 15], start=True, stop=True)
                for g in range(2):
                    last = t.matmul(PS[0:T_CMP, 5, g * HD:(g + 1) * HD],
                                    cw[0:HD, 96 + g * 15:96 + g * 15 + 15], LP["cv2"][0:HD, :],
                                    start=True, stop=True)
                last.then_inc(*e.inc("cmp2"))
                pe.wait_ge(*e.at("cmp_kv", 2))
                pe.wait_ge(*e.at("lc_in", 0, 16))
                for g in range(2):
                    last = t.matmul(PS[:, 6, g * HD:(g + 1) * HD], rep_sel[0:T_CMP, g, :],
                                    cw[0:T_CMP, 160 + g * HD:160 + (g + 1) * HD], start=True, stop=True)
                last.then_inc(*e.inc("cmp3"))
                for m in range(MT):
                    for g in range(2):
                        for j in range(4):
                            last = t.matmul(PS[:, 2 * m + g, j * 16:j * 16 + T_CMP],
                                            qn[g * HD:(g + 1) * HD, j, m * P:(m + 1) * P],
                                            cw[g * HD:(g + 1) * HD, 128:128 + T_CMP], start=True, stop=True)
                    last.then_inc(*e.inc("cscores"))
                for m in range(MT):
                    pe.wait_ge(*e.at("cprobs", m + 1))
                    t.transpose(PS[:, 4 + m, 0:P], cw[:, 288 + 0:288 + P] if m == 0 else pt[:, 1, 0:P],
                                ident).then_inc(*e.inc("cprobs_t"))
                pe.wait_ge(*e.at("vb", 1))
                for m in range(MT):
                    pe.wait_ge(*e.at("cpt", m + 1))
                    t.matmul(PS[:, 6 + m, :], pt[:, 0, m * P:(m + 1) * P], vb[:], start=True,
                             stop=True).then_inc(*e.inc("cout"))
                pe.wait_ge(*e.at("cout_used", 2))
                attention(UNITS["lay"])
                pe.wait_ge(*e.at("y", 4))
                turn(y, 1)
                out_proj(16)

            e.enter("na")
            used.clear()
            pe.wait_ge(*e.at("xn", 2))
            turn(xn_n, 0)
            pe.wait_ge(*e.at("h", 4))
            for s in range(6):
                b = (gbank(2 * s), gbank(2 * s + 1))
                if s < 4:
                    feat_slot(2 * s, b)
                else:
                    tok_slot(2 * s, b, 512)
                if s >= 1:
                    ada(s - 1)
            ada(5)
            attention(UNITS["na"])
            pe.wait_ge(*e.at("o_used", 4))
            turn(nao, 1)
            out_proj(12)

            e.enter("ffn")
            used.clear()
            pe.wait_ge(*e.at("xn", 2))
            turn(xn_f, 0)
            pe.wait_ge(*e.at("h", 4))
            ffn()

            e.enter("mla")
            used.clear()
            pe.wait_ge(*e.at("xn", 2))
            turn(xn_m, 0)
            pe.wait_ge(*e.at("h", 4))
            tok_slot(0, (0, 1), 416, first=False)
            pe.wait_ge(*e.at("cn", 4))
            for k in range(4):
                for m in range(MT):
                    last = t.transpose(PS[:, 4 + k // 2, ((k % 2) * 2 + m) * P:((k % 2) * 2 + m + 1) * P],
                                       cn[:, m, k * P:(k + 1) * P], ident)
            last.then_inc(*e.inc("c_t"))
            pe.wait_ge(*e.at("c", 2))
            for half in range(2):
                w = arrived(2 + half)
                if half == 0:
                    pe.wait_ge(*e.at("down_used", 2))
                for f in range(8):
                    b = 4 * half + f // 2
                    for k in range(2):
                        lhs = [a[:, k * D + f * P:k * D + (f + 1) * P] for a in w]
                        last = mm3(PS[:, b, (f % 2) * S:(f % 2 + 1) * S], lhs, (hh[:, k, :], hl[:, k, :]),
                                   k == 0 and f % 2 == 0, k == 1)
                last.then_inc(*e.inc("split_used"))
            w = arrived(4)
            pe.wait_ge(*e.at("mq", 4))
            for f in range(8):
                lhs = [a[:, f * P:(f + 1) * P] for a in w]
                last = mm3(PS[:, f // 2, (f % 2) * S:(f % 2 + 1) * S], lhs, (hh[:, 2, :], hl[:, 2, :]),
                           f % 2 == 0, True)
            last.then_inc(*e.inc("mk_sum"))
            pe.wait_ge(*e.at("mr", 2))
            for m in range(MT):
                lhs = [a[:, 2, m * P:(m + 1) * P] for a in (hh, hl)]
                for c in range(2):
                    rhs = [a[:, D + c * 512:D + (c + 1) * 512] for a in w]
                    last = mm3(PS[:, 4 + 2 * m + c, :], lhs, rhs, True, True)
            last.then_inc(*e.inc("split_used"))
            pe.wait_ge(*e.at("mkv", 5))
            attention(UNITS["mla"])
            pe.wait_ge(*e.at("o_used", 4))
            turn(mo, 1)
            out_proj(5)

            e.enter("rt")
            used.clear()
            pe.wait_ge(*e.at("xn", 2))
            turn(xn_f, 0)
            pe.wait_ge(*e.at("h", 4))
            for m in range(MT):
                for i, a in enumerate((hh, hl)):
                    for kt in range(KT):
                        last = t.matmul(PS[:, m, 0:NEXP], a[:, kt, m * P:(m + 1) * P].bitcast(F32),
                                        pcol("router", kt * NEXP, (kt + 1) * NEXP),
                                        start=i == 0 and kt == 0, stop=i == 1 and kt == KT - 1)
                last.then_inc(*e.inc("router"))
            pe.wait_ge(*e.at("route_read", 2))

            experts()

        @block.scalar
        def _(act):
            a = nc.scalar
            e = Count(sg)
            done = [0]

            def hi_to(n):
                for i in range(done[0], min(n, SPLITS[e.phase])):
                    step = STEP_OF_SPLIT[e.phase][i]
                    r = RAW_AT[e.phase][step]
                    act.wait_ge(*e.at(f"raw_in{r}", sum(q == r for q in RAW_AT[e.phase][:step + 1]), 16))
                    if SPL_NEED[e.phase][i] is not None:
                        act.wait_ge(*e.at("split_used", SPL_NEED[e.phase][i]))
                    a.activation(wh[:, SPL_AT[e.phase][i], :], raw[:, r, :], ACT.Copy).then_inc(*e.inc("hi"))
                done[0] = max(done[0], min(n, SPLITS[e.phase]))

            def start(phase, rep=0):
                e.enter(phase, rep)
                done[0] = 0
                hi_to(SPL)

            def squares(xn):
                if e.phase == "end":
                    act.wait_ge(*e.at("x_last", MT))
                else:
                    act.wait_ge(*e.at("x", 0))
                for m in range(MT):
                    a.activation(xn[:, m, :], x[:, m, :], ACT.Square,
                                 accum_out=st[:, s_sq + m:s_sq + m + 1]).then_inc(*e.inc("sq"))

            def h_hi(stage):
                for b in range(4):
                    dst = hh[:, 2 * b:2 * b + 2, :]
                    if stage == 0:
                        act.wait_ge(*e.at("hb", b + 1))
                        src = hb[:, (2 * b) % 4:(2 * b) % 4 + 2, :]
                    else:
                        act.wait_ge(*e.at("turned", 5 + b))
                        src = PS[:, 4 + b, :].rearrange("p (k s) -> p k s", k=2)
                    a.activation(dst, src, ACT.Copy).then_inc(*e.inc("h_hi"))

            def get_brow(unit):
                act.dma_start(brow[:], dram["brow"][unit]).then_inc(*e.inc("brow", 16))

            def ada_out(j, buf):
                act.wait_ge(*e.at("ada_sum", j + 1))
                j6 = j % 6
                if j6 < 4:
                    ins = a.activation(modc[:, buf, j6 * 4:j6 * 4 + 4], PS[:, 3, 0:4], ACT.Copy)
                else:
                    ins = a.activation(gate[buf][:, (j6 - 4) * 512:(j6 - 3) * 512], PS[:, 3, :], ACT.Copy)
                ins.then_inc(*e.inc("bank3"))

            def summed(n):
                act.wait_ge(*e.at("split_used", n + 2))

            def out_feat(s, dst, scale):
                summed(2 * s)
                for i in range(2):
                    b = gbank(2 * s + i)
                    src = PS[:, b, :].rearrange("p (k s) -> p k s", k=2)
                    a.activation(dst[:, 2 * i:2 * i + 2, :], src, ACT.Copy,
                                 scale=scale).then_inc(*e.inc(f"bank{b}"))

            def out_tok(s, dst):
                summed(2 * s)
                for m in range(MT):
                    b = gbank(2 * s + m)
                    w = dst.shape[2]
                    a.activation(dst[:, m, :], PS[:, b, 0:w], ACT.Copy).then_inc(*e.inc(f"bank{b}"))

            def exps(units):
                for i, u in enumerate(units):
                    act.wait_ge(*e.at("logits", i + 1))
                    if i >= 2:
                        act.wait_ge(*e.at("probs_t", i - 1))
                    c = i % 48
                    a.activation(pr[:, i % 2, 0:u["nk"]], lg[:, i % 2, 0:u["nk"]], ACT.Exp,
                                 bias=mn(c), scale=-1.0, accum_out=sm(c)).then_inc(*e.inc("probs"))

            def ffn():
                for s in range(FFN_SLOTS):
                    n = ffn_up(s)
                    hi_to(n + 2 + SPL)
                    summed(n)
                    for f in range(2):
                        q = 2 * s + f
                        if q >= 4:
                            act.wait_ge(*e.at("act", q - 3))
                        a.activation(hb[:, q % 4, :], PS[:, gbank(q), 0:S], ACT.Tanh,
                                     scale=0.5).then_inc(*e.inc("tanh"))
                    for f in range(2):
                        q = 2 * s + f
                        act.wait_ge(*e.at(f"bank{gbank(q)}", uses_to(q)))
                        if s >= 2:
                            act.wait_ge(*e.at("split_used", ffn_down(s - 2) + 1))
                        a.activation(ah[:, s % 2, f, :], hb[:, q % 4, :], ACT.Copy).then_inc(*e.inc("act_hi"))
                    if s >= 1:
                        if s == 7:
                            get_brow(5)
                        ada_out(s - 1, 1 if s - 1 < 6 else 2)
                        hi_to(ffn_down(s - 1) + 1 + SPL)
                hi_to(SPLITS["ffn"])
                ada_out(FFN_SLOTS - 1, 2)
                ada_out(FFN_SLOTS, 2)

            def x_hi():
                for i in range(2):
                    act.wait_ge(*e.at("x_f", i + 1))
                    a.activation(hh[:, 4 * i:4 * i + 4, 0:P], xg[:, 4 * i:4 * i + 4, :],
                                 ACT.Copy).then_inc(*e.inc("x_hi"))

            def keep_rows():
                act.wait_ge(*e.at("split_used", SPLITS["more"] if e.phase == "more" else 0))
                for c in range(2):
                    a.activation(ysb[:, c * 512:(c + 1) * 512], PS[:, 4 + c, :],
                                 ACT.Copy).then_inc(*e.inc("y_sb"))

            def expert(alone=False):
                def act_hi(s):
                    act.wait_ge(*e.at("act_turned", s + 1))
                    a.activation(ah[:, s % 2, :, 0:P], PS[:, 2, 0:S].rearrange("p (k s) -> p k s", k=2),
                                 ACT.Copy).then_inc(*e.inc("act_hi"))

                hi_to(2)
                if alone:
                    x_hi()
                else:
                    keep_rows()
                for s in range(MOE_SLOTS):
                    n = moe_up(s)
                    hi_to(n + 1 + SPL)
                    summed(n)
                    a.activation(hb[:, s % 2, :], PS[:, s % 2, 0:S], ACT.Tanh, scale=0.5).then_inc(*e.inc("tanh"))
                    if s == 0:
                        act.wait_ge(*e.at("sel_turned", 1))
                        a.activation(selt[:], PS[:, 4, 0:S], ACT.Copy).then_inc(*e.inc("sel_t"))
                    hi_to(n + 2 + SPL)
                    if s >= 1:
                        act_hi(s - 1)
                act_hi(MOE_SLOTS - 1)
                if alone:
                    keep_rows()
                else:
                    x_hi()

            def experts():
                e.enter("go")
                x_hi()
                with act.Fori(0, NEXP) as rep:
                    e.enter("moe", rep)
                    done[0] = 0
                    expert()
                e.enter("fin")
                keep_rows()
                act.wait_ge(*e.at("over", 0))
                count = overfull(act)
                with act.Fori(0, MORE) as rep:
                    e.enter("more", rep)
                    done[0] = 0
                    with act.If(count > rep):
                        expert(alone=True)

            e.enter("pre")
            get_brow(0)
            act.wait_ge(*e.at("par_in", 1, 16))
            act.wait_ge(*e.at("consts", 2))
            c2 = pcol("cc").rearrange("p (c k) -> p c k", c=2)
            a.activation(cs[:], c2, ACT.Tanh, scale=0.5).then_inc(*e.inc("cs_tanh"))
            for j in range(6):
                ada_out(j, 1)

            with act.Fori(0, 2) as rep:
                start("lay", rep)
                act.wait_ge(*e.at("x_in", 0, 16))
                squares(xn_l)
                act.wait_ge(*e.at("y", 0))
                act.dma_start(gpost[:], dram["gpost"][rep]).then_inc(*e.inc("gpost", 16))
                act.dma_start(brow[:], dram["brow"][rep + 1]).then_inc(*e.inc("brow", 16))
                h_hi(0)
                for s in range(8):
                    hi_to(2 * s + 2 + SPL)
                    if s == 0:
                        out_feat(s, qm, -QS)
                    if s == 1:
                        out_feat(s, km, 1.0)
                    if s == 2:
                        out_tok(s, vm)
                    if s in (3, 7):
                        if s == 7:
                            act.wait_ge(*e.at("gg", 1))
                        z = zm if s == 3 else zn
                        summed(2 * s)
                        for m in range(MT):
                            a.activation(z[:, m, :], PS[:, gbank(2 * s + m), :], ACT.Tanh,
                                         scale=0.5).then_inc(*e.inc("z_tanh"))
                    if s == 4:
                        out_feat(s, qn, -QS)
                    if s == 5:
                        summed(2 * s)
                        b = gbank(2 * s + 1)
                        a.activation(ksw[:], PS[:, b, :].rearrange("p (k s) -> p k s", k=2),
                                     ACT.Copy).then_inc(*e.inc(f"bank{b}"))
                    if s == 6:
                        out_tok(s, vsw)
                    if 1 <= s <= 6:
                        ada_out(s - 1, 1)
                gl = vsw[:, :, 256:280]
                for b in range(3):
                    act.wait_ge(*e.at(f"bank{b}", sum(gbank(q) == b for q in range(16))))
                a.activation(gl, gl, ACT.Tanh, scale=0.5).then_inc(*e.inc("g_tanh"))
                act.wait_ge(*e.at("cmp_u", 1))
                a.activation(cw[0:HD, 64:128], cw[0:HD, 0:64], ACT.Tanh,
                             scale=0.7978845608028654).then_inc(*e.inc("cmp_tanh"))
                act.wait_ge(*e.at("cmp2", 1))
                a.activation(cw[:, 128:128 + T_CMP], PS[:, 4, 0:T_CMP], ACT.Copy,
                             scale=0.5).then_inc(*e.inc("cmp_kv"))
                a.activation(cw[0:T_CMP, 160:288], PS[0:T_CMP, 5, 0:P], ACT.Copy,
                             scale=0.5).then_inc(*e.inc("cmp_kv"))
                for m in range(MT):
                    act.wait_ge(*e.at("clogits", m + 1))
                    dst = (cw[:, 288:416] if m == 0 else pt[:, 1, 0:P]).rearrange("p (h t) -> p h t", h=8)
                    src = hb[:, m, 0:P].rearrange("p (h t) -> p h t", h=8)
                    a.activation(dst[:, :, 0:T_CMP], src[:, :, 0:T_CMP], ACT.Exp,
                                 scale=-1.0).then_inc(*e.inc("cexp"))
                exps(UNITS["lay"])
                h_hi(1)
                hi_to(20)
                act.wait_ge(*e.at("split_used", 20))
                for i in range(4):
                    a.activation(xn_l[:, i // 2, (i % 2) * 512:(i % 2 + 1) * 512], PS[:, 4 + i, :], ACT.Square,
                                 accum_out=st[:, 240 + i:241 + i]).then_inc(*e.inc("ysq"))

            start("na")
            squares(xn_n)
            act.dma_start(rp[:], dram["rp"]).then_inc(*e.inc("rp_in", 16))
            get_brow(3)
            h_hi(0)
            for s in range(6):
                hi_to(2 * s + 2 + SPL)
                if s < 2:
                    out_feat(s, naq[:, 4 * s:4 * s + 4, :], -QS)
                elif s < 4:
                    out_feat(s, nak[:, 4 * (s - 2):4 * (s - 2) + 4, :], 1.0)
                else:
                    out_tok(s, nav[:, :, (s - 4) * 512:(s - 3) * 512])
                if s >= 1:
                    ada_out(s - 1, 0)
            ada_out(5, 0)
            exps(UNITS["na"])
            h_hi(1)
            hi_to(16)

            start("ffn")
            squares(xn_f)
            get_brow(4)
            h_hi(0)
            ffn()

            start("mla")
            squares(xn_m)
            h_hi(0)
            summed(0)
            for m in range(MT):
                a.activation(dsb[:, m, :], PS[:, m, 0:416], ACT.Copy).then_inc(*e.inc("down_used"))
            act.wait_ge(*e.at("down_used", 2))
            for m in range(MT):
                for i, (c0, c1) in enumerate(((0, 256), (256, 384))):
                    a.activation(cn[:, m, c0:c1], dsb[:, m, c0:c1], ACT.Square,
                                 accum_out=st[:,
                                              s_sq + 2 + 2 * i + m:s_sq + 3 + 2 * i + m]).then_inc(*e.inc("sq"))
            act.wait_ge(*e.at("c_f", 1))
            a.activation(hh[:, 0:3, :], hb[:, 0:3, :], ACT.Copy).then_inc(*e.inc("c_hi"))
            hi_to(5)
            act.wait_ge(*e.at("split_used", 3))
            for i in range(4):
                src = PS[:, i, :].rearrange("p (k s) -> p k s", k=2)
                a.activation(mq[:, 2 * i:2 * i + 2, :], src, ACT.Copy, scale=-MS).then_inc(*e.inc("mq"))
            act.wait_ge(*e.at("mk_sum", 1))
            for i in range(4):
                src = PS[:, i, :].rearrange("p (k s) -> p k s", k=2)
                a.activation(mk[:, 2 * i:2 * i + 2, :], src, ACT.Copy).then_inc(*e.inc("mkv"))
            hi_to(8)
            exps(UNITS["mla"])
            h_hi(1)
            hi_to(9)

            e.enter("rt")
            squares(xn_f)
            act.dma_start(fnorm[:], dram["fnorm"]).then_inc(*e.inc("fnorm", 16))
            act.dma_start(rc[:], dram["rc"]).then_inc(*e.inc("rc", 16))
            h_hi(0)
            for m in range(MT):
                act.wait_ge(*e.at("rmax", m + 1))
                a.activation(rw[:, m * 8:m * 8 + 8], rw[:, m * 8:m * 8 + 8], ACT.Exp,
                             bias=rw[:, 16 + m:17 + m], accum_out=rw[:, 18 + m:19 + m]).then_inc(*e.inc("rexp"))

            experts()

            e.enter("end")
            squares(xn_f)

        @block.vector
        def _(dve):
            v = nc.vector
            e = Count(sg)
            done = [0]

            def link(ins):
                name = "dve" if e.phase != "end" else "dve_end"
                ins.then_inc(*e.inc(name))
                dve.wait_ge(*e.last(name))

            def raw_to(n):
                ph = e.phase
                for i in range(done[0], min(n, len(STEPS[ph]))):
                    step, r = STEPS[ph][i], RAW_AT[ph][i]
                    if step[0] == "w":
                        s = SPL_AT[ph][step[1]]
                        dve.wait_ge(*e.at("hi", step[1] + 1))
                        v.tensor_tensor(wl[:, s, :], raw[:, r, :], wh[:, s, :].bitcast(F32),
                                        ALU.subtract).then_inc(*e.inc("raw_used"))
                        dve.wait_ge(*e.last("raw_used"))
                    elif step[0] == "ada":
                        _, j, kh = step
                        dve.wait_ge(*e.at(f"raw_in{r}", sum(q == r for q in RAW_AT[ph][:i + 1]), 16))
                        dst = acc[:, j % 2, :]
                        if kh == 0:
                            if j >= 2:
                                dve.wait_ge(*e.at("ada_sum", j - 1))
                        c = cs[:, 1, :] if ph == "ffn" or ph == "na" else csc[:]
                        for k in range(4):
                            kt = kh * 4 + k
                            w = raw[:, r, k * 512:(k + 1) * 512]
                            if kt == 0:
                                ins = v.tensor_scalar(dst, w, c[:, kt:kt + 1], None, ALU.mult)
                            else:
                                ins = v.scalar_tensor_tensor(out=dst, in0=w, scalar=c[:, kt:kt + 1], in1=dst,
                                                             op0=ALU.mult, op1=ALU.add)
                            if k < 3:
                                link(ins)
                            else:
                                ins.then_inc(*e.inc("raw_used"))
                                dve.wait_ge(*e.last("raw_used"))
                    else:
                        return i
                    done[0] = i + 1

            def split_to(n):
                ph = e.phase
                n = min(n, SPLITS[ph])
                raw_to(STEP_OF_SPLIT[ph][n - 1] + 1)

            def start(phase, rep=0):
                e.enter(phase, rep)
                done[0] = 0

            def norm(xn, wa, wb):
                dve.wait_ge(*e.at("rstd", 1))
                for m in range(MT):
                    v.tensor_scalar(xn[:, m, :], x[:, m, :], st[:, s_rs + m:s_rs + m + 1], None,
                                    ALU.mult).then_inc(*e.inc("xn"))
                    dve.wait_ge(*e.last("xn"))

                def lo(b):
                    dve.wait_ge(*e.at("h_hi", b + 1))
                    v.tensor_tensor(hl[:, 2 * b:2 * b + 2, :], hb[:, (2 * b) % 4:(2 * b) % 4 + 2, :],
                                    hh[:, 2 * b:2 * b + 2, :].bitcast(F32), ALU.subtract).then_inc(*e.inc("h"))
                    dve.wait_ge(*e.last("h"))

                for b in range(4):
                    dve.wait_ge(*e.at("turned", b + 1))
                    for k in range(2):
                        kt = 2 * b + k
                        ins = v.tensor_scalar(hb[:, kt % 4, :], PS[:, 4 + b, k * S:(k + 1) * S],
                                              wa[:, kt:kt + 1], wb[:, kt:kt + 1], ALU.mult, ALU.add)
                        if k == 0:
                            link(ins)
                        else:
                            ins.then_inc(*e.inc("hb"))
                            dve.wait_ge(*e.last("hb"))
                    if b >= 1:
                        lo(b - 1)
                lo(3)

            def make_ab(buf, bcol, gpre=None):
                dve.wait_ge(*e.at("bank3", 0))
                link(v.tensor_tensor(modc[:, buf, :], modc[:, buf, :], bcol, ALU.add))
                if gpre is not None:
                    link(v.scalar_tensor_tensor(out=ab[:, 0, :], in0=modc[:, buf, 8:16], scalar=1.0, in1=gpre,
                                                op0=ALU.add, op1=ALU.mult))
                else:
                    link(v.tensor_scalar(ab[:, 0, :], modc[:, buf, 8:16], 1.0, None, ALU.add))
                link(v.tensor_copy(ab[:, 1, :], modc[:, buf, 0:8]))

            def h_lo_psum():
                for b in range(4):
                    dve.wait_ge(*e.at("h_hi", 5 + b))
                    v.tensor_tensor(hl[:, 2 * b:2 * b + 2, :],
                                    PS[:, 4 + b, :].rearrange("p (k s) -> p k s", k=2),
                                    hh[:, 2 * b:2 * b + 2, :].bitcast(F32), ALU.subtract).then_inc(*e.inc("h"))
                    dve.wait_ge(*e.last("h"))

            def attention(units, finish):
                def logits(i):
                    u = units[i]
                    dve.wait_ge(*e.at("scores", i + 1))
                    if i >= 2:
                        dve.wait_ge(*e.at("probs", i - 1))
                    n = u["nk"]
                    dve.sem_inc(settled)
                    v.tensor_tensor_reduce(lg[:, i % 2, 0:n], u["bias"], PS[:, S_BANK[i % 2], 0:n],
                                           1.0, 3e38, ALU.add, ALU.min, mn(i % 48)).then_inc(*e.inc("logits"))
                    dve.wait_ge(*e.last("logits"))

                def copy_pt(i):
                    n = units[i]["nk"]
                    dve.wait_ge(*e.at("probs_t", i + 1))
                    if i >= 2:
                        dve.wait_ge(*e.at("pv", i - 1))
                    v.tensor_copy(pt[:, i % 2, 0:n], PS[:, PT_BANK[i % 2], 0:n]).then_inc(*e.inc("pt"))
                    dve.wait_ge(*e.last("pt"))

                n = len(units)
                logits(0)
                for i in range(n):
                    if i + 1 < n:
                        logits(i + 1)
                    copy_pt(i)
                    if i % 8 == 2 and i > 8:
                        out_group(i // 8 - 1, units, finish)
                out_group(n // 8 - 1, units, finish)

            def out_group(g, units, finish):
                dve.wait_ge(*e.at("probs", 8 * g + 8))
                c = (8 * g) % 48
                link(v.reciprocal(rinv(0, 8), st[:, 96 + c:104 + c]))
                dve.wait_ge(*e.at("pv", 8 * g + 8))
                o = PS[:, O_BANK[g % 2], :].rearrange("p (h d) -> p h d", h=8)
                finish(units[8 * g], o, rinv(0, 8))

            def bc(w):
                return w.unsqueeze(2).broadcast_to([P, 8, HD])

            def update_x(g, n_wait):
                dve.wait_ge(*e.at("split_used", n_wait))
                for m in range(MT):
                    tmp = hb[:].rearrange("p a b -> p (a b)")
                    src = PS[:, 4 + 2 * m:6 + 2 * m, :].rearrange("p a b -> p (a b)")
                    link(v.tensor_tensor(tmp, src, g[:], ALU.mult))
                    v.tensor_tensor(x[:, m, :], x[:, m, :], tmp, ALU.add).then_inc(*e.inc("x"))
                    dve.wait_ge(*e.last("x"))

            def ffn():
                for s in range(FFN_SLOTS):
                    n = ffn_up(s)
                    split_to(n + 2 + SPL)
                    dve.wait_ge(*e.at("split_used", n + 2))
                    for f in range(2):
                        q = 2 * s + f
                        b = gbank(q)
                        t_ = hb[:, q % 4, :]
                        dve.wait_ge(*e.at("tanh", q + 1))
                        link(v.scalar_tensor_tensor(out=t_, in0=t_, scalar=1.0, in1=PS[:, b, 0:S],
                                                    op0=ALU.add, op1=ALU.mult))
                        v.scalar_tensor_tensor(out=t_, in0=t_, scalar=0.5, in1=PS[:, b, S:2 * S],
                                               op0=ALU.mult, op1=ALU.mult).then_inc(*e.inc(f"bank{b}"))
                        dve.wait_ge(*e.at(f"bank{b}", uses_to(q)))
                    for f in range(2):
                        q = 2 * s + f
                        dve.wait_ge(*e.at("act_hi", q + 1))
                        v.tensor_tensor(al[:, s % 2, f, :], hb[:, q % 4, :],
                                        ah[:, s % 2, f, :].bitcast(F32), ALU.subtract).then_inc(*e.inc("act"))
                        dve.wait_ge(*e.last("act"))
                    if s >= 1:
                        split_to(ffn_down(s - 1) + 1 + SPL)
                raw_to(999)

            def x_f():
                for i in range(2):
                    dve.wait_ge(*e.at("gathered", i + 1))
                    for k in range(4):
                        kt = 4 * i + k
                        ins = v.tensor_scalar(xg[:, kt, :], PS[:, 6 + i, k * P:(k + 1) * P],
                                              ab[:, 0, kt:kt + 1], ab[:, 1, kt:kt + 1], ALU.mult, ALU.add)
                        if k < 3:
                            link(ins)
                    ins.then_inc(*e.inc("x_f"))
                    dve.wait_ge(*e.last("x_f"))

            def x_lo():
                for i in range(2):
                    dve.wait_ge(*e.at("x_hi", i + 1))
                    v.tensor_tensor(hl[:, 4 * i:4 * i + 4, 0:P], xg[:, 4 * i:4 * i + 4, :],
                                    hh[:, 4 * i:4 * i + 4, 0:P].bitcast(F32),
                                    ALU.subtract).then_inc(*e.inc("x_lo"))
                    dve.wait_ge(*e.last("x_lo"))

            def select(column, rnd):
                for m in range(MT):
                    ins = v.tensor_scalar(sel[:, m, :], row_no[:, rnd * P:(rnd + 1) * P],
                                          pos_of[:, m, column], None, ALU.is_equal)
                    if m == 0:
                        link(ins)
                ins.then_inc(*e.inc("sel"))
                dve.wait_ge(*e.last("sel"))

            def add_rows(column):
                for i, b in enumerate(C_BANK):
                    m, c = divmod(i, 2)
                    dve.wait_ge(*e.at("combined", i + 1))
                    part = ysum[:, m, c * 512:(c + 1) * 512]
                    v.scalar_tensor_tensor(out=part, in0=PS[:, b, :], scalar=wcol[:, m, column], in1=part,
                                           op0=ALU.mult, op1=ALU.add).then_inc(*e.inc("y_used"))
                    dve.wait_ge(*e.last("y_used"))

            def expert(own, other, alone=False):
                def act_lo(s):
                    dve.wait_ge(*e.at("act_hi", s + 1))
                    v.tensor_tensor(al[:, s % 2, :, 0:P], PS[:, 2, 0:S].rearrange("p (k s) -> p k s", k=2),
                                    ah[:, s % 2, :, 0:P].bitcast(F32), ALU.subtract).then_inc(*e.inc("act_lo"))
                    dve.wait_ge(*e.last("act_lo"))

                if alone:
                    select(other, 1)
                    split_to(2)
                    x_f()
                    x_lo()
                for s in range(MOE_SLOTS):
                    n = moe_up(s)
                    split_to(n + 1 + SPL)
                    dve.wait_ge(*e.at("tanh", s + 1))
                    t_ = hb[:, s % 2, :]
                    link(v.scalar_tensor_tensor(out=t_, in0=t_, scalar=1.0, in1=PS[:, s % 2, 0:S],
                                                op0=ALU.add, op1=ALU.mult))
                    v.scalar_tensor_tensor(out=t_, in0=t_, scalar=0.5, in1=PS[:, s % 2, S:2 * S],
                                           op0=ALU.mult, op1=ALU.mult).then_inc(*e.inc("act_tok"))
                    dve.wait_ge(*e.last("act_tok"))
                    if s == 0 and not alone:
                        add_rows(own)
                    split_to(n + 2 + SPL)
                    if s >= 1:
                        act_lo(s - 1)
                    if s == 2 and not alone:
                        dve.wait_ge(*e.at("sel_turned", 1))
                        select(other, 0)
                if alone:
                    act_lo(MOE_SLOTS - 1)
                    add_rows(own)
                else:
                    x_f()
                    act_lo(MOE_SLOTS - 1)
                    x_lo()

            def experts():
                e.enter("go")
                dve.wait_ge(*e.at("ranked", 1))
                for m in range(MT):
                    link(v.scalar_tensor_tensor(out=pos_of[:, m, 0:NEXP], in0=PS[:, 3, m * 8:m * 8 + 8],
                                                scalar=1.0, in1=rw[:, 240 + m * 8:248 + m * 8],
                                                op0=ALU.add, op1=ALU.mult))
                    link(v.tensor_scalar(pos_of[:, m, 0:NEXP], pos_of[:, m, 0:NEXP], -1.0, None, ALU.add))
                full, ahead, pairs, hit = rw[:, 256:264], rw[:, 264:272], rw[:, 64:128], rw[:, 272:280]
                found = rw[:, 280:281 + MORE]
                link(v.tensor_scalar(full, PS[:, 3, 16:24], P + 0.5, None, ALU.is_gt))
                link(v.tensor_tensor(pairs.rearrange("p (a b) -> p a b", a=8),
                                     pcol("lower").rearrange("p (a b) -> p a b", a=8),
                                     full.unsqueeze(1).broadcast_to([P, 8, 8]), ALU.mult))
                link(v.tensor_reduce(ahead, pairs.rearrange("p (a b) -> p a b", a=8), AX_X, ALU.add))
                link(v.tensor_reduce(found[:, 0:1], full, AX_X, ALU.add))
                for i in range(MORE):
                    link(v.scalar_tensor_tensor(out=hit, in0=ahead, scalar=float(i), in1=full,
                                                op0=ALU.is_equal, op1=ALU.mult))
                    link(v.tensor_tensor(hit, hit, row_no[:, 0:NEXP], ALU.mult))
                    link(v.tensor_reduce(found[:, i + 1:i + 2], hit, AX_X, ALU.add))
                v.tensor_copy(over[:], found).then_inc(*e.inc("over"))
                dve.wait_ge(*e.last("over"))
                v.memset(selt[:], 0.0).then_inc(*e.inc("sel_t"))
                dve.wait_ge(*e.last("sel_t"))
                select(slice(0, 1), 0)
                x_f()
                x_lo()
                with dve.Fori(0, NEXP) as rep:
                    start("moe", rep)
                    expert(bass.ds(rep, 1), bass.ds(rep + 1, 1))
                e.enter("fin")
                add_rows(slice(NEXP, NEXP + 1))
                count = overfull(dve)
                with dve.Fori(0, MORE) as rep:
                    start("more", rep)
                    with dve.If(count > rep):
                        which = dve.value_load(over[0:1, bass.ds(rep + 1, 1)], min_val=0, max_val=NEXP - 1)
                        expert(bass.ds(which + 1, 1), bass.ds(which, 1), alone=True)
                        dve.sem_inc(settled)

            e.enter("pre")
            c2 = pcol("cc").rearrange("p (c k) -> p c k", c=2)
            dve.wait_ge(*e.at("cs_tanh", 1))
            dve.wait_ge(*e.at("consts", 2))
            link(v.scalar_tensor_tensor(out=cs[:], in0=cs[:], scalar=1.0, in1=c2, op0=ALU.add, op1=ALU.mult))
            link(v.tensor_scalar(cs[:], cs[:], 0.5, None, ALU.mult))
            link(v.tensor_copy(csc[:], cs[:, 0, :]))
            raw_to(99)

            with dve.Fori(0, 2) as rep:
                start("lay", rep)
                dve.wait_ge(*e.at("par_in", 0, 16))
                dve.wait_ge(*e.at("x_in", 0, 16))
                link(v.tensor_copy(csc[:], cs[:, bass.ds(rep, 1), :].rearrange("p a b -> p (a b)")))
                v.tensor_copy(lpc[:],
                              lpall[:, bass.ds(rep, 1), :].rearrange("p a b -> p (a b)")).then_inc(*e.inc("lp"))
                dve.wait_ge(*e.last("lp"))
                make_ab(1, LP["bcol"], LP["gpre"])
                split_to(2)
                norm(xn_l, ab[:, 0, :], ab[:, 1, :])
                dve.wait_ge(*e.at("gpost", 1, 16))
                v.tensor_tensor(gate[0][:], gate[1][:], gpost[:], ALU.mult).then_inc(*e.inc("gg"))
                dve.wait_ge(*e.last("gg"))
                for s in range(8):
                    if s < 6:
                        split_to(2 * s + 2 + SPL)
                    if s in (3, 7):
                        z = zm if s == 3 else zn
                        for m in range(MT):
                            b = gbank(2 * s + m)
                            dve.wait_ge(*e.at("z_tanh", (2 if s == 7 else 0) + m + 1))
                            v.scalar_tensor_tensor(out=z[:, m, :], in0=z[:, m, :], scalar=1.0,
                                                   in1=PS[:, b,
                                                          :], op0=ALU.add, op1=ALU.mult).then_inc(*e.inc(f"bank{b}"))
                            dve.wait_ge(*e.at(f"bank{b}", uses_to(2 * s + m)))
                    if s == 5:
                        dve.wait_ge(*e.at("split_used", 12))
                        b = gbank(10)
                        for w in range(2):
                            for g in range(2):
                                src = PS[g * HD:(g + 1) * HD, b, w * S:(w + 1) * S]
                                v.tensor_copy(kk[0:HD, w, g, :], src).then_inc(*e.inc("kk"))
                                dve.wait_ge(*e.last("kk"))
                                ins = v.tensor_copy(kk[HD:P, w, g, 0:S - 1], src[:, 1:S])
                                if (w, g) == (1, 1):
                                    ins.then_inc(*e.inc(f"bank{b}"))
                                    dve.wait_ge(*e.at(f"bank{b}", uses_to(10)))
                                else:
                                    ins.then_inc(*e.inc("kk"))
                                    dve.wait_ge(*e.last("kk"))
                    if s == 5:
                        split_to(16)
                raw_to(999)
                dve.wait_ge(*e.at("g_tanh", 1))
                gl = vsw[:, :, 256:280]
                link(v.tensor_scalar(gl, gl, 0.5, 0.5, ALU.mult, ALU.add))
                dve.wait_ge(*e.at("cmp1", 1))
                xc, u_ = cw[0:HD, 0:64], cw[0:HD, 416:480]
                link(v.memset(cw[0:HD, 0:128], 0.0))
                bias = st[0:HD, 232:234]
                link(v.tensor_copy(bias, PS[0:HD, 6:8, 0:1].rearrange("p a b -> p (a b)")))
                for w in range(2):
                    link(v.tensor_scalar(xc[:, w * 32:w * 32 + 30], PS[0:HD, 4 + w, 0:30], bias[:, w:w + 1], None,
                                         ALU.add))
                link(v.tensor_tensor(u_, xc, xc, ALU.mult))
                link(v.tensor_scalar(u_, u_, 0.044715, 1.0, ALU.mult, ALU.add))
                link(v.tensor_copy(hb[0:HD, 0, 0:64], xc))
                v.tensor_tensor(xc, u_, xc, ALU.mult).then_inc(*e.inc("cmp_u"))
                dve.wait_ge(*e.last("cmp_u"))
                dve.wait_ge(*e.at("cmp_tanh", 1))
                v.scalar_tensor_tensor(out=cw[0:HD, 64:128], in0=cw[0:HD, 64:128], scalar=1.0,
                                       in1=hb[0:HD, 0,
                                              0:64], op0=ALU.add, op1=ALU.mult).then_inc(*e.inc("cmp_act"))
                dve.wait_ge(*e.last("cmp_act"))
                dve.wait_ge(*e.at("cmp_act", 1))
                v.memset(st[:, 236:237], 0.0).then_inc(*e.inc("raw_used"))
                dve.wait_ge(*e.last("raw_used"))
                done[0] = STEPS["lay"].index(("ck",)) + 1
                split_to(19)
                dve.wait_ge(*e.at("cmp3", 1))
                dve.wait_ge(*e.at("lc_in", 0, 16))
                link(v.memset(cw[:, 288:416], 0.0))
                link(v.memset(pt[:, 1, 0:P], 0.0))
                for g in range(2):
                    ins = v.tensor_tensor(
                        vb[:].rearrange("p (h d) -> p h d", h=8)[:, 4 * g:4 * g + 4, :],
                        PS[:, 6, g * HD:(g + 1) * HD].unsqueeze(1).broadcast_to([P, 4, HD]),
                        mask8[:, 4 * g:4 * g + 4].unsqueeze(2).broadcast_to([P, 4, HD]), ALU.mult)
                    if g == 0:
                        link(ins)
                ins.then_inc(*e.inc("vb"))
                dve.wait_ge(*e.last("vb"))
                for m in range(MT):
                    dve.wait_ge(*e.at("cscores", m + 1))
                    l8 = hb[:, m, 0:P].rearrange("p (h t) -> p h t", h=8)[:, :, 0:T_CMP]
                    for g in range(2):
                        link(v.tensor_tensor(l8[:, 4 * g:4 * g + 4, :],
                                             PS[:, 2 * m + g, 0:64].rearrange("p (j t) -> p j t", j=4)[:, :, 0:T_CMP],
                                             alibi_c[:, m, 4 * g:4 * g + 4, 0:T_CMP], ALU.add))
                    link(v.tensor_reduce(rinv(0, 8), l8, AX_X, ALU.min))
                    v.tensor_tensor(l8, l8, rinv(0, 8).unsqueeze(2).broadcast_to([P, 8, T_CMP]),
                                    ALU.subtract).then_inc(*e.inc("clogits"))
                    dve.wait_ge(*e.last("clogits"))
                for m in range(MT):
                    dve.wait_ge(*e.at("cexp", m + 1))
                    ex = (cw[:, 288:416] if m == 0 else pt[:, 1, 0:P]).rearrange("p (h t) -> p h t", h=8)[:, :, 0:T_CMP]
                    link(v.tensor_reduce(st[:, 240 + 8 * m:248 + 8 * m], ex, AX_X, ALU.add))
                    v.tensor_tensor(ex, ex, ok_c[:, m, 0:T_CMP].unsqueeze(1).broadcast_to([P, 8, T_CMP]),
                                    ALU.mult).then_inc(*e.inc("cprobs"))
                    dve.wait_ge(*e.last("cprobs"))
                for m in range(MT):
                    dve.wait_ge(*e.at("cprobs_t", m + 1))
                    v.tensor_copy(pt[:, 0, m * P:(m + 1) * P], PS[:, 4 + m, 0:P]).then_inc(*e.inc("cpt"))
                    dve.wait_ge(*e.last("cpt"))

                def gate_of(m, c):
                    return vsw[:, m, 256:280].rearrange("p (h c) -> p h c", c=3)[:, :, c:c + 1].rearrange("p h c -> p (h c)")

                for m in range(MT):
                    link(v.reciprocal(rinv(0, 8), st[:, 240 + 8 * m:248 + 8 * m]))
                    link(v.tensor_tensor(wgt(), rinv(0, 8), gate_of(m, 0), ALU.mult))
                    dve.wait_ge(*e.at("cout", m + 1))
                    v.tensor_tensor(y[:, m, 512:1024].rearrange("p (h d) -> p h d", h=8),
                                    PS[:, 6 + m, :].rearrange("p (h d) -> p h d", h=8), bc(wgt()),
                                    ALU.mult).then_inc(*e.inc("cout_used"))
                    dve.wait_ge(*e.last("cout_used"))

                def finish(u, o, ri):
                    m = u["m"]
                    t3 = tmpo[:].rearrange("p (h d) -> p h d", h=8)
                    if u["branch"] == "moba":
                        v.scalar_tensor_tensor(out=t3, in0=o, scalar=0.5, in1=bc(ri), op0=ALU.mult,
                                               op1=ALU.mult).then_inc(*e.inc("o_used"))
                        dve.wait_ge(*e.last("o_used"))
                        v.tensor_tensor(y[:, m, 0:512], tmpo[:], zm[:, m, :], ALU.mult).then_inc(*e.inc("y"))
                        dve.wait_ge(*e.last("y"))
                        return
                    c = 1 if u["branch"] == "sel" else 2
                    link(v.tensor_tensor(wgt(), ri, gate_of(m, c), ALU.mult))
                    v.tensor_tensor(t3, o, bc(wgt()), ALU.mult).then_inc(*e.inc("o_used"))
                    dve.wait_ge(*e.last("o_used"))
                    link(v.tensor_tensor(y[:, m, 512:1024], y[:, m, 512:1024], tmpo[:], ALU.add))
                    if c == 2:
                        v.scalar_tensor_tensor(out=y[:, m, 512:1024], in0=y[:, m, 512:1024], scalar=0.5,
                                               in1=zn[:, m,
                                                      :], op0=ALU.mult, op1=ALU.mult).then_inc(*e.inc("y"))
                        dve.wait_ge(*e.last("y"))

                attention(UNITS["lay"], finish)
                h_lo_psum()
                raw_to(999)
                dve.wait_ge(*e.at("ysq", 4))
                link(v.tensor_tensor(st[:, s_sq + 2:s_sq + 3], st[:, 240:241], st[:, 241:242], ALU.add))
                v.tensor_tensor(st[:, s_sq + 3:s_sq + 4], st[:, 242:243], st[:, 243:244],
                                ALU.add).then_inc(*e.inc("sq"))
                dve.wait_ge(*e.at("sq", 3))
                dve.wait_ge(*e.at("rstd", 2))
                for m in range(MT):
                    tmp = hb[:].rearrange("p a b -> p (a b)")
                    src = PS[:, 4 + 2 * m:6 + 2 * m, :].rearrange("p a b -> p (a b)")
                    link(v.scalar_tensor_tensor(out=tmp, in0=src, scalar=st[:, s_rs + 2 + m:s_rs + 3 + m],
                                                in1=gate[0][:], op0=ALU.mult, op1=ALU.mult))
                    v.tensor_tensor(x[:, m, :], x[:, m, :], tmp, ALU.add).then_inc(*e.inc("x"))
                    dve.wait_ge(*e.last("x"))

            start("na")
            make_ab(1, pcol("bcol", 0, 16))
            split_to(2)
            norm(xn_n, ab[:, 0, :], ab[:, 1, :])
            for s in range(6):
                split_to(min(2 * s + 2 + SPL, 15))
            dve.wait_ge(*e.at("rp_in", 1, 16))
            link(v.tensor_tensor(rp[:], pcol("namask").unsqueeze(1).broadcast_to([P, 96, 64]), rp[:], ALU.subtract))

            def finish_plain(dst):
                def finish(u, o, ri):
                    m, b = u["m"], u["branch"]
                    v.tensor_tensor(dst[:, m, b * 512:(b + 1) * 512].rearrange("p (h d) -> p h d", h=8),
                                    o, bc(ri), ALU.mult).then_inc(*e.inc("o_used"))
                    dve.wait_ge(*e.last("o_used"))
                return finish

            attention(UNITS["na"], finish_plain(nao))
            h_lo_psum()
            raw_to(999)
            update_x(gate[1], 16)

            start("ffn")
            make_ab(0, pcol("bcol", 16, 32))
            split_to(2)
            norm(xn_f, ab[:, 0, :], ab[:, 1, :])
            ffn()
            update_x(gate[0], SPLITS["ffn"])

            start("mla")
            make_ab(1, pcol("bcol", 32, 48))
            split_to(3)
            norm(xn_m, ab[:, 0, :], ab[:, 1, :])
            dve.wait_ge(*e.at("rstd", 2))
            dve.wait_ge(*e.at("down_used", 2))
            kt4 = hb[:, 3, 0:128]
            for m in range(MT):
                v.tensor_scalar(cn[:, m, 0:256], dsb[:, m, 0:256], st[:, s_rs + 2 + m:s_rs + 3 + m], None,
                                ALU.mult).then_inc(*e.inc("cn"))
                dve.wait_ge(*e.last("cn"))
                link(v.tensor_scalar(cn[:, m, 256:384], dsb[:, m, 256:384], st[:, s_rs + 4 + m:s_rs + 5 + m], None,
                                     ALU.mult))
                x1, x2 = dsb[:, m, 384:400], dsb[:, m, 400:416]
                cc, ss = pcol("kcos", m * 16, m * 16 + 16), pcol("ksin", m * 16, m * 16 + 16)
                q = [kt4[:, i * 16:(i + 1) * 16] for i in range(4)]
                for dst, p0, p1 in ((q[0], x1, cc), (q[1], x2, ss), (q[2], x1, ss), (q[3], x2, cc)):
                    link(v.tensor_tensor(dst, p0, p1, ALU.mult))
                k0 = cn[:, m, 384:512].rearrange("p (r i) -> p r i", r=4)
                link(v.tensor_tensor(k0[:, :, 0:16], q[0].unsqueeze(1).broadcast_to([P, 4, 16]),
                                     q[1].unsqueeze(1).broadcast_to([P, 4, 16]), ALU.subtract))
                v.tensor_tensor(k0[:, :, 16:32], q[2].unsqueeze(1).broadcast_to([P, 4, 16]),
                                q[3].unsqueeze(1).broadcast_to([P, 4, 16]), ALU.add).then_inc(*e.inc("cn"))
                dve.wait_ge(*e.last("cn"))
            dve.wait_ge(*e.at("c_t", 1))
            for k in range(3):
                ins = v.tensor_scalar(hb[:, k, :], PS[:, 4 + k // 2, (k % 2) * S:(k % 2 + 1) * S],
                                      pcol("lnorm", k, k + 1), None, ALU.mult)
                if k < 2:
                    link(ins)
            ins.then_inc(*e.inc("c_f"))
            dve.wait_ge(*e.last("c_f"))
            v.tensor_copy(kr[:], PS[:, 5, S:2 * S]).then_inc(*e.inc("c"))
            dve.wait_ge(*e.last("c"))
            dve.wait_ge(*e.at("c_hi", 1))
            v.tensor_tensor(hl[:, 0:3, :], hb[:, 0:3, :], hh[:, 0:3, :].bitcast(F32),
                            ALU.subtract).then_inc(*e.inc("c"))
            dve.wait_ge(*e.last("c"))
            split_to(5)
            dve.wait_ge(*e.at("split_used", 4))
            tab = lambda n: pcol(n).unsqueeze(1).broadcast_to([P, 4, S])
            link(v.tensor_tensor(mt2[:], PS[:, 6:8, :].rearrange("p a b -> p (a b)").rearrange("p (k s) -> p k s", s=S),
                                 tab("qsin"), ALU.mult))
            v.tensor_tensor(mr[:], PS[:, 4:6, :].rearrange("p a b -> p (a b)").rearrange("p (k s) -> p k s", s=S),
                            tab("qcos"), ALU.mult).then_inc(*e.inc("mr"))
            dve.wait_ge(*e.last("mr"))
            v.tensor_tensor(mr[:], mr[:], mt2[:], ALU.add).then_inc(*e.inc("mr"))
            dve.wait_ge(*e.last("mr"))
            dve.wait_ge(*e.at("split_used", 5))
            v.tensor_copy(mv[:].rearrange("p m d -> p (m d)"),
                          PS[:, 4:8, :].rearrange("p a b -> p (a b)")).then_inc(*e.inc("mkv"))
            split_to(8)
            attention(UNITS["mla"], finish_plain(mo))
            h_lo_psum()
            raw_to(999)
            update_x(gate[1], 9)

            e.enter("rt")
            make_ab(2, pcol("bcol", 48, 64))
            norm(xn_f, ab[:, 0, :], ab[:, 1, :])
            for m in range(MT):
                r8 = rw[:, m * 8:m * 8 + 8]
                dve.wait_ge(*e.at("router", m + 1))
                v.tensor_copy(r8, PS[:, m, 0:NEXP]).then_inc(*e.inc("route_read"))
                dve.wait_ge(*e.last("route_read"))
                link(v.tensor_reduce(rw[:, 16 + m:17 + m], r8, AX_X, ALU.max))
                v.tensor_scalar(rw[:, 16 + m:17 + m], rw[:, 16 + m:17 + m], -1.0, None,
                                ALU.mult).then_inc(*e.inc("rmax"))
                dve.wait_ge(*e.last("rmax"))
            for m in range(MT):
                r8 = rw[:, m * 8:m * 8 + 8]
                dve.wait_ge(*e.at("rexp", m + 1))
                link(v.reciprocal(rw[:, 20:21], rw[:, 18 + m:19 + m]))
                link(v.tensor_scalar(r8, r8, rw[:, 20:21], None, ALU.mult))
                other = r8.unsqueeze(1).broadcast_to([P, 8, 8])
                own = r8.unsqueeze(2).broadcast_to([P, 8, 8])
                gt = rw[:, 64:128].rearrange("p (a b) -> p a b", a=8)
                eq = rw[:, 128:192].rearrange("p (a b) -> p a b", a=8)
                link(v.tensor_tensor(gt, other, own, ALU.is_gt))
                link(v.tensor_tensor(eq, other, own, ALU.is_equal))
                link(v.tensor_tensor(rw[:, 128:192], rw[:, 128:192], pcol("lower"), ALU.mult))
                link(v.tensor_tensor(rw[:, 64:128], rw[:, 64:128], rw[:, 128:192], ALU.add))
                link(v.tensor_reduce(rw[:, 24:32], gt, AX_X, ALU.add))
                chosen = rw[:, 240 + m * 8:248 + m * 8]
                link(v.tensor_scalar(chosen, rw[:, 24:32], 1.5, None, ALU.is_lt))
                link(v.tensor_tensor(r8, r8, chosen, ALU.mult))
                link(v.tensor_reduce(rw[:, 21:22], r8, AX_X, ALU.add))
                link(v.reciprocal(rw[:, 22:23], rw[:, 21:22]))
                link(v.tensor_scalar(wcol[:, m, 1:NEXP + 1], r8, rw[:, 22:23], None, ALU.mult))
                link(v.memset(wcol[:, m, 0:1], 0.0))
                v.memset(pos_of[:, m, NEXP:NEXP + 1], -1.0).then_inc(*e.inc("chosen"))
                dve.wait_ge(*e.last("chosen"))
            link(v.memset(ysum[:], 0.0))

            experts()

            e.enter("end")
            dve.wait_ge(*e.at("bank3", 0))
            for m in range(MT):
                tmp = hb[:].rearrange("p a b -> p (a b)")
                link(v.tensor_tensor(tmp, ysum[:, m, :], gate[2][:], ALU.mult))
                v.tensor_tensor(x[:, m, :], x[:, m, :], tmp, ALU.add).then_inc(*e.inc("x_last"))
                dve.wait_ge(*e.last("x_last"))
            dve.wait_ge(*e.at("rstd", 1))
            dve.wait_ge(*e.at("fnorm", 0, 16))
            for m in range(MT):
                v.scalar_tensor_tensor(out=xn_f[:, m, :], in0=x[:, m, :],
                                       scalar=st[:, s_rs + m:s_rs + m + 1], in1=fnorm[:],
                                       op0=ALU.mult, op1=ALU.mult).then_inc(*e.inc("final"))
                dve.wait_ge(*e.last("final"))
    return sg


def tables():
    f = np.float32
    p = np.arange(P)
    slopes = (2.0 ** (-8.0 * np.arange(1, 9) / 8)).astype(f)
    c = {}
    c["ident"] = np.eye(P, dtype=f)
    c["zeros"] = np.zeros((P, S), f)
    al = np.zeros((P, 8, 384), f)
    for m in range(MT):
        n = (m + 1) * P
        d = (m * P + p)[:, None] - np.arange(n)[None, :]
        b = slopes[None, :, None] * d[:, None, :]
        al[:, :, m * P:m * P + n] = np.where(d[:, None, :] >= 0, b, FAR)
    c["alibi"] = al.reshape(P, -1)
    ac = np.zeros((P, MT, 8, 16), f)
    ok = np.zeros((P, MT, 16), f)
    for m in range(MT):
        d = (m * P + p)[:, None] - (np.arange(16) * 16 + 31)[None, :]
        ac[:, m] = np.where(d[:, None, :] >= 0, slopes[None, :, None] * d[:, None, :], FAR)
        ok[:, m] = d >= 0
    c["alibi_c"] = ac.reshape(P, -1)
    c["ok_c"] = ok.reshape(P, -1)
    rs = np.zeros((P, 2, P), f)
    for g in range(2):
        for h in range(4 * g, 4 * g + 4):
            for t in range(T_CMP):
                rs[t, g, h * 16 + t] = 1.0
    c["rep_sel"] = rs.reshape(P, -1)
    c["mask8"] = (p[:, None] // 16 == np.arange(8)[None, :]).astype(f)
    col = p % 64
    first = np.clip(col - 8, 0, 48)[:, None]
    kc = np.arange(64)[None, :]
    c["namask"] = np.where((kc >= first) & (kc < first + 16), 0.0, FAR).astype(f)
    t = np.arange(S)
    inv = (10000.0 ** (-np.arange(8, dtype=f) / 8)).astype(f)
    ang = np.concatenate([(t // 64).astype(f)[:, None] * inv, (t % 64).astype(f)[:, None] * inv], axis=1)
    cos, sin = np.cos(ang).astype(f), np.sin(ang).astype(f)
    c["kcos"] = cos.reshape(MT, P, 16).transpose(1, 0, 2).reshape(P, 32)
    c["ksin"] = sin.reshape(MT, P, 16).transpose(1, 0, 2).reshape(P, 32)
    i = p % 32
    c["qcos"] = (-MS * cos[:, i % 16].T).astype(f)
    c["qsin"] = (np.where(i < 16, MS, -MS)[:, None] * sin[:, i % 16].T).astype(f)
    c["lower"] = np.broadcast_to(np.tril(np.ones((8, 8), f), -1).reshape(1, 64), (P, 64))
    return c


def kernel(**inputs):
    import concourse.bacc as bacc
    from concourse.bass_utils import run_bass_kernel_spmd

    a = {k: np.asarray(v) for k, v in inputs.items()}
    f = np.float32

    def cols(vec):
        return np.ascontiguousarray(vec.reshape(-1, P).T)

    def ktiles(w):
        n = w.shape[0] // P
        return w.reshape(n, P, -1).transpose(1, 0, 2).reshape(P, -1)

    ws = np.zeros((NSTEPS, P, STEP), f)
    pos = [0]

    def put(block):
        ws[pos[0], :, :block.shape[1]] = block
        pos[0] += 1

    def halves(w):
        return [ktiles(w[:512]), ktiles(w[512:])]

    def emit(phase, splits, ada, ck=None):
        for step in STEPS[phase]:
            if step[0] == "w":
                put(splits[step[1]])
            elif step[0] == "ada":
                u, j = divmod(step[1], 6)
                put(halves(ada[u][:, j * 512:(j + 1) * 512])[step[2]])
            else:
                put(ck)

    units = [a["w_ada"][0], a["w_ada"][1]]
    bias = [a["b_ada"][0], a["b_ada"][1]]
    for l in range(2):
        for h in range(2):
            units.append(a["w_ada_2"][l][:, h * 3072:(h + 1) * 3072])
            bias.append(a["b_ada_2"][l][h * 3072:(h + 1) * 3072])

    def mlp_blocks(gu, down, slots, lag):
        n = slots * 256
        ups = [np.concatenate([gu[:, s * 256:(s + 1) * 256], gu[:, n + s * 256:n + (s + 1) * 256]], axis=1)
               for s in range(slots)]
        out = list(halves(ups[0]))
        for s in range(1, slots):
            out += halves(ups[s])
            if s >= lag:
                out.append(ktiles(down[(s - lag) * 256:(s - lag + 1) * 256]))
        return out + [ktiles(down[s * 256:(s + 1) * 256]) for s in range(slots - lag, slots)]

    emit("pre", [], [units[0]])
    nsa = np.concatenate([np.arange(h * HD, (h + 1) * HD) for j in range(4) for h in (j, 4 + j)])
    for l in range(2):
        w = a["w_in"][l]
        q, kvo = w[:, 2048:2560][:, nsa], 2560
        part = lambda i: w[:, kvo + i * P:kvo + (i + 1) * P]
        slots = [w[:, 0:512], w[:, 512:1024], w[:, 1024:1536], w[:, 1536:2048], q,
                 np.concatenate([part(0), part(1), part(2), part(4)], axis=1),
                 np.concatenate([part(3), part(5), w[:, 3328:3352]], axis=1), w[:, 3352:3864],
                 a["w_out"][l][:, 0:512], a["w_out"][l][:, 512:1024]]
        ck = np.concatenate([ktiles(a["w_ck1"][l]), ktiles(a["w_cv1"][l])], axis=1)
        emit("lay", [b for s in slots for b in halves(s)], [units[l + 1]], ck)
    w, wo = a["na_w_qkv_2"][0], a["na_w_o_2"][0]
    slots = [w[:, s * 512:(s + 1) * 512] for s in range(6)] + [wo[:, 0:512], wo[:, 512:1024]]
    emit("na", [b for s in slots for b in halves(s)], [units[3]])
    emit("ffn", mlp_blocks(a["ffn_w_gu_2"][0], a["ffn_w_down_2"][0], FFN_SLOTS, 1), [units[4], units[5]])
    uq = a["mla_w_uq_2"][0].reshape(256, 16, 96)
    nope, r1, r2 = uq[:, :, :64], uq[:, :, 64::2], uq[:, :, 65::2]
    ukv = a["mla_w_ukv_2"][0].reshape(P, 16, 2, 64)
    down = a["mla_w_down_2"][0]
    down = np.concatenate([down[:, :384], down[:, 384::2], down[:, 385::2]], axis=1)
    wo = a["mla_w_o_2"][0]
    emit("mla", halves(down) + [
        ktiles(nope.reshape(256, 1024)),
        ktiles(np.concatenate([np.concatenate([r1, r2], axis=2).reshape(256, 512),
                               np.concatenate([r2, r1], axis=2).reshape(256, 512)], axis=1)),
        np.concatenate([ukv[:, :, 0].reshape(P, 1024), ukv[:, :, 1].reshape(P, 1024)], axis=1),
    ] + halves(wo[:, 0:512]) + halves(wo[:, 512:1024]), [])
    for x in range(NEXP):
        emit("moe", mlp_blocks(a["moe_w_gu_2"][0, x], a["moe_w_down_2"][0, x], MOE_SLOTS, 2), [])
    assert pos[0] == NSTEPS

    c = tables()

    def rows64(w):
        out = np.zeros((P, w.shape[1]), f)
        out[:HD] = w
        return out

    lp = np.stack([np.concatenate([
        cols(a["g_pre"][l]), cols(bias[l][:2048]), ktiles(a["pe_k"][l].reshape(-1, 1)),
        ktiles(a["pe_v"][l].reshape(-1, 1)), rows64(a["w_ck2"][l]), rows64(a["w_cv2"][l])], axis=1)
        for l in range(2)], axis=1)
    c["lpall"] = lp.reshape(P, -1)
    c["bcol"] = np.concatenate([cols(bias[u][:2048]) for u in range(2, 6)], axis=1)
    c["cc"] = np.concatenate([cols(a["c"][0]), cols(a["c_2"][0])], axis=1)
    c["lnorm"] = np.concatenate([cols(a["mla_q_norm_2"][0]), cols(a["mla_kv_norm_2"][0])], axis=1)
    c["router"] = ktiles(a["moe_w_router_2"][0])
    par_names = ["ident", "zeros", "namask", "kcos", "ksin", "qcos", "qsin", "lower", "lpall", "bcol", "cc",
                 "lnorm", "router"]
    lc_names = ["alibi", "alibi_c", "ok_c", "rep_sel", "mask8"]
    dc = np.clip(np.arange(64)[None, :] - (np.arange(P) % 64)[:, None] + 15, 0, 30)
    dr = np.arange(6)[None, :] + 5 - (np.arange(P) // 64)[:, None]
    rp = a["na_rpb_2"][0][:, dr[:, :, None], dc[:, None, :]].transpose(1, 0, 2, 3).reshape(P, 96, 64)
    arrays = {
        "ws": ws,
        "x": a["x"][0].reshape(MT, P, D).transpose(1, 0, 2),
        "par": np.concatenate([c[n] for n in par_names], axis=1),
        "lc": np.concatenate([c[n] for n in lc_names], axis=1),
        "rp": rp,
        "brow": np.stack([b[2048:] for b in bias])[:, None, :],
        "gpost": np.ascontiguousarray(np.broadcast_to(a["g_post"][:, None, :], (2, P, D))),
        "rc": np.concatenate([np.broadcast_to(np.arange(S, dtype=f), (P, S)),
                              (np.arange(P)[:, None] < np.arange(P)[None, :]).astype(f)], axis=1),
        "fnorm": np.ascontiguousarray(np.broadcast_to(a["final_norm_2"][None, :], (P, D))),
    }
    arrays = {k: np.ascontiguousarray(v, dtype=f) for k, v in arrays.items()}

    nc = bacc.Bacc("TRN2", target_bir_lowering=False, num_devices=1)
    dram = {k: nc.dram_tensor(f"in_{k}", v.shape, F32, kind="ExternalInput").ap() for k, v in arrays.items()}
    dram["out"] = nc.dram_tensor("out_0", (P, MT, D), F32, kind="ExternalOutput").ap()
    dram["par_cols"] = [(n, c[n].shape[1]) for n in par_names]
    dram["lc_cols"] = [(n, c[n].shape[1]) for n in lc_names]
    build(nc, dram)
    r = run_bass_kernel_spmd(nc, [{f"in_{k}": v for k, v in arrays.items()}], core_ids=[0])
    return r.results[0]["out_0"].transpose(1, 0, 2).reshape(1, S, D)
```

```python
from contextlib import ExitStack

import numpy as np
import concourse.bass as bass
from concourse import mybir

F32 = mybir.dt.float32
F32R = mybir.dt.float32r
ALU = mybir.AluOpType
ACT = mybir.ActivationFunctionType
AX_X = mybir.AxisListType.X

P = 128
D = 1024
S = 256
MT = S // P
KT = D // P
HD = 64
STEP = 2048
RAW = 6
SPL = 3
EPS = 1e-6
FAR = 1e12
QS = HD ** -0.5
MS = 96 ** -0.5
NEXP = 8
FFN_SLOTS = 11
MOE_SLOTS = 7
T_CMP = 15

PHASES = ["pre", "lay", "na", "ffn", "mla", "rt", "go", "moe", "fin", "more", "end"]
MORE = 2 * S // (P + 1)
REPS = {"lay": 2, "moe": NEXP, "more": MORE}


def ada_steps(j):
    return [("ada", j, 0), ("ada", j, 1)]


def layer_steps():
    out, n = [], 0
    for s in range(8):
        out += [("w", n), ("w", n + 1)]
        n += 2
        if s < 6:
            out += ada_steps(s)
    return out + [("w", n), ("w", n + 1), ("w", n + 2), ("ck",), ("w", n + 3)]


def na_steps():
    out = []
    for s in range(6):
        out += [("w", 2 * s), ("w", 2 * s + 1)] + ada_steps(s)
    return out + [("w", 12 + i) for i in range(4)]


def ffn_steps():
    out, n = [], 0
    for s in range(FFN_SLOTS):
        out += [("w", n), ("w", n + 1)] + ada_steps(s)
        n += 2
        if s >= 1:
            out.append(("w", n))
            n += 1
    return out + ada_steps(FFN_SLOTS) + [("w", n)]


STEPS = {
    "pre": [x for j in range(6) for x in ada_steps(j)],
    "lay": layer_steps(),
    "na": na_steps(),
    "ffn": ffn_steps(),
    "mla": [("w", i) for i in range(9)],
    "moe": [("w", i) for i in range(3 * MOE_SLOTS)],
    "more": [("w", i) for i in range(3 * MOE_SLOTS)],
}
STEPS = {p: STEPS.get(p, []) for p in PHASES}
SPLITS = {p: sum(x[0] == "w" for x in STEPS[p]) for p in PHASES}
NSTEPS = sum(len(STEPS[p]) * REPS.get(p, 1) for p in PHASES if p != "more")


def ffn_up(s):
    return 0 if s == 0 else 3 * s - 1


def ffn_down(s):
    return 3 * s + 4 if s < FFN_SLOTS - 1 else 3 * FFN_SLOTS - 1


def moe_up(s):
    return 2 * s if s < 2 else 3 * s - 2


def moe_down(s):
    return min(3 * s + 6, 2 * MOE_SLOTS + s)


def ring_plan(size, lengths):
    place, need, start = {}, {}, 0
    owner = [None] * size
    total = 0
    for p in PHASES:
        n, reps = lengths[p], REPS.get(p, 1)
        pad = -n % size if reps > 1 else 0
        place[p] = [(start + i) % size for i in range(n)]
        need[p] = [None] * n
        for _ in range(reps):
            for i in range(n):
                last = owner[place[p][i]]
                if last is not None:
                    k = last + 1 - total
                    need[p][i] = k if need[p][i] is None else max(need[p][i], k)
                owner[place[p][i]] = total + i
            total += n
        start = (start + n + pad) % size
    return place, need


RAW_AT, RAW_NEED = ring_plan(RAW, {p: len(STEPS[p]) for p in PHASES})
SPL_AT, SPL_NEED = ring_plan(SPL, SPLITS)
STEP_OF_SPLIT = {p: [i for i, x in enumerate(STEPS[p]) if x[0] == "w"] for p in PHASES}

COUNTS = {
    "act": {"ffn": 22},
    "act_hi": {"ffn": 22, "moe": 7, "more": 7},
    "act_lo": {"moe": 7, "more": 7},
    "act_tok": {"moe": 7, "more": 7},
    "act_turned": {"moe": 7, "more": 7},
    "ada_sum": {"pre": 6, "lay": 6, "na": 6, "ffn": 12},
    "bank0": {"lay": 6, "na": 4, "ffn": 8},
    "bank1": {"lay": 5, "na": 4, "ffn": 7},
    "bank2": {"lay": 5, "na": 4, "ffn": 7},
    "bank3": {"pre": 6, "lay": 6, "na": 6, "ffn": 12},
    "brow": {"pre": 1, "lay": 1, "na": 1, "ffn": 2},
    "c": {"mla": 2},
    "c_f": {"mla": 1},
    "c_hi": {"mla": 1},
    "c_t": {"mla": 1},
    "cexp": {"lay": 1},
    "chosen": {"rt": 1},
    "clogits": {"lay": 1},
    "cmp1": {"lay": 1},
    "cmp2": {"lay": 1},
    "cmp_act": {"lay": 1},
    "cmp_kv": {"lay": 2},
    "cmp_tanh": {"lay": 1},
    "cmp_u": {"lay": 1},
    "cn": {"mla": 4},
    "combined": {"moe": 4, "fin": 4, "more": 4},
    "consts": {"pre": 2},
    "cout": {"lay": 2},
    "cout_used": {"lay": 2},
    "cprobs": {"lay": 2},
    "cprobs_t": {"lay": 1},
    "cpt": {"lay": 1},
    "cs_tanh": {"pre": 1},
    "cscores": {"lay": 2},
    "down_used": {"mla": 2},
    "dve": {"pre": 39, "lay": 85, "na": 52, "ffn": 105, "mla": 30, "rt": 24, "go": 24, "moe": 14, "more": 14},
    "dve_end": {"end": 2},
    "final": {"end": 2},
    "fnorm": {"rt": 1},
    "g_tanh": {"lay": 1},
    "gathered": {"go": 2, "moe": 2, "more": 2},
    "gg": {"lay": 1},
    "gpost": {"lay": 1},
    "h": {"lay": 8, "na": 8, "ffn": 4, "mla": 8, "rt": 4},
    "h_hi": {"lay": 8, "na": 8, "ffn": 4, "mla": 8, "rt": 4},
    "hb": {"lay": 2, "na": 2, "ffn": 2, "mla": 2, "rt": 2},
    "hb_act": {"lay": 4, "na": 4, "ffn": 4, "mla": 4, "rt": 4},
    "hi": {"lay": 20, "na": 16, "ffn": 33, "mla": 9, "moe": 21, "more": 21},
    "kk": {"lay": 1},
    "lc_in": {"pre": 1},
    "logits": {"lay": 48, "na": 32, "mla": 32},
    "lp": {"lay": 1},
    "mc": {"mla": 1},
    "mean_sq": {"lay": 2, "na": 1, "ffn": 1, "mla": 3, "rt": 1, "end": 1},
    "mk_sum": {"mla": 1},
    "mkv": {"mla": 5},
    "mq": {"mla": 4},
    "mr": {"mla": 2},
    "o_used": {"lay": 6, "na": 4, "mla": 4},
    "over": {"go": 1},
    "par_in": {"pre": 1},
    "probs": {"lay": 48, "na": 32, "mla": 32},
    "probs_t": {"lay": 48, "na": 32, "mla": 32},
    "pt": {"lay": 48, "na": 32, "mla": 32},
    "pv": {"lay": 48, "na": 32, "mla": 32},
    "ranked": {"go": 1},
    "raw_in0": {"pre": 2, "lay": 6, "na": 5, "ffn": 10, "mla": 1, "moe": 4, "more": 4},
    "raw_in1": {"pre": 2, "lay": 6, "na": 5, "ffn": 9, "mla": 2, "moe": 3, "more": 3},
    "raw_in2": {"pre": 2, "lay": 6, "na": 5, "ffn": 9, "mla": 2, "moe": 3, "more": 3},
    "raw_in3": {"pre": 2, "lay": 5, "na": 5, "ffn": 9, "mla": 2, "moe": 3, "more": 3},
    "raw_in4": {"pre": 2, "lay": 5, "na": 4, "ffn": 10, "mla": 1, "moe": 4, "more": 4},
    "raw_in5": {"pre": 2, "lay": 5, "na": 4, "ffn": 10, "mla": 1, "moe": 4, "more": 4},
    "raw_used": {"pre": 12, "lay": 33, "na": 28, "ffn": 57, "mla": 9, "moe": 21, "more": 21},
    "rc": {"rt": 1},
    "rexp": {"rt": 1},
    "rmax": {"rt": 1},
    "router": {"rt": 1},
    "router_hi": {"rt": 1},
    "router_lo": {"rt": 1},
    "router_sb": {"rt": 1},
    "router_t": {"rt": 1},
    "rp_in": {"na": 1},
    "rstd": {"lay": 2, "na": 1, "ffn": 1, "mla": 2, "rt": 1, "end": 1},
    "scores": {"lay": 48, "na": 32, "mla": 32},
    "sel": {"go": 1, "moe": 1, "more": 1},
    "sel_t": {"go": 1, "moe": 1, "more": 1},
    "sel_turned": {"moe": 1, "more": 1},
    "split_used": {"pre": 3, "lay": 20, "na": 16, "ffn": 33, "mla": 9, "moe": 21, "more": 21},
    "sq": {"lay": 3, "na": 2, "ffn": 2, "mla": 6, "rt": 2, "end": 2},
    "stored": {"end": 2},
    "tanh": {"ffn": 22, "moe": 7, "more": 7},
    "turned": {"lay": 8, "na": 8, "ffn": 4, "mla": 8, "rt": 4},
    "vb": {"lay": 1},
    "x": {"pre": 2, "lay": 2, "na": 2, "ffn": 2, "mla": 2},
    "x_f": {"go": 2, "moe": 2, "more": 2},
    "x_hi": {"go": 2, "moe": 2, "more": 2},
    "x_in": {"pre": 1},
    "x_last": {"end": 2},
    "x_lo": {"go": 2, "moe": 2, "more": 2},
    "xn": {"lay": 2, "na": 2, "ffn": 2, "mla": 2, "rt": 2},
    "y": {"pre": 1, "lay": 4},
    "y_sb": {"moe": 2, "fin": 2, "more": 2},
    "y_used": {"moe": 4, "fin": 4, "more": 4},
    "ysq": {"lay": 4},
    "z_tanh": {"lay": 4},
}


class Signals:

    def __init__(self, nc, ctx):
        self.nc, self.ctx, self.sems, self.made = nc, ctx, {}, {}

    def sem(self, name):
        if name not in self.sems:
            self.sems[name] = self.ctx.enter_context(self.nc.semaphore(name))
        return self.sems[name]

    def value(self, name, phase, rep, k):
        c = COUNTS.get(name, {})
        base = 0
        for p in PHASES:
            if p == phase:
                break
            base += c.get(p, 0) * REPS.get(p, 1)
        per = c.get(phase, 0)
        return base + k + (rep * per if per and not isinstance(rep, int) else 0)


class Count:

    def __init__(self, signals):
        self.sg = signals
        self.phase, self.rep = "pre", 0
        self.own = {}

    def enter(self, phase, rep=0):
        self.phase, self.rep, self.own = phase, rep, {}

    def at(self, name, k, unit=1):
        v = self.sg.value(name, self.phase, self.rep, k)
        assert not isinstance(v, int) or v > 0, (name, self.phase, k, v)
        return self.sg.sem(name), v * unit

    def inc(self, name, unit=1):
        d = self.sg.made.setdefault(name, {})
        d[self.phase] = d.get(self.phase, 0) + 1
        self.own[name] = self.own.get(name, 0) + 1
        return self.sg.sem(name), unit

    def last(self, name):
        return self.at(name, self.own[name])


def build(nc, dram):
    ctx = ExitStack()
    with ctx:
        at = [nc.sbuf_base + (-nc.sbuf_base) % 64]

        def sb(name, shape, dt=F32, offset=None):
            size = int(np.prod(shape[1:])) * 4
            size += -size % 32
            if offset is None:
                offset = at[0]
                at[0] += size
            return nc.alloc_sbuf_tensor_at(name, shape, dt, offset=offset)

        raw = sb("raw", [P, RAW, STEP])
        wh = sb("w_hi", [P, SPL, STEP], F32R)
        wl = sb("w_lo", [P, SPL, STEP], F32R)
        hh = sb("h_hi", [P, KT, S], F32R)
        hl = sb("h_lo", [P, KT, S], F32R)
        x = sb("x", [P, MT, D])
        gate = [sb("gate0", [P, D]), sb("gate1", [P, D])]
        acc = sb("acc", [P, 2, 512])
        brow = sb("brow", [1, D])
        par = sb("par", [P, dram["par"].shape[1]])
        cs = sb("cs", [P, 2, KT])
        csc = sb("cs_cur", [P, KT])
        modc = sb("modc", [P, 3, 16])
        ab = sb("ab", [P, 2, KT])
        st = sb("st", [P, 256])
        ones = sb("ones", [P, P])
        spare = sb("spare", [P, 8])
        work = at[0]
        hb = sb("hb", [P, 4, S])
        sb("hb_rest", [P, 2, S])
        pt = sb("pt", [P, 2, S])
        lg = sb("lg", [P, 3, S], offset=work)
        pr = sb("pr", [P, 3, S], offset=work + 3 * S * 4)
        gate2_at = at[0]
        gate.append(sb("gate2", [P, D]))
        arena = at[0]
        top = nc.sbuf_top

        def region(start):
            pos = [start]

            def take(name, shape, dt=F32):
                off = pos[0]
                size = int(np.prod(shape[1:])) * 4
                pos[0] += size + (-size % 32)
                assert pos[0] <= top, (name, pos[0] - top)
                return nc.alloc_sbuf_tensor_at(name, shape, dt, offset=off)
            return take, pos

        scaled_y = nc.alloc_sbuf_tensor_at("scaled_y", [P, MT, D], F32, offset=work)

        take, pos = region(gate2_at)
        lc = take("lc", [P, dram["lc"].shape[1]])
        y_at = pos[0]
        y = take("y", [P, MT, D])
        qm = take("qm", [P, 4, S])
        km = take("km", [P, 4, S])
        vm = take("vm", [P, MT, 512])
        zm = take("zm", [P, MT, 512])
        qn = take("qn", [P, 4, S])
        ksw = take("ksw", [P, 2, S])
        vsw = take("vsw", [P, MT, 280])
        zn_at = pos[0]
        zn = take("zn", [P, MT, 512])
        lpc = take("lpc", [P, 184])
        cw = take("cw", [P, 512])
        ce = take("ce", [P, MT, P])
        kk_at = pos[0]
        kk = take("kk", [P, 8, P])
        xn_l = nc.alloc_sbuf_tensor_at("xn_l", [P, MT, D], F32, offset=y_at)
        gpost = nc.alloc_sbuf_tensor_at("gpost", [P, D], F32, offset=zn_at)
        vb = nc.alloc_sbuf_tensor_at("vb", [P, 512], F32, offset=kk_at)
        tmpo = nc.alloc_sbuf_tensor_at("tmpo", [P, 512], F32, offset=kk_at + 2048)
        take, pos = region(gate2_at)
        rp = take("rp", [P, 16 * 6, 64])
        naq = take("naq", [P, 8, S])
        nak = take("nak", [P, 8, S])
        nav = take("nav", [P, MT, D])
        o_at = pos[0]
        nao = take("nao", [P, MT, D])
        xn_n = nc.alloc_sbuf_tensor_at("xn_n", [P, MT, D], F32, offset=o_at)
        take, pos = region(arena)
        ysum = take("ysum", [P, MT, D])
        xn_f = take("xn_f", [P, MT, D])
        ah = take("a_hi", [P, 2, 2, S], F32R)
        al = take("a_lo", [P, 2, 2, S], F32R)
        fnorm = take("fnorm", [P, D])
        rw = take("rw", [P, 320])
        wrh = take("router_hi", [P, KT * NEXP], F32R)
        wrl = take("router_lo", [P, KT * NEXP], F32R)
        ysb = take("ysb", [P, D])
        xg = take("xg", [P, KT, P])
        sel = take("sel", [P, MT, P])
        selt = take("sel_t", [P, S])
        rc = take("rc", [P, dram["rc"].shape[1]])
        row_no, before = rc[:, 0:S], rc[:, S:S + P]
        wcol = take("wcol", [P, MT, NEXP + 1])
        pos_of = take("pos_of", [P, MT, NEXP + 1])
        over = nc.alloc_sbuf_tensor_at("over", [P, 1 + MORE], mybir.dt.int32, offset=pos[0])
        take, pos = region(arena)
        dsb = take("dsb", [P, MT, 416])
        cn = take("cn", [P, MT, 512])
        mq = take("mq", [P, 8, S])
        mr = take("mr", [P, 4, S])
        mt2 = take("mt2", [P, 4, S])
        kr = take("kr", [P, S])
        mk = take("mk", [P, 8, S])
        mv = take("mv", [P, MT, D])
        mo = take("mo", [P, MT, D])
        mc = take("mc", [P, 3 * S])
        xn_m = nc.alloc_sbuf_tensor_at("xn_m", [P, MT, D], F32, offset=arena)

        PS = ctx.enter_context(nc.psum_tensor("PS", [P, 8, 512], F32))

        pc = {}
        o = 0
        for name, n in dram["par_cols"]:
            pc[name] = (o, n)
            o += n

        def pcol(name, a=0, b=None):
            s0, n = pc[name]
            return par[:, s0 + a:s0 + (n if b is None else b)]

        lcc = {}
        o = 0
        for name, n in dram["lc_cols"]:
            lcc[name] = (o, n)
            o += n

        def lcol(name):
            s0, n = lcc[name]
            return lc[:, s0:s0 + n]

        ident = pcol("ident")
        alibi = lcol("alibi").rearrange("p (h k) -> p h k", h=8)
        alibi_c = lcol("alibi_c").rearrange("p (m h t) -> p m h t", m=2, h=8)
        ok_c = lcol("ok_c").rearrange("p (m t) -> p m t", m=2)
        rep_sel = lcol("rep_sel").rearrange("p (g q) -> p g q", g=2)
        mask8 = lcol("mask8")
        LP = {}
        o = 0
        for name, n in (("gpre", 8), ("bcol", 16), ("pek", 16), ("pev", 16), ("ck2", 64), ("cv2", 64)):
            LP[name] = lpc[:, o:o + n]
            o += n
        lpall = pcol("lpall").rearrange("p (l n) -> p l n", l=2)

        SQ = slice(0, 8)
        s_sq, s_ms, s_rs, s_half = 0, 8, 16, 24
        mn = lambda u: st[:, 32 + u:33 + u]
        sm = lambda u: st[:, 96 + u:97 + u]
        rinv = lambda a, b: st[:, 160 + a:160 + b]
        wgt = lambda: st[:, 224:232]

        sg = Signals(nc, ctx)
        settled = sg.sem("settled")

        def attention_units(kind):
            out = []
            groups = {"lay": [(b, m) for b in ("moba", "sel", "win") for m in range(2)],
                      "na": [(b, m) for b in (0, 1) for m in range(2)],
                      "mla": [(b, m) for b in (0, 1) for m in range(2)]}[kind]
            for gi, (b, m) in enumerate(groups):
                for h in range(8):
                    u = dict(group=gi, branch=b, m=m, col=h, nk=S)
                    tok = slice(m * P, (m + 1) * P)
                    if kind == "lay":
                        u["nk"] = nk = (m + 1) * P
                        u["bias"] = alibi[:, h, m * P:m * P + nk]
                        if b == "moba":
                            r = slice((h % 2) * HD, (h % 2) * HD + HD)
                            u["s"] = [(qm[r, h // 2, tok], km[r, h // 2, 0:nk])]
                            u["v"] = [vm[:, t, h * HD:(h + 1) * HD] for t in range(m + 1)]
                        else:
                            w, g, j = (0 if b == "sel" else 1), h // 4, h % 4
                            r = slice(g * HD, g * HD + HD)
                            u["s"] = [(qn[r, j, tok], ksw[r, w, 0:nk])]
                            u["v"] = [vsw[:, t, w * P + g * HD:w * P + (g + 1) * HD] for t in range(m + 1)]
                    elif kind == "na":
                        hh_ = b * 8 + h
                        r = slice((hh_ % 2) * HD, (hh_ % 2) * HD + HD)
                        u["s"] = [(naq[r, hh_ // 2, tok], nak[r, hh_ // 2, :])]
                        u["v"] = [nav[:, t, hh_ * HD:(hh_ + 1) * HD] for t in range(2)]
                        first = 2 if m == 0 else 0
                        u["bias"] = rp[:, hh_ * 6 + first:hh_ * 6 + first + 4, :].rearrange("p a b -> p (a b)")
                    else:
                        hh_ = b * 8 + h
                        r = slice((hh_ % 2) * HD, (hh_ % 2) * HD + HD)
                        rr = slice((hh_ % 4) * 32, (hh_ % 4) * 32 + 32)
                        u["s"] = [(mq[r, hh_ // 2, tok], mk[r, hh_ // 2, :]),
                                  (mr[rr, hh_ // 4, tok], kr[rr, :])]
                        u["v"] = [mv[:, t, hh_ * HD:(hh_ + 1) * HD] for t in range(2)]
                        u["bias"] = mc[:, 0:S]
                    out.append(u)
            return out

        UNITS = {k: attention_units(k) for k in ("lay", "na", "mla")}
        S_BANK, PT_BANK, O_BANK, C_BANK = (4, 5, 6), (0, 1), (2, 3), (6, 7, 3, 2)

        def gbank(use):
            return use % 3

        def overfull(engine):
            return engine.value_load(over[0:1, 0:1], min_val=0, max_val=MORE)

        def uses_to(use):
            return sum(gbank(q) == gbank(use) for q in range(use + 1))

        block = ctx.enter_context(nc.Block())

        @block.sync
        def _(sp):
            e = Count(sg)

            def stream(phase, rep, base):
                for i in range(len(STEPS[phase])):
                    if RAW_NEED[phase][i] is not None:
                        sp.wait_ge(*e.at("raw_used", RAW_NEED[phase][i]))
                    r = RAW_AT[phase][i]
                    src = rep * len(STEPS[phase]) + base + i if not isinstance(rep, int) else base + i
                    sp.dma_start(raw[:, r, :], dram["ws"][src]).then_inc(*e.inc(f"raw_in{r}", 16))

            base = 0
            for p in ("pre", "lay", "na", "ffn", "mla", "moe"):
                if p == "lay":
                    sp.dma_start(x[:], dram["x"]).then_inc(*e.inc("x_in", 16))
                    sp.dma_start(lc[:], dram["lc"]).then_inc(*e.inc("lc_in", 16))
                if p == "pre":
                    e.enter(p)
                    sp.dma_start(par[:], dram["par"]).then_inc(*e.inc("par_in", 16))
                if p in REPS:
                    with sp.Fori(0, REPS[p]) as rep:
                        e.enter(p, rep)
                        stream(p, rep, base)
                else:
                    if p != "pre":
                        e.enter(p)
                    stream(p, 0, base)
                if p != "moe":
                    base += len(STEPS[p]) * REPS.get(p, 1)
            sp.wait_ge(*e.at("over", 0))
            count = overfull(sp)
            with sp.Fori(0, MORE) as rep:
                e.enter("more", rep)
                with sp.If(count > rep):
                    which = sp.value_load(over[0:1, bass.ds(rep + 1, 1)], min_val=0, max_val=NEXP - 1)
                    stream("more", which, base)
            e.enter("end")
            for m in range(MT):
                sp.wait_ge(*e.at("final", m + 1))
                sp.dma_start(dram["out"][:, m, :], xn_f[:, m, :]).then_inc(*e.inc("stored", 16))
            sp.wait_ge(*e.at("stored", MT, 16))

        @block.gpsimd
        def _(pool):
            g = nc.gpsimd
            e = Count(sg)
            e.enter("pre")
            g.memset(ones[:], 1.0).then_inc(*e.inc("consts"))
            g.memset(st[:], -0.5).then_inc(*e.inc("consts"))

            def rstd(sq_wait, spans):
                pool.wait_ge(*e.at("sq", sq_wait))
                pool.sem_inc(settled)
                for a, b, n in spans:
                    g.tensor_scalar(st[:, s_ms + a:s_ms + b], st[:, s_sq + a:s_sq + b],
                                    1.0 / n, EPS, ALU.mult, ALU.add).then_inc(*e.inc("mean_sq"))
                    pool.wait_ge(*e.last("mean_sq"))
                    pool.sem_inc(settled)
                a, b = spans[0][0], spans[-1][1]
                g.tensor_tensor(st[:, s_rs + a:s_rs + b], st[:, s_ms + a:s_ms + b],
                                st[:, s_half:s_half + b - a], ALU.pow).then_inc(*e.inc("rstd"))

            for name, n in (("x", MT), ("y", 1), ("split_used", SPL)):
                for _ in range(n):
                    g.memset(spare[:], 0.0).then_inc(*e.inc(name))
                    pool.wait_ge(*e.at(name, e.own[name]))
            pool.wait_ge(*e.at("consts", 2))
            with pool.Fori(0, 2) as rep:
                e.enter("lay", rep)
                rstd(2, [(0, 2, D)])
                rstd(3, [(2, 4, D)])
            e.enter("na")
            rstd(2, [(0, 2, D)])
            e.enter("ffn")
            rstd(2, [(0, 2, D)])
            e.enter("mla")
            rstd(2, [(0, 2, D)])
            rstd(6, [(2, 4, 256), (4, 6, 128)])
            e.enter("rt")
            rstd(2, [(0, 2, D)])
            e.enter("end")
            rstd(2, [(0, 2, D)])

        @block.tensor
        def _(pe):
            t = nc.tensor
            e = Count(sg)

            def mm3(out, lhs, rhs, start, stop):
                t.matmul(out, lhs[0], rhs[0], start=start, stop=False, skip_group_check=True)
                t.matmul(out, lhs[0], rhs[1], start=False, stop=False, skip_group_check=True)
                return t.matmul(out, lhs[1], rhs[0], start=False, stop=stop, skip_group_check=True)

            def arrived(n):
                pe.wait_ge(*e.at("raw_used", STEP_OF_SPLIT[e.phase][n] + 1))
                r = SPL_AT[e.phase][n]
                return wh[:, r, :], wl[:, r, :]

            used = {}

            def bank_free(b):
                if used.get(b, 0) or e.phase == "moe":
                    pe.wait_ge(*e.at(f"bank{b}", used.get(b, 0)))
                used[b] = used.get(b, 0) + 1

            def tok_slot(n, banks, width, first=True):
                for kh in range(2):
                    w = arrived(n + kh)
                    for m in range(MT):
                        if kh == 0 and first:
                            bank_free(banks[m])
                        for k in range(4):
                            kt = kh * 4 + k
                            lhs = [a[:, kt, m * P:(m + 1) * P] for a in (hh, hl)]
                            rhs = [a[:, k * width:(k + 1) * width] for a in w]
                            last = mm3(PS[:, banks[m], 0:width], lhs, rhs, kt == 0, kt == KT - 1)
                    last.then_inc(*e.inc("split_used"))

            def feat_slot(n, banks, order=(0, 1, 2, 3)):
                for kh in range(2):
                    w = arrived(n + kh)
                    for i, f in enumerate(order):
                        b = banks[i // 2]
                        if kh == 0 and i % 2 == 0:
                            bank_free(b)
                        for k in range(4):
                            kt = kh * 4 + k
                            lhs = [a[:, k * 512 + f * P:k * 512 + (f + 1) * P] for a in w]
                            last = mm3(PS[:, b, (i % 2) * S:(i % 2 + 1) * S], lhs, (hh[:, kt, :], hl[:, kt, :]),
                                       kt == 0 and i % 2 == 0, kt == KT - 1)
                    last.then_inc(*e.inc("split_used"))

            def ada(j):
                pe.wait_ge(*e.at("raw_used", [i for i, s in enumerate(STEPS[e.phase]) if s == ("ada", j, 1)][0] + 1))
                bank_free(3)
                a = acc[:, j % 2, :]
                if j % 6 < 4:
                    for c in range(4):
                        last = t.matmul(PS[:, 3, c:c + 1], a[:, c * P:(c + 1) * P], ones[:, 0:1],
                                        start=True, stop=True)
                else:
                    if j % 6 == 4:
                        pe.wait_ge(*e.at("brow", j // 6 + 1, 16))
                    t.matmul(PS[:, 3, :], ones[:], a, start=True, stop=False)
                    c = (j % 6 - 4) * 512
                    last = t.matmul(PS[:, 3, :], ones[0:1, :], brow[0:1, c:c + 512], start=False, stop=True)
                last.then_inc(*e.inc("ada_sum"))

            def turn(src, stage):
                for b in range(4):
                    for k in range(2):
                        for m in range(MT):
                            kt = 2 * b + k
                            c = (k * 2 + m) * P
                            last = t.transpose(PS[:, 4 + b, c:c + P], src[:, m, kt * P:(kt + 1) * P], ident)
                    last.then_inc(*e.inc("turned"))

            def attention(units, between={}):
                banks = range(4)

                def scores(i):
                    u = units[i]
                    if i >= 3:
                        pe.wait_ge(*e.at("logits", i - 2))
                    for j, (q, k) in enumerate(u["s"]):
                        last = t.matmul(PS[:, S_BANK[i % 3], 0:u["nk"]], q, k,
                                        start=j == 0, stop=j == len(u["s"]) - 1)
                    last.then_inc(*e.inc("scores"))

                def turn_probs(i):
                    u = units[i]
                    pe.wait_ge(*e.at("probs", i + 1))
                    if i >= 2:
                        pe.wait_ge(*e.at("pt", i - 1))
                    for c in range(u["nk"] // P):
                        last = t.transpose(PS[:, PT_BANK[i % 2], c * P:(c + 1) * P],
                                           pr[:, i % 3, c * P:(c + 1) * P], ident)
                    last.then_inc(*e.inc("probs_t"))

                def values(i):
                    u = units[i]
                    pe.wait_ge(*e.at("pt", i + 1))
                    if u["col"] == 0 and u["group"] >= 2:
                        pe.wait_ge(*e.at("o_used", u["group"] - 1))
                    nkt = u["nk"] // P
                    for c in range(nkt):
                        last = t.matmul(PS[:, O_BANK[u["group"] % 2], u["col"] * HD:(u["col"] + 1) * HD],
                                        pt[:, i % 2, c * P:(c + 1) * P], u["v"][c],
                                        start=c == 0, stop=c == nkt - 1)
                    last.then_inc(*e.inc("pv"))

                n = len(units)
                scores(0)
                scores(1)
                for b in banks:
                    if used.get(b, 0) > 0:
                        pe.wait_ge(*e.at(f"bank{b}", used.get(b, 0)))
                for i in range(n + 1):
                    if i in between:
                        between[i]()
                    if i + 2 < n:
                        scores(i + 2)
                    if i < n:
                        turn_probs(i)
                    if i >= 1:
                        values(i - 1)

            def out_proj(n):
                pe.wait_ge(*e.at("h", 8))
                for s in range(2):
                    tok_slot(n + 2 * s, (4 + s, 6 + s), 512, first=False)

            def ffn():
                def down(s):
                    w = arrived(ffn_down(s))
                    pe.wait_ge(*e.at("act", 2 * (s + 1)))
                    for k in range(2):
                        for m in range(MT):
                            lhs = [a[:, s % 2, k, m * P:(m + 1) * P] for a in (ah, al)]
                            for c in range(2):
                                rhs = [a[:, k * D + c * 512:k * D + (c + 1) * 512] for a in w]
                                last = mm3(PS[:, 4 + 2 * m + c, :], lhs, rhs,
                                           s == 0 and k == 0, s == FFN_SLOTS - 1 and k == 1)
                    last.then_inc(*e.inc("split_used"))

                for s in range(FFN_SLOTS):
                    feat_slot(ffn_up(s), (gbank(2 * s), gbank(2 * s + 1)), (0, 2, 1, 3))
                    if s >= 1:
                        ada(s - 1)
                        down(s - 1)
                ada(FFN_SLOTS - 1)
                down(FFN_SLOTS - 1)
                ada(FFN_SLOTS)

            def gather():
                for kt in range(KT):
                    for m in range(MT):
                        last = t.matmul(PS[:, 6 + kt // 4, (kt % 4) * P:(kt % 4 + 1) * P],
                                        xn_f[:, m, kt * P:(kt + 1) * P], sel[:, m, :],
                                        start=m == 0, stop=m == MT - 1)
                    if kt % 4 == 3:
                        last.then_inc(*e.inc("gathered"))

            def combine():
                for i, b in enumerate(C_BANK):
                    m, c = divmod(i, 2)
                    t.matmul(PS[:, b, :], selt[:, m * P:(m + 1) * P], ysb[:, c * 512:(c + 1) * 512],
                             start=True, stop=True).then_inc(*e.inc("combined"))

            def expert(alone=False):
                def up(s):
                    for kh in range(2):
                        w = arrived(moe_up(s) + kh)
                        for k in range(4):
                            kt = kh * 4 + k
                            last = mm3(PS[:, s % 2, :], (hh[:, kt, 0:P], hl[:, kt, 0:P]),
                                       [a[:, k * 512:(k + 1) * 512] for a in w], kt == 0, kt == KT - 1)
                        last.then_inc(*e.inc("split_used"))

                def turn_act(s):
                    pe.wait_ge(*e.at("act_tok", s + 1))
                    if s >= 1:
                        pe.wait_ge(*e.at("act_lo", s))
                    for f in range(2):
                        last = t.transpose(PS[:, 2, f * P:(f + 1) * P], hb[:, s % 2, f * P:(f + 1) * P], ident)
                    last.then_inc(*e.inc("act_turned"))

                def down(s):
                    w = arrived(moe_down(s))
                    pe.wait_ge(*e.at("act_lo", s + 1))
                    for k in range(2):
                        for c in range(2):
                            last = mm3(PS[:, 4 + c, :], (ah[:, s % 2, k, 0:P], al[:, s % 2, k, 0:P]),
                                       [a[:, k * D + c * 512:k * D + (c + 1) * 512] for a in w],
                                       s == 0 and k == 0, s == MOE_SLOTS - 1 and k == 1)
                    last.then_inc(*e.inc("split_used"))

                if alone:
                    pe.wait_ge(*e.at("sel", 1))
                    gather()
                pe.wait_ge(*e.at("x_lo", 2 if alone else 0))
                up(0)
                if not alone:
                    pe.wait_ge(*e.at("y_sb", 2))
                    pe.wait_ge(*e.at("sel_t", 0))
                    combine()
                    pe.wait_ge(*e.at("sel", 0))
                for m in range(MT):
                    last = t.transpose(PS[:, 4, m * P:(m + 1) * P], sel[:, m, :], ident)
                last.then_inc(*e.inc("sel_turned"))
                up(1)
                if not alone:
                    pe.wait_ge(*e.at("y_used", 4))
                pe.wait_ge(*e.at("sel_t", 1))
                turn_act(0)
                for s in range(2, MOE_SLOTS):
                    up(s)
                    turn_act(s - 1)
                    down(s - 2)
                if not alone:
                    pe.wait_ge(*e.at("sel", 1))
                    gather()
                turn_act(MOE_SLOTS - 1)
                down(MOE_SLOTS - 2)
                down(MOE_SLOTS - 1)
                if alone:
                    pe.wait_ge(*e.at("y_sb", 2))
                    combine()

            def experts():
                e.enter("go")
                pe.wait_ge(*e.at("rc", 0, 16))
                pe.wait_ge(*e.at("chosen", 0))
                ch = [rw[:, 240 + m * 8:248 + m * 8] for m in range(MT)]
                t.matmul(PS[:, 3, 0:8], before, ch[0], start=True, stop=True)
                t.matmul(PS[:, 3, 8:16], ones[:], ch[0], start=True, stop=False)
                t.matmul(PS[:, 3, 8:16], before, ch[1], start=False, stop=True)
                t.matmul(PS[:, 3, 16:24], ones[:], ch[0], start=True, stop=False)
                t.matmul(PS[:, 3, 16:24], ones[:], ch[1], start=False, stop=True).then_inc(*e.inc("ranked"))
                pe.wait_ge(*e.at("sel", 1))
                gather()
                with pe.Fori(0, NEXP) as rep:
                    e.enter("moe", rep)
                    expert()
                e.enter("fin")
                pe.wait_ge(*e.at("y_sb", 2))
                pe.wait_ge(*e.at("sel_t", 0))
                combine()
                count = overfull(pe)
                with pe.Fori(0, MORE) as rep:
                    e.enter("more", rep)
                    with pe.If(count > rep):
                        expert(alone=True)

            e.enter("pre")
            pe.wait_ge(*e.at("par_in", 1, 16))
            pe.wait_ge(*e.at("consts", 2))
            for j in range(6):
                ada(j)

            with pe.Fori(0, 2) as rep:
                e.enter("lay", rep)
                used.clear()
                pe.wait_ge(*e.at("xn", 2))
                turn(xn_l, 0)
                pe.wait_ge(*e.at("h", 4))
                for s in range(8):
                    b = (gbank(2 * s), gbank(2 * s + 1))
                    if s in (0, 1, 4, 5):
                        feat_slot(2 * s, b)
                    else:
                        tok_slot(2 * s, b, 280 if s == 6 else 512)
                    if 1 <= s <= 6:
                        ada(s - 1)
                def cmp1():
                    pe.wait_ge(*e.at("kk", 1))
                    ck = STEPS["lay"].index(("ck",))
                    rk = RAW_AT["lay"][ck]
                    fills = sum(r == rk for r in RAW_AT["lay"][:ck + 1])
                    pe.wait_ge(*e.at(f"raw_in{rk}", fills, 16))
                    pe.wait_ge(*e.at("lp", 1))
                    out = PS[:, 7, 0:6 * T_CMP].rearrange("p (g t) -> p g t", g=6)
                    for i in range(16):
                        last = t.matmul(out, raw[:, rk, i * P:(i + 1) * P],
                                        kk[:, 0:6, i:i + 8 * (T_CMP - 1) + 1:8], start=i == 0, stop=i == 15)
                    last.then_inc(*e.inc("cmp1"))

                def cmp2():
                    pe.wait_ge(*e.at("cmp_act", 1))
                    pe.sem_inc(settled)
                    for g in range(2):
                        t.matmul(PS[g * HD:(g + 1) * HD, 7, 0:T_CMP], LP["ck2"][0:HD, :],
                                 cw[0:HD, 64 + g * 15:64 + g * 15 + 15], start=True, stop=True)
                    for g in range(2):
                        last = t.matmul(PS[0:T_CMP, 3, g * HD:(g + 1) * HD],
                                        cw[HD:P, 64 + g * 15:64 + g * 15 + 15], LP["cv2"][HD:P, :],
                                        start=True, stop=True)
                    last.then_inc(*e.inc("cmp2"))

                def cmp_scores():
                    pe.wait_ge(*e.at("cmp_kv", 2))
                    pe.wait_ge(*e.at("lc_in", 0, 16))
                    for g in range(2):
                        t.matmul(PS[:, 7, g * HD:(g + 1) * HD], rep_sel[0:T_CMP, g, :],
                                 cw[0:T_CMP, 160 + g * HD:160 + (g + 1) * HD], start=True, stop=True)
                    for g in range(2):
                        for m in range(MT):
                            for j in range(4):
                                c = P + (2 * m + g) * 64 + j * 16
                                last = t.matmul(PS[:, 7, c:c + T_CMP],
                                                qn[g * HD:(g + 1) * HD, j, m * P:(m + 1) * P],
                                                cw[g * HD:(g + 1) * HD, 128:128 + T_CMP], start=True, stop=True)
                        last.then_inc(*e.inc("cscores"))
                        if g == 0:
                            pe.wait_ge(*e.last("cscores"))
                            pe.sem_inc(settled)

                def cmp_turn():
                    pe.wait_ge(*e.at("cprobs", 2))
                    for m in range(MT):
                        last = t.transpose(PS[:, 7, m * P:(m + 1) * P], ce[:, m, :], ident)
                    last.then_inc(*e.inc("cprobs_t"))

                def cmp_out(m):
                    if m == 0:
                        pe.wait_ge(*e.at("vb", 1))
                        pe.wait_ge(*e.at("cpt", 1))
                    else:
                        pe.wait_ge(*e.at("cout_used", 1))
                    t.matmul(PS[:, 7, :], ce[:, m, :], vb[:], start=True, stop=True).then_inc(*e.inc("cout"))

                attention(UNITS["lay"], {1: cmp1, 6: cmp2, 8: cmp_scores, 13: cmp_turn,
                                         16: lambda: cmp_out(0), 19: lambda: cmp_out(1)})
                pe.wait_ge(*e.at("y", 4))
                turn(y, 1)
                out_proj(16)

            e.enter("na")
            used.clear()
            pe.wait_ge(*e.at("xn", 2))
            turn(xn_n, 0)
            pe.wait_ge(*e.at("h", 4))
            for s in range(6):
                b = (gbank(2 * s), gbank(2 * s + 1))
                if s < 4:
                    feat_slot(2 * s, b)
                else:
                    tok_slot(2 * s, b, 512)
                if s >= 1:
                    ada(s - 1)
            ada(5)
            attention(UNITS["na"])
            pe.wait_ge(*e.at("o_used", 4))
            turn(nao, 1)
            out_proj(12)

            e.enter("ffn")
            used.clear()
            pe.wait_ge(*e.at("xn", 2))
            turn(xn_f, 0)
            pe.wait_ge(*e.at("h", 4))
            ffn()

            e.enter("mla")
            used.clear()
            pe.wait_ge(*e.at("xn", 2))
            turn(xn_m, 0)
            pe.wait_ge(*e.at("h", 4))
            tok_slot(0, (0, 1), 416, first=False)
            pe.wait_ge(*e.at("cn", 4))
            for k in range(4):
                for m in range(MT):
                    last = t.transpose(PS[:, 4 + k // 2, ((k % 2) * 2 + m) * P:((k % 2) * 2 + m + 1) * P],
                                       cn[:, m, k * P:(k + 1) * P], ident)
            last.then_inc(*e.inc("c_t"))
            pe.wait_ge(*e.at("c", 2))
            for half in range(2):
                w = arrived(2 + half)
                if half == 0:
                    pe.wait_ge(*e.at("down_used", 2))
                for f in range(8):
                    b = 4 * half + f // 2
                    for k in range(2):
                        lhs = [a[:, k * D + f * P:k * D + (f + 1) * P] for a in w]
                        last = mm3(PS[:, b, (f % 2) * S:(f % 2 + 1) * S], lhs, (hh[:, k, :], hl[:, k, :]),
                                   k == 0 and f % 2 == 0, k == 1)
                last.then_inc(*e.inc("split_used"))
            w = arrived(4)
            pe.wait_ge(*e.at("mq", 4))
            for f in range(8):
                lhs = [a[:, f * P:(f + 1) * P] for a in w]
                last = mm3(PS[:, f // 2, (f % 2) * S:(f % 2 + 1) * S], lhs, (hh[:, 2, :], hl[:, 2, :]),
                           f % 2 == 0, True)
            last.then_inc(*e.inc("mk_sum"))
            pe.wait_ge(*e.at("mr", 2))
            for m in range(MT):
                lhs = [a[:, 2, m * P:(m + 1) * P] for a in (hh, hl)]
                for c in range(2):
                    rhs = [a[:, D + c * 512:D + (c + 1) * 512] for a in w]
                    last = mm3(PS[:, 4 + 2 * m + c, :], lhs, rhs, True, True)
            last.then_inc(*e.inc("split_used"))
            pe.wait_ge(*e.at("mkv", 5))
            attention(UNITS["mla"])
            pe.wait_ge(*e.at("o_used", 4))
            turn(mo, 1)
            out_proj(5)

            e.enter("rt")
            used.clear()
            pe.wait_ge(*e.at("xn", 2))
            turn(xn_f, 0)
            pe.wait_ge(*e.at("h", 4))
            pe.wait_ge(*e.at("router_lo", 1))
            for kt in range(KT):
                last = mm3(PS[0:NEXP, 0, 0:S], [w[:, kt * NEXP:(kt + 1) * NEXP] for w in (wrh, wrl)],
                           (hh[:, kt, :], hl[:, kt, :]), kt == 0, kt == KT - 1)
            last.then_inc(*e.inc("router_t"))
            pe.wait_ge(*e.at("router_sb", 1))
            for m in range(MT):
                last = t.matmul(PS[:, 1, m * NEXP:(m + 1) * NEXP], xg[0:NEXP, m, :],
                                ident[0:NEXP, 0:NEXP], start=True, stop=True)
            last.then_inc(*e.inc("router"))

            experts()

        @block.scalar
        def _(act):
            a = nc.scalar
            e = Count(sg)
            done = [0]

            def hi_to(n):
                for i in range(done[0], min(n, SPLITS[e.phase])):
                    step = STEP_OF_SPLIT[e.phase][i]
                    r = RAW_AT[e.phase][step]
                    act.wait_ge(*e.at(f"raw_in{r}", sum(q == r for q in RAW_AT[e.phase][:step + 1]), 16))
                    if SPL_NEED[e.phase][i] is not None:
                        act.wait_ge(*e.at("split_used", SPL_NEED[e.phase][i]))
                    a.activation(wh[:, SPL_AT[e.phase][i], :], raw[:, r, :], ACT.Copy).then_inc(*e.inc("hi"))
                done[0] = max(done[0], min(n, SPLITS[e.phase]))

            def start(phase, rep=0):
                e.enter(phase, rep)
                done[0] = 0
                hi_to(1)

            def squares(xn):
                for m in range(MT):
                    if e.phase == "end":
                        act.wait_ge(*e.at("x_last", m + 1))
                    else:
                        act.wait_ge(*e.at("x", m + 1 - MT))
                    a.activation(xn[:, m, :], x[:, m, :], ACT.Square,
                                 accum_out=st[:, s_sq + m:s_sq + m + 1]).then_inc(*e.inc("sq"))
                if SPLITS[e.phase]:
                    hi_to(SPL)

            def h_hi(stage):
                def scaled(b):
                    act.wait_ge(*e.at("turned", b + 1))
                    if b == 3:
                        act.wait_ge(*e.at("h", 2))
                    for k in range(2):
                        kt = 2 * b + k
                        a.activation(hb[:, kt % 4, :], PS[:, 4 + b, k * S:(k + 1) * S], ACT.Identity,
                                     scale=ab[:, 0, kt:kt + 1], bias=ab[:, 1, kt:kt + 1]).then_inc(*e.inc("hb_act"))

                def hi(b):
                    a.activation(hh[:, 2 * b:2 * b + 2, :], hb[:, (2 * b) % 4:(2 * b) % 4 + 2, :],
                                 ACT.Copy).then_inc(*e.inc("h_hi"))

                if stage == 0:
                    scaled(1)
                    act.wait_ge(*e.at("hb", 1))
                    hi(0)
                    act.wait_ge(*e.at("hb_act", 2))
                    hi(1)
                    scaled(3)
                    act.wait_ge(*e.at("hb", 2))
                    hi(2)
                    act.wait_ge(*e.at("hb_act", 4))
                    hi(3)
                    return
                for b in range(4):
                    act.wait_ge(*e.at("turned", 5 + b))
                    a.activation(hh[:, 2 * b:2 * b + 2, :], PS[:, 4 + b, :].rearrange("p (k s) -> p k s", k=2),
                                 ACT.Copy).then_inc(*e.inc("h_hi"))

            def get_brow(unit):
                act.dma_start(brow[:], dram["brow"][unit]).then_inc(*e.inc("brow", 16))

            def ada_out(j, buf):
                act.wait_ge(*e.at("ada_sum", j + 1))
                j6 = j % 6
                if j6 < 4:
                    ins = a.activation(modc[:, buf, j6 * 4:j6 * 4 + 4], PS[:, 3, 0:4], ACT.Copy)
                else:
                    ins = a.activation(gate[buf][:, (j6 - 4) * 512:(j6 - 3) * 512], PS[:, 3, :], ACT.Copy)
                ins.then_inc(*e.inc("bank3"))

            def summed(n):
                act.wait_ge(*e.at("split_used", n + 2))

            def out_feat(s, dst, scale):
                summed(2 * s)
                for i in range(2):
                    b = gbank(2 * s + i)
                    src = PS[:, b, :].rearrange("p (k s) -> p k s", k=2)
                    a.activation(dst[:, 2 * i:2 * i + 2, :], src, ACT.Copy,
                                 scale=scale).then_inc(*e.inc(f"bank{b}"))

            def out_tok(s, dst):
                summed(2 * s)
                for m in range(MT):
                    b = gbank(2 * s + m)
                    w = dst.shape[2]
                    a.activation(dst[:, m, :], PS[:, b, 0:w], ACT.Copy).then_inc(*e.inc(f"bank{b}"))

            def exps(units, between={}):
                for i, u in enumerate(units):
                    if i in between:
                        between[i]()
                    act.wait_ge(*e.at("logits", i + 1))
                    if i >= 3:
                        act.wait_ge(*e.at("probs_t", i - 2))
                    c = i % 48
                    a.activation(pr[:, i % 3, 0:u["nk"]], lg[:, i % 3, 0:u["nk"]], ACT.Exp,
                                 bias=mn(c), scale=-1.0, accum_out=sm(c)).then_inc(*e.inc("probs"))

            def ffn():
                for s in range(FFN_SLOTS):
                    n = ffn_up(s)
                    hi_to(n + 2 + SPL)
                    summed(n)
                    for f in range(2):
                        q = 2 * s + f
                        if q >= 4:
                            act.wait_ge(*e.at("act", q - 3))
                        a.activation(hb[:, q % 4, :], PS[:, gbank(q), 0:S], ACT.Tanh,
                                     scale=0.5).then_inc(*e.inc("tanh"))
                    for f in range(2):
                        q = 2 * s + f
                        act.wait_ge(*e.at(f"bank{gbank(q)}", uses_to(q)))
                        if s >= 2:
                            act.wait_ge(*e.at("split_used", ffn_down(s - 2) + 1))
                        a.activation(ah[:, s % 2, f, :], hb[:, q % 4, :], ACT.Copy).then_inc(*e.inc("act_hi"))
                    if s >= 1:
                        if s == 7:
                            get_brow(5)
                        ada_out(s - 1, 1 if s - 1 < 6 else 2)
                        hi_to(ffn_down(s - 1) + 1 + SPL)
                hi_to(SPLITS["ffn"])
                ada_out(FFN_SLOTS - 1, 2)
                ada_out(FFN_SLOTS, 2)

            def x_hi():
                for i in range(2):
                    act.wait_ge(*e.at("x_f", i + 1))
                    a.activation(hh[:, 4 * i:4 * i + 4, 0:P], xg[:, 4 * i:4 * i + 4, :],
                                 ACT.Copy).then_inc(*e.inc("x_hi"))

            def keep_rows():
                act.wait_ge(*e.at("split_used", SPLITS["more"] if e.phase == "more" else 0))
                for c in range(2):
                    a.activation(ysb[:, c * 512:(c + 1) * 512], PS[:, 4 + c, :],
                                 ACT.Copy).then_inc(*e.inc("y_sb"))

            def expert(alone=False):
                def act_hi(s):
                    act.wait_ge(*e.at("act_turned", s + 1))
                    a.activation(ah[:, s % 2, :, 0:P], PS[:, 2, 0:S].rearrange("p (k s) -> p k s", k=2),
                                 ACT.Copy).then_inc(*e.inc("act_hi"))

                hi_to(2)
                if alone:
                    x_hi()
                else:
                    keep_rows()
                for s in range(MOE_SLOTS):
                    n = moe_up(s)
                    hi_to(n + 1 + SPL)
                    summed(n)
                    a.activation(hb[:, s % 2, :], PS[:, s % 2, 0:S], ACT.Tanh, scale=0.5).then_inc(*e.inc("tanh"))
                    if s == 0:
                        act.wait_ge(*e.at("sel_turned", 1))
                        a.activation(selt[:], PS[:, 4, 0:S], ACT.Copy).then_inc(*e.inc("sel_t"))
                    hi_to(n + 2 + SPL)
                    if s >= 1:
                        act_hi(s - 1)
                act_hi(MOE_SLOTS - 1)
                if alone:
                    keep_rows()
                else:
                    x_hi()

            def experts():
                e.enter("go")
                x_hi()
                with act.Fori(0, NEXP) as rep:
                    e.enter("moe", rep)
                    done[0] = 0
                    expert()
                e.enter("fin")
                keep_rows()
                act.wait_ge(*e.at("over", 0))
                count = overfull(act)
                with act.Fori(0, MORE) as rep:
                    e.enter("more", rep)
                    done[0] = 0
                    with act.If(count > rep):
                        expert(alone=True)

            e.enter("pre")
            get_brow(0)
            act.wait_ge(*e.at("par_in", 1, 16))
            act.wait_ge(*e.at("consts", 2))
            c2 = pcol("cc").rearrange("p (c k) -> p c k", c=2)
            a.activation(cs[:], c2, ACT.Tanh, scale=0.5).then_inc(*e.inc("cs_tanh"))
            for j in range(6):
                ada_out(j, 1)

            with act.Fori(0, 2) as rep:
                start("lay", rep)
                act.wait_ge(*e.at("x_in", 0, 16))
                squares(xn_l)
                act.wait_ge(*e.at("y", 0))
                act.dma_start(gpost[:], dram["gpost"][rep]).then_inc(*e.inc("gpost", 16))
                act.dma_start(brow[:], dram["brow"][rep + 1]).then_inc(*e.inc("brow", 16))
                h_hi(0)
                for s in range(8):
                    hi_to(min(2 * s + 2 + SPL, 17))
                    if s == 0:
                        out_feat(s, qm, -QS)
                    if s == 1:
                        out_feat(s, km, 1.0)
                    if s == 2:
                        out_tok(s, vm)
                    if s in (3, 7):
                        if s == 7:
                            act.wait_ge(*e.at("gg", 1))
                        z = zm if s == 3 else zn
                        summed(2 * s)
                        for m in range(MT):
                            a.activation(z[:, m, :], PS[:, gbank(2 * s + m), :], ACT.Tanh,
                                         scale=0.5).then_inc(*e.inc("z_tanh"))
                    if s == 4:
                        out_feat(s, qn, -QS)
                    if s == 5:
                        summed(2 * s)
                        b = gbank(2 * s + 1)
                        a.activation(ksw[:], PS[:, b, :].rearrange("p (k s) -> p k s", k=2),
                                     ACT.Copy).then_inc(*e.inc(f"bank{b}"))
                    if s == 6:
                        out_tok(s, vsw)
                    if 1 <= s <= 6:
                        ada_out(s - 1, 1)
                gl = vsw[:, :, 256:280]
                for b in range(3):
                    act.wait_ge(*e.at(f"bank{b}", sum(gbank(q) == b for q in range(16))))
                a.activation(gl, gl, ACT.Tanh, scale=0.5).then_inc(*e.inc("g_tanh"))
                hi_to(18)

                def cmp_tanh():
                    act.wait_ge(*e.at("cmp_u", 1))
                    a.activation(cw[:, 64:96], cw[:, 0:32], ACT.Tanh,
                                 scale=0.7978845608028654).then_inc(*e.inc("cmp_tanh"))

                def cmp_kv():
                    act.wait_ge(*e.at("cmp2", 1))
                    a.activation(cw[:, 128:128 + T_CMP], PS[:, 7, 0:T_CMP], ACT.Copy,
                                 scale=0.5).then_inc(*e.inc("cmp_kv"))
                    a.activation(cw[0:T_CMP, 160:288], PS[0:T_CMP, 3, 0:P], ACT.Copy,
                                 scale=0.5).then_inc(*e.inc("cmp_kv"))

                def cmp_exp():
                    act.wait_ge(*e.at("clogits", 1))
                    e8 = ce[:].rearrange("p m (h t) -> p (m h) t", t=16)[:, :, 0:T_CMP]
                    a.activation(e8, e8, ACT.Exp, scale=-1.0).then_inc(*e.inc("cexp"))

                exps(UNITS["lay"], {2: lambda: hi_to(19), 4: cmp_tanh, 7: cmp_kv, 11: cmp_exp})
                h_hi(1)
                hi_to(20)
                for c in range(2):
                    act.wait_ge(*e.at("split_used", 18 + 2 * c))
                    for m in range(MT):
                        a.activation(xn_l[:, m, c * 512:(c + 1) * 512], PS[:, 4 + 2 * m + c, :], ACT.Square,
                                     accum_out=st[:, 240 + 2 * m + c:241 + 2 * m + c]).then_inc(*e.inc("ysq"))

            start("na")
            squares(xn_n)
            act.dma_start(rp[:], dram["rp"]).then_inc(*e.inc("rp_in", 16))
            get_brow(3)
            h_hi(0)
            for s in range(6):
                hi_to(2 * s + 2 + SPL)
                if s < 2:
                    out_feat(s, naq[:, 4 * s:4 * s + 4, :], -QS)
                elif s < 4:
                    out_feat(s, nak[:, 4 * (s - 2):4 * (s - 2) + 4, :], 1.0)
                else:
                    out_tok(s, nav[:, :, (s - 4) * 512:(s - 3) * 512])
                if s >= 1:
                    ada_out(s - 1, 0)
            ada_out(5, 0)
            exps(UNITS["na"])
            h_hi(1)
            hi_to(16)

            start("ffn")
            squares(xn_f)
            get_brow(4)
            h_hi(0)
            ffn()

            start("mla")
            squares(xn_m)
            act.dma_start(mc[:], dram["mc"]).then_inc(*e.inc("mc", 16))
            h_hi(0)
            summed(0)
            for m in range(MT):
                a.activation(dsb[:, m, :], PS[:, m, 0:416], ACT.Copy).then_inc(*e.inc("down_used"))
            act.wait_ge(*e.at("down_used", 2))
            for m in range(MT):
                for i, (c0, c1) in enumerate(((0, 256), (256, 384))):
                    a.activation(cn[:, m, c0:c1], dsb[:, m, c0:c1], ACT.Square,
                                 accum_out=st[:,
                                              s_sq + 2 + 2 * i + m:s_sq + 3 + 2 * i + m]).then_inc(*e.inc("sq"))
            act.wait_ge(*e.at("c_f", 1))
            a.activation(hh[:, 0:3, :], hb[:, 0:3, :], ACT.Copy).then_inc(*e.inc("c_hi"))
            hi_to(5)
            act.wait_ge(*e.at("split_used", 3))
            for i in range(4):
                src = PS[:, i, :].rearrange("p (k s) -> p k s", k=2)
                a.activation(mq[:, 2 * i:2 * i + 2, :], src, ACT.Copy, scale=-MS).then_inc(*e.inc("mq"))
            act.wait_ge(*e.at("mk_sum", 1))
            for i in range(4):
                src = PS[:, i, :].rearrange("p (k s) -> p k s", k=2)
                a.activation(mk[:, 2 * i:2 * i + 2, :], src, ACT.Copy).then_inc(*e.inc("mkv"))
            hi_to(8)
            exps(UNITS["mla"])
            h_hi(1)
            hi_to(9)

            e.enter("rt")
            squares(xn_f)
            act.dma_start(fnorm[:], dram["fnorm"]).then_inc(*e.inc("fnorm", 16))
            act.dma_start(rc[:], dram["rc"]).then_inc(*e.inc("rc", 16))
            a.activation(wrh[:], pcol("router"), ACT.Copy).then_inc(*e.inc("router_hi"))
            h_hi(0)
            act.wait_ge(*e.at("router_t", 1))
            a.activation(xg[0:NEXP, 0:2, :], PS[0:NEXP, 0, 0:S].rearrange("p (m s) -> p m s", m=2),
                         ACT.Copy).then_inc(*e.inc("router_sb"))
            act.wait_ge(*e.at("rmax", 1))
            a.activation(rw[:, 0:16], rw[:, 0:16], ACT.Exp).then_inc(*e.inc("rexp"))

            experts()

            e.enter("end")
            squares(xn_f)

        @block.vector
        def _(dve):
            v = nc.vector
            e = Count(sg)
            done = [0]

            def link(ins):
                name = "dve" if e.phase != "end" else "dve_end"
                ins.then_inc(*e.inc(name))
                dve.wait_ge(*e.last(name))

            def raw_to(n):
                ph = e.phase
                for i in range(done[0], min(n, len(STEPS[ph]))):
                    step, r = STEPS[ph][i], RAW_AT[ph][i]
                    if step[0] == "w":
                        s = SPL_AT[ph][step[1]]
                        dve.wait_ge(*e.at("hi", step[1] + 1))
                        v.tensor_tensor(wl[:, s, :], raw[:, r, :], wh[:, s, :].bitcast(F32),
                                        ALU.subtract).then_inc(*e.inc("raw_used"))
                        dve.wait_ge(*e.last("raw_used"))
                    elif step[0] == "ada":
                        _, j, kh = step
                        dve.wait_ge(*e.at(f"raw_in{r}", sum(q == r for q in RAW_AT[ph][:i + 1]), 16))
                        dst = acc[:, j % 2, :]
                        if kh == 0:
                            if j >= 2:
                                dve.wait_ge(*e.at("ada_sum", j - 1))
                        c = cs[:, 1, :] if ph == "ffn" or ph == "na" else csc[:]
                        for k in range(4):
                            kt = kh * 4 + k
                            w = raw[:, r, k * 512:(k + 1) * 512]
                            if kt == 0:
                                ins = v.tensor_scalar(dst, w, c[:, kt:kt + 1], None, ALU.mult)
                            else:
                                ins = v.scalar_tensor_tensor(out=dst, in0=w, scalar=c[:, kt:kt + 1], in1=dst,
                                                             op0=ALU.mult, op1=ALU.add)
                            if k < 3:
                                link(ins)
                            else:
                                ins.then_inc(*e.inc("raw_used"))
                                dve.wait_ge(*e.last("raw_used"))
                    else:
                        return i
                    done[0] = i + 1

            def split_to(n):
                ph = e.phase
                n = min(n, SPLITS[ph])
                raw_to(STEP_OF_SPLIT[ph][n - 1] + 1)

            def start(phase, rep=0):
                e.enter(phase, rep)
                done[0] = 0

            def norm(xn, wa, wb):
                dve.wait_ge(*e.at("rstd", 1))
                for m in range(MT):
                    v.tensor_scalar(xn[:, m, :], x[:, m, :], st[:, s_rs + m:s_rs + m + 1], None,
                                    ALU.mult).then_inc(*e.inc("xn"))
                    dve.wait_ge(*e.last("xn"))

                def lo(b):
                    dve.wait_ge(*e.at("h_hi", b + 1))
                    v.tensor_tensor(hl[:, 2 * b:2 * b + 2, :], hb[:, (2 * b) % 4:(2 * b) % 4 + 2, :],
                                    hh[:, 2 * b:2 * b + 2, :].bitcast(F32), ALU.subtract).then_inc(*e.inc("h"))
                    dve.wait_ge(*e.last("h"))

                def scaled(b):
                    dve.wait_ge(*e.at("turned", b + 1))
                    for k in range(2):
                        kt = 2 * b + k
                        ins = v.tensor_scalar(hb[:, kt % 4, :], PS[:, 4 + b, k * S:(k + 1) * S],
                                              wa[:, kt:kt + 1], wb[:, kt:kt + 1], ALU.mult, ALU.add)
                        if k == 0:
                            link(ins)
                    ins.then_inc(*e.inc("hb"))
                    dve.wait_ge(*e.last("hb"))

                scaled(0)
                lo(0)
                scaled(2)
                lo(1)
                lo(2)
                lo(3)

            def make_ab(buf, bcol, gpre=None):
                dve.wait_ge(*e.at("bank3", 0))
                link(v.tensor_tensor(modc[:, buf, :], modc[:, buf, :], bcol, ALU.add))
                if gpre is not None:
                    link(v.scalar_tensor_tensor(out=ab[:, 0, :], in0=modc[:, buf, 8:16], scalar=1.0, in1=gpre,
                                                op0=ALU.add, op1=ALU.mult))
                else:
                    link(v.tensor_scalar(ab[:, 0, :], modc[:, buf, 8:16], 1.0, None, ALU.add))
                link(v.tensor_copy(ab[:, 1, :], modc[:, buf, 0:8]))

            def h_lo_psum():
                for b in range(4):
                    dve.wait_ge(*e.at("h_hi", 5 + b))
                    v.tensor_tensor(hl[:, 2 * b:2 * b + 2, :],
                                    PS[:, 4 + b, :].rearrange("p (k s) -> p k s", k=2),
                                    hh[:, 2 * b:2 * b + 2, :].bitcast(F32), ALU.subtract).then_inc(*e.inc("h"))
                    dve.wait_ge(*e.last("h"))

            def attention(units, finish, between={}):
                def logits(i):
                    u = units[i]
                    dve.wait_ge(*e.at("scores", i + 1))
                    if i >= 3:
                        dve.wait_ge(*e.at("probs", i - 2))
                    n = u["nk"]
                    dve.sem_inc(settled)
                    v.tensor_tensor_reduce(lg[:, i % 3, 0:n], u["bias"], PS[:, S_BANK[i % 3], 0:n],
                                           1.0, 3e38, ALU.add, ALU.min, mn(i % 48)).then_inc(*e.inc("logits"))
                    dve.wait_ge(*e.last("logits"))

                def copy_pt(i):
                    n = units[i]["nk"]
                    dve.wait_ge(*e.at("probs_t", i + 1))
                    if i >= 2:
                        dve.wait_ge(*e.at("pv", i - 1))
                    v.tensor_copy(pt[:, i % 2, 0:n], PS[:, PT_BANK[i % 2], 0:n]).then_inc(*e.inc("pt"))
                    dve.wait_ge(*e.last("pt"))

                n = len(units)
                logits(0)
                logits(1)
                for i in range(n):
                    if i in between:
                        between[i]()
                    if i + 2 < n:
                        logits(i + 2)
                    copy_pt(i)
                    if i % 8 == 2 and i > 8:
                        out_group(i // 8 - 1, units, finish)
                out_group(n // 8 - 1, units, finish)

            def out_group(g, units, finish):
                dve.wait_ge(*e.at("probs", 8 * g + 8))
                c = (8 * g) % 48
                link(v.reciprocal(rinv(0, 8), st[:, 96 + c:104 + c]))
                dve.wait_ge(*e.at("pv", 8 * g + 8))
                o = PS[:, O_BANK[g % 2], :].rearrange("p (h d) -> p h d", h=8)
                finish(units[8 * g], o, rinv(0, 8))

            def bc(w):
                return w.unsqueeze(2).broadcast_to([P, 8, HD])

            def update_x(g, done_by):
                for c in range(2):
                    dve.wait_ge(*e.at("split_used", done_by[c]))
                    half = slice(c * 512, (c + 1) * 512)
                    for m in range(MT):
                        tmp = scaled_y[:, m, half]
                        link(v.tensor_tensor(tmp, PS[:, 4 + 2 * m + c, :], g[:, half], ALU.mult))
                        ins = v.tensor_tensor(x[:, m, half], x[:, m, half], tmp, ALU.add)
                        if c == 0:
                            link(ins)
                        else:
                            ins.then_inc(*e.inc("x"))
                            dve.wait_ge(*e.last("x"))

            def ffn():
                for s in range(FFN_SLOTS):
                    n = ffn_up(s)
                    split_to(n + 2 + SPL)
                    dve.wait_ge(*e.at("split_used", n + 2))
                    for f in range(2):
                        q = 2 * s + f
                        b = gbank(q)
                        t_ = hb[:, q % 4, :]
                        dve.wait_ge(*e.at("tanh", q + 1))
                        link(v.scalar_tensor_tensor(out=t_, in0=t_, scalar=1.0, in1=PS[:, b, 0:S],
                                                    op0=ALU.add, op1=ALU.mult))
                        v.scalar_tensor_tensor(out=t_, in0=t_, scalar=0.5, in1=PS[:, b, S:2 * S],
                                               op0=ALU.mult, op1=ALU.mult).then_inc(*e.inc(f"bank{b}"))
                        dve.wait_ge(*e.at(f"bank{b}", uses_to(q)))
                    for f in range(2):
                        q = 2 * s + f
                        dve.wait_ge(*e.at("act_hi", q + 1))
                        v.tensor_tensor(al[:, s % 2, f, :], hb[:, q % 4, :],
                                        ah[:, s % 2, f, :].bitcast(F32), ALU.subtract).then_inc(*e.inc("act"))
                        dve.wait_ge(*e.last("act"))
                    if s >= 1:
                        split_to(ffn_down(s - 1) + 1 + SPL)
                raw_to(999)

            def x_f():
                for i in range(2):
                    dve.wait_ge(*e.at("gathered", i + 1))
                    for k in range(4):
                        kt = 4 * i + k
                        ins = v.tensor_scalar(xg[:, kt, :], PS[:, 6 + i, k * P:(k + 1) * P],
                                              ab[:, 0, kt:kt + 1], ab[:, 1, kt:kt + 1], ALU.mult, ALU.add)
                        if k < 3:
                            link(ins)
                    ins.then_inc(*e.inc("x_f"))
                    dve.wait_ge(*e.last("x_f"))

            def x_lo():
                for i in range(2):
                    dve.wait_ge(*e.at("x_hi", i + 1))
                    v.tensor_tensor(hl[:, 4 * i:4 * i + 4, 0:P], xg[:, 4 * i:4 * i + 4, :],
                                    hh[:, 4 * i:4 * i + 4, 0:P].bitcast(F32),
                                    ALU.subtract).then_inc(*e.inc("x_lo"))
                    dve.wait_ge(*e.last("x_lo"))

            def select(column, rnd):
                for m in range(MT):
                    ins = v.tensor_scalar(sel[:, m, :], row_no[:, rnd * P:(rnd + 1) * P],
                                          pos_of[:, m, column], None, ALU.is_equal)
                    if m == 0:
                        link(ins)
                ins.then_inc(*e.inc("sel"))
                dve.wait_ge(*e.last("sel"))

            def add_rows(column):
                for i, b in enumerate(C_BANK):
                    m, c = divmod(i, 2)
                    dve.wait_ge(*e.at("combined", i + 1))
                    part = ysum[:, m, c * 512:(c + 1) * 512]
                    v.scalar_tensor_tensor(out=part, in0=PS[:, b, :], scalar=wcol[:, m, column], in1=part,
                                           op0=ALU.mult, op1=ALU.add).then_inc(*e.inc("y_used"))
                    dve.wait_ge(*e.last("y_used"))

            def expert(own, other, alone=False):
                def act_lo(s):
                    dve.wait_ge(*e.at("act_hi", s + 1))
                    v.tensor_tensor(al[:, s % 2, :, 0:P], PS[:, 2, 0:S].rearrange("p (k s) -> p k s", k=2),
                                    ah[:, s % 2, :, 0:P].bitcast(F32), ALU.subtract).then_inc(*e.inc("act_lo"))
                    dve.wait_ge(*e.last("act_lo"))

                if alone:
                    select(other, 1)
                    split_to(2)
                    x_f()
                    x_lo()
                for s in range(MOE_SLOTS):
                    n = moe_up(s)
                    split_to(n + 1 + SPL)
                    dve.wait_ge(*e.at("tanh", s + 1))
                    t_ = hb[:, s % 2, :]
                    link(v.scalar_tensor_tensor(out=t_, in0=t_, scalar=1.0, in1=PS[:, s % 2, 0:S],
                                                op0=ALU.add, op1=ALU.mult))
                    v.scalar_tensor_tensor(out=t_, in0=t_, scalar=0.5, in1=PS[:, s % 2, S:2 * S],
                                           op0=ALU.mult, op1=ALU.mult).then_inc(*e.inc("act_tok"))
                    dve.wait_ge(*e.last("act_tok"))
                    if s == 0 and not alone:
                        add_rows(own)
                    split_to(n + 2 + SPL)
                    if s >= 1:
                        act_lo(s - 1)
                    if s == 2 and not alone:
                        dve.wait_ge(*e.at("sel_turned", 1))
                        select(other, 0)
                if alone:
                    act_lo(MOE_SLOTS - 1)
                    add_rows(own)
                else:
                    x_f()
                    act_lo(MOE_SLOTS - 1)
                    x_lo()

            def experts():
                e.enter("go")
                dve.wait_ge(*e.at("ranked", 1))
                for m in range(MT):
                    link(v.scalar_tensor_tensor(out=pos_of[:, m, 0:NEXP], in0=PS[:, 3, m * 8:m * 8 + 8],
                                                scalar=1.0, in1=rw[:, 240 + m * 8:248 + m * 8],
                                                op0=ALU.add, op1=ALU.mult))
                    link(v.tensor_scalar(pos_of[:, m, 0:NEXP], pos_of[:, m, 0:NEXP], -1.0, None, ALU.add))
                full, ahead, pairs, hit = rw[:, 256:264], rw[:, 264:272], rw[:, 64:128], rw[:, 272:280]
                found = rw[:, 280:281 + MORE]
                link(v.tensor_scalar(full, PS[:, 3, 16:24], P + 0.5, None, ALU.is_gt))
                link(v.tensor_tensor(pairs.rearrange("p (a b) -> p a b", a=8),
                                     pcol("lower").rearrange("p (a b) -> p a b", a=8),
                                     full.unsqueeze(1).broadcast_to([P, 8, 8]), ALU.mult))
                link(v.tensor_reduce(ahead, pairs.rearrange("p (a b) -> p a b", a=8), AX_X, ALU.add))
                link(v.tensor_reduce(found[:, 0:1], full, AX_X, ALU.add))
                for i in range(MORE):
                    link(v.scalar_tensor_tensor(out=hit, in0=ahead, scalar=float(i), in1=full,
                                                op0=ALU.is_equal, op1=ALU.mult))
                    link(v.tensor_tensor(hit, hit, row_no[:, 0:NEXP], ALU.mult))
                    link(v.tensor_reduce(found[:, i + 1:i + 2], hit, AX_X, ALU.add))
                v.tensor_copy(over[:], found).then_inc(*e.inc("over"))
                dve.wait_ge(*e.last("over"))
                v.memset(selt[:], 0.0).then_inc(*e.inc("sel_t"))
                dve.wait_ge(*e.last("sel_t"))
                select(slice(0, 1), 0)
                x_f()
                x_lo()
                with dve.Fori(0, NEXP) as rep:
                    start("moe", rep)
                    expert(bass.ds(rep, 1), bass.ds(rep + 1, 1))
                e.enter("fin")
                add_rows(slice(NEXP, NEXP + 1))
                count = overfull(dve)
                with dve.Fori(0, MORE) as rep:
                    start("more", rep)
                    with dve.If(count > rep):
                        which = dve.value_load(over[0:1, bass.ds(rep + 1, 1)], min_val=0, max_val=NEXP - 1)
                        expert(bass.ds(which + 1, 1), bass.ds(which, 1), alone=True)
                        dve.sem_inc(settled)

            e.enter("pre")
            c2 = pcol("cc").rearrange("p (c k) -> p c k", c=2)
            dve.wait_ge(*e.at("cs_tanh", 1))
            dve.wait_ge(*e.at("consts", 2))
            link(v.scalar_tensor_tensor(out=cs[:], in0=cs[:], scalar=1.0, in1=c2, op0=ALU.add, op1=ALU.mult))
            link(v.tensor_scalar(cs[:], cs[:], 0.5, None, ALU.mult))
            link(v.tensor_copy(csc[:], cs[:, 0, :]))
            raw_to(99)

            with dve.Fori(0, 2) as rep:
                start("lay", rep)
                dve.wait_ge(*e.at("par_in", 0, 16))
                dve.wait_ge(*e.at("x_in", 0, 16))
                link(v.tensor_copy(csc[:], cs[:, bass.ds(rep, 1), :].rearrange("p a b -> p (a b)")))
                v.tensor_copy(lpc[:],
                              lpall[:, bass.ds(rep, 1), :].rearrange("p a b -> p (a b)")).then_inc(*e.inc("lp"))
                dve.wait_ge(*e.last("lp"))
                split_to(1)
                make_ab(1, LP["bcol"], LP["gpre"])
                norm(xn_l, ab[:, 0, :], ab[:, 1, :])
                dve.wait_ge(*e.at("gpost", 1, 16))
                v.tensor_tensor(gate[0][:], gate[1][:], gpost[:], ALU.mult).then_inc(*e.inc("gg"))
                dve.wait_ge(*e.last("gg"))
                for s in range(8):
                    if s < 5:
                        split_to(2 * s + 2 + SPL)
                    if s == 7:
                        split_to(17)
                    if s in (3, 7):
                        z = zm if s == 3 else zn
                        for m in range(MT):
                            b = gbank(2 * s + m)
                            dve.wait_ge(*e.at("z_tanh", (2 if s == 7 else 0) + m + 1))
                            v.scalar_tensor_tensor(out=z[:, m, :], in0=z[:, m, :], scalar=1.0,
                                                   in1=PS[:, b, :], op0=ALU.add,
                                                   op1=ALU.mult).then_inc(*e.inc(f"bank{b}"))
                            dve.wait_ge(*e.at(f"bank{b}", uses_to(2 * s + m)))
                    if s == 5:
                        dve.wait_ge(*e.at("split_used", 12))
                        b = gbank(10)
                        for g in range(2):
                            src = PS[g * HD:(g + 1) * HD, b, :].rearrange("p (w s) -> p w s", w=2)
                            link(v.tensor_copy(kk[0:HD, g:g + 4:3, :], src[:, :, 0:S:2]))
                            ins = v.tensor_copy(kk[HD:P, g:g + 4:3, :], src[:, :, 1:S:2])
                            if g == 0:
                                link(ins)
                        ins.then_inc(*e.inc(f"bank{b}"))
                        dve.wait_ge(*e.at(f"bank{b}", uses_to(10)))
                        for w in range(2):
                            link(v.memset(kk[:, 3 * w + 2, :], 0.0))
                        link(v.tensor_copy(kk[:, 2, 0:16], LP["pek"]))
                        v.tensor_copy(kk[:, 5, 0:16], LP["pev"]).then_inc(*e.inc("kk"))
                        dve.wait_ge(*e.last("kk"))
                        split_to(16)
                dve.wait_ge(*e.at("g_tanh", 1))
                gl = vsw[:, :, 256:280]
                link(v.tensor_scalar(gl, gl, 0.5, 0.5, ALU.mult, ALU.add))
                def cmp_u():
                    dve.wait_ge(*e.at("cmp1", 1))
                    xc, u_ = cw[:, 0:32], cw[:, 416:448]
                    link(v.memset(cw[:, 0:128], 0.0))
                    for w in range(2):
                        r, c = slice(w * HD, (w + 1) * HD), w * 3 * T_CMP
                        link(v.tensor_copy(st[r, 232:233], PS[r, 7, c + 30:c + 31]))
                        link(v.tensor_scalar(xc[r, 0:30], PS[r, 7, c:c + 30], st[r, 232:233], None, ALU.add))
                    link(v.tensor_tensor(u_, xc, xc, ALU.mult))
                    link(v.tensor_scalar(u_, u_, 0.044715, 1.0, ALU.mult, ALU.add))
                    link(v.tensor_copy(cw[:, 288:320], xc))
                    v.tensor_tensor(xc, u_, xc, ALU.mult).then_inc(*e.inc("cmp_u"))
                    dve.wait_ge(*e.last("cmp_u"))

                def cmp_act():
                    dve.wait_ge(*e.at("cmp_tanh", 1))
                    v.scalar_tensor_tensor(out=cw[:, 64:96], in0=cw[:, 64:96], scalar=1.0,
                                           in1=cw[:, 288:320], op0=ALU.add,
                                           op1=ALU.mult).then_inc(*e.inc("cmp_act"))
                    dve.wait_ge(*e.last("cmp_act"))
                    v.memset(st[:, 236:237], 0.0).then_inc(*e.inc("raw_used"))
                    dve.wait_ge(*e.last("raw_used"))
                    done[0] = STEPS["lay"].index(("ck",)) + 1

                def cmp_logits():
                    dve.wait_ge(*e.at("cscores", 2))
                    dve.wait_ge(*e.at("lc_in", 0, 16))
                    link(v.memset(ce[:], 0.0))
                    for g in range(2):
                        ins = v.tensor_tensor(
                            vb[:].rearrange("p (h d) -> p h d", h=8)[:, 4 * g:4 * g + 4, :],
                            PS[:, 7, g * HD:(g + 1) * HD].unsqueeze(1).broadcast_to([P, 4, HD]),
                            mask8[:, 4 * g:4 * g + 4].unsqueeze(2).broadcast_to([P, 4, HD]), ALU.mult)
                        if g == 0:
                            link(ins)
                    ins.then_inc(*e.inc("vb"))
                    dve.wait_ge(*e.last("vb"))
                    l8 = ce[:].rearrange("p m (h t) -> p (m h) t", t=16)[:, :, 0:T_CMP]
                    sc = PS[:, 7, P:P + 256].rearrange("p (mh t) -> p mh t", t=16)[:, :, 0:T_CMP]
                    al8 = lcol("alibi_c").rearrange("p (mh t) -> p mh t", t=16)[:, :, 0:T_CMP]
                    link(v.tensor_tensor(l8, sc, al8, ALU.add))
                    link(v.tensor_reduce(rinv(0, 16), l8, AX_X, ALU.min))
                    v.tensor_tensor(l8, l8, rinv(0, 16).unsqueeze(2).broadcast_to([P, 16, T_CMP]),
                                    ALU.subtract).then_inc(*e.inc("clogits"))
                    dve.wait_ge(*e.last("clogits"))

                def cmp_probs():
                    dve.wait_ge(*e.at("cexp", 1))
                    ex = ce[:].rearrange("p m (h t) -> p (m h) t", t=16)[:, :, 0:T_CMP]
                    link(v.tensor_reduce(st[:, 240:256], ex, AX_X, ALU.add))
                    for m in range(MT):
                        em = ce[:, m, :].rearrange("p (h t) -> p h t", t=16)[:, :, 0:T_CMP]
                        v.tensor_tensor(em, em, ok_c[:, m, 0:T_CMP].unsqueeze(1).broadcast_to([P, 8, T_CMP]),
                                        ALU.mult).then_inc(*e.inc("cprobs"))
                        dve.wait_ge(*e.last("cprobs"))

                def cmp_pt():
                    dve.wait_ge(*e.at("cprobs_t", 1))
                    v.tensor_copy(ce[:].rearrange("p m t -> p (m t)"), PS[:, 7, 0:S]).then_inc(*e.inc("cpt"))
                    dve.wait_ge(*e.last("cpt"))

                def gate_of(m, c):
                    gates = vsw[:, m, 256:280].rearrange("p (h c) -> p h c", c=3)
                    return gates[:, :, c:c + 1].rearrange("p h c -> p (h c)")

                def cmp_y(m):
                    link(v.reciprocal(rinv(8, 16), st[:, 240 + 8 * m:248 + 8 * m]))
                    link(v.tensor_tensor(wgt(), rinv(8, 16), gate_of(m, 0), ALU.mult))
                    dve.wait_ge(*e.at("cout", m + 1))
                    v.tensor_tensor(y[:, m, 512:1024].rearrange("p (h d) -> p h d", h=8),
                                    PS[:, 7, :].rearrange("p (h d) -> p h d", h=8), bc(wgt()),
                                    ALU.mult).then_inc(*e.inc("cout_used"))
                    dve.wait_ge(*e.last("cout_used"))

                compressed = {3: cmp_u, 2: lambda: split_to(18), 4: lambda: split_to(19), 5: cmp_act,
                              10: cmp_logits, 12: cmp_probs, 15: cmp_pt, 18: lambda: cmp_y(0),
                              21: lambda: cmp_y(1)}

                def finish(u, o, ri):
                    m = u["m"]
                    t3 = tmpo[:].rearrange("p (h d) -> p h d", h=8)
                    if u["branch"] == "moba":
                        v.scalar_tensor_tensor(out=t3, in0=o, scalar=0.5, in1=bc(ri), op0=ALU.mult,
                                               op1=ALU.mult).then_inc(*e.inc("o_used"))
                        dve.wait_ge(*e.last("o_used"))
                        v.tensor_tensor(y[:, m, 0:512], tmpo[:], zm[:, m, :], ALU.mult).then_inc(*e.inc("y"))
                        dve.wait_ge(*e.last("y"))
                        return
                    c = 1 if u["branch"] == "sel" else 2
                    link(v.tensor_tensor(wgt(), ri, gate_of(m, c), ALU.mult))
                    v.tensor_tensor(t3, o, bc(wgt()), ALU.mult).then_inc(*e.inc("o_used"))
                    dve.wait_ge(*e.last("o_used"))
                    link(v.tensor_tensor(y[:, m, 512:1024], y[:, m, 512:1024], tmpo[:], ALU.add))
                    if c == 2:
                        v.scalar_tensor_tensor(out=y[:, m, 512:1024], in0=y[:, m, 512:1024], scalar=0.5,
                                               in1=zn[:, m,
                                                      :], op0=ALU.mult, op1=ALU.mult).then_inc(*e.inc("y"))
                        dve.wait_ge(*e.last("y"))

                attention(UNITS["lay"], finish, compressed)
                h_lo_psum()
                raw_to(999)
                for c in range(2):
                    half = slice(c * 512, (c + 1) * 512)
                    for m in range(MT):
                        dve.wait_ge(*e.at("ysq", 2 * c + m + 1))
                        link(v.tensor_tensor(scaled_y[:, m, half], PS[:, 4 + 2 * m + c, :], gate[0][:, half],
                                             ALU.mult))
                link(v.tensor_tensor(st[:, s_sq + 2:s_sq + 3], st[:, 240:241], st[:, 241:242], ALU.add))
                v.tensor_tensor(st[:, s_sq + 3:s_sq + 4], st[:, 242:243], st[:, 243:244],
                                ALU.add).then_inc(*e.inc("sq"))
                dve.wait_ge(*e.at("rstd", 2))
                for m in range(MT):
                    v.scalar_tensor_tensor(out=x[:, m, :], in0=scaled_y[:, m, :],
                                           scalar=st[:, s_rs + 2 + m:s_rs + 3 + m], in1=x[:, m, :],
                                           op0=ALU.mult, op1=ALU.add).then_inc(*e.inc("x"))
                    dve.wait_ge(*e.last("x"))

            start("na")
            split_to(1)
            make_ab(1, pcol("bcol", 0, 16))
            norm(xn_n, ab[:, 0, :], ab[:, 1, :])
            for s in range(6):
                split_to(min(2 * s + 2 + SPL, 15))
            dve.wait_ge(*e.at("rp_in", 1, 16))
            link(v.tensor_tensor(rp[:], pcol("namask").unsqueeze(1).broadcast_to([P, 96, 64]), rp[:], ALU.subtract))

            def finish_plain(dst):
                def finish(u, o, ri):
                    m, b = u["m"], u["branch"]
                    v.tensor_tensor(dst[:, m, b * 512:(b + 1) * 512].rearrange("p (h d) -> p h d", h=8),
                                    o, bc(ri), ALU.mult).then_inc(*e.inc("o_used"))
                    dve.wait_ge(*e.last("o_used"))
                return finish

            attention(UNITS["na"], finish_plain(nao))
            h_lo_psum()
            raw_to(999)
            update_x(gate[1], (14, 16))

            start("ffn")
            split_to(1)
            make_ab(0, pcol("bcol", 16, 32))
            norm(xn_f, ab[:, 0, :], ab[:, 1, :])
            ffn()
            update_x(gate[0], (SPLITS["ffn"], SPLITS["ffn"]))

            start("mla")
            split_to(1)
            make_ab(1, pcol("bcol", 32, 48))
            norm(xn_m, ab[:, 0, :], ab[:, 1, :])
            split_to(3)
            dve.wait_ge(*e.at("rstd", 2))
            dve.wait_ge(*e.at("down_used", 2))
            kt4 = hb[:, 3, 0:128]
            for m in range(MT):
                v.tensor_scalar(cn[:, m, 0:256], dsb[:, m, 0:256], st[:, s_rs + 2 + m:s_rs + 3 + m], None,
                                ALU.mult).then_inc(*e.inc("cn"))
                dve.wait_ge(*e.last("cn"))
                link(v.tensor_scalar(cn[:, m, 256:384], dsb[:, m, 256:384], st[:, s_rs + 4 + m:s_rs + 5 + m], None,
                                     ALU.mult))
                x1, x2 = dsb[:, m, 384:400], dsb[:, m, 400:416]
                cc, ss = pcol("kcos", m * 16, m * 16 + 16), pcol("ksin", m * 16, m * 16 + 16)
                q = [kt4[:, i * 16:(i + 1) * 16] for i in range(4)]
                for dst, p0, p1 in ((q[0], x1, cc), (q[1], x2, ss), (q[2], x1, ss), (q[3], x2, cc)):
                    link(v.tensor_tensor(dst, p0, p1, ALU.mult))
                k0 = cn[:, m, 384:512].rearrange("p (r i) -> p r i", r=4)
                link(v.tensor_tensor(k0[:, :, 0:16], q[0].unsqueeze(1).broadcast_to([P, 4, 16]),
                                     q[1].unsqueeze(1).broadcast_to([P, 4, 16]), ALU.subtract))
                v.tensor_tensor(k0[:, :, 16:32], q[2].unsqueeze(1).broadcast_to([P, 4, 16]),
                                q[3].unsqueeze(1).broadcast_to([P, 4, 16]), ALU.add).then_inc(*e.inc("cn"))
                dve.wait_ge(*e.last("cn"))
            dve.wait_ge(*e.at("c_t", 1))
            for k in range(3):
                ins = v.tensor_scalar(hb[:, k, :], PS[:, 4 + k // 2, (k % 2) * S:(k % 2 + 1) * S],
                                      pcol("lnorm", k, k + 1), None, ALU.mult)
                if k < 2:
                    link(ins)
            ins.then_inc(*e.inc("c_f"))
            dve.wait_ge(*e.last("c_f"))
            v.tensor_copy(kr[:], PS[:, 5, S:2 * S]).then_inc(*e.inc("c"))
            dve.wait_ge(*e.last("c"))
            dve.wait_ge(*e.at("c_hi", 1))
            v.tensor_tensor(hl[:, 0:3, :], hb[:, 0:3, :], hh[:, 0:3, :].bitcast(F32),
                            ALU.subtract).then_inc(*e.inc("c"))
            dve.wait_ge(*e.last("c"))
            split_to(5)
            dve.wait_ge(*e.at("split_used", 4))
            dve.wait_ge(*e.at("mc", 1, 16))
            tab = lambda i: mc[:, i * S:(i + 1) * S].unsqueeze(1).broadcast_to([P, 4, S])
            link(v.tensor_tensor(mt2[:], PS[:, 6:8, :].rearrange("p a b -> p (a b)").rearrange("p (k s) -> p k s", s=S),
                                 tab(2), ALU.mult))
            v.tensor_tensor(mr[:], PS[:, 4:6, :].rearrange("p a b -> p (a b)").rearrange("p (k s) -> p k s", s=S),
                            tab(1), ALU.mult).then_inc(*e.inc("mr"))
            dve.wait_ge(*e.last("mr"))
            v.tensor_tensor(mr[:], mr[:], mt2[:], ALU.add).then_inc(*e.inc("mr"))
            dve.wait_ge(*e.last("mr"))
            dve.wait_ge(*e.at("split_used", 5))
            v.tensor_copy(mv[:].rearrange("p m d -> p (m d)"),
                          PS[:, 4:8, :].rearrange("p a b -> p (a b)")).then_inc(*e.inc("mkv"))
            split_to(8)
            attention(UNITS["mla"], finish_plain(mo))
            h_lo_psum()
            raw_to(999)
            update_x(gate[1], (7, 9))

            e.enter("rt")
            make_ab(2, pcol("bcol", 48, 64))
            dve.wait_ge(*e.at("router_hi", 1))
            v.tensor_tensor(wrl[:], pcol("router"), wrh[:].bitcast(F32), ALU.subtract).then_inc(*e.inc("router_lo"))
            dve.wait_ge(*e.last("router_lo"))
            norm(xn_f, ab[:, 0, :], ab[:, 1, :])
            link(v.memset(ysum[:], 0.0))
            link(v.memset(wcol[:, :, 0:1], 0.0))
            link(v.memset(pos_of[:, :, NEXP:NEXP + 1], -1.0))
            r8 = rw[:, 0:16].rearrange("p (m x) -> p m x", m=2)
            spread = lambda c: rw[:, c:c + 2].unsqueeze(2).broadcast_to([P, 2, 8])
            dve.wait_ge(*e.at("router", 1))
            link(v.tensor_copy(rw[:, 0:16], PS[:, 1, 0:16]))
            link(v.tensor_reduce(rw[:, 16:18], r8, AX_X, ALU.max))
            v.tensor_tensor(r8, r8, spread(16), ALU.subtract).then_inc(*e.inc("rmax"))
            dve.wait_ge(*e.last("rmax"))
            dve.wait_ge(*e.at("rexp", 1))
            link(v.tensor_reduce(rw[:, 18:20], r8, AX_X, ALU.add))
            link(v.reciprocal(rw[:, 20:22], rw[:, 18:20]))
            link(v.tensor_tensor(r8, r8, spread(20), ALU.mult))
            gt, eq = xg[:, 2, :], xg[:, 3, :]
            chosen = rw[:, 240:256]
            for m in range(MT):
                other = r8[:, m].unsqueeze(1).broadcast_to([P, 8, 8])
                own = r8[:, m].unsqueeze(2).broadcast_to([P, 8, 8])
                c = slice(m * 64, (m + 1) * 64)
                link(v.tensor_tensor(gt[:, c].rearrange("p (a b) -> p a b", a=8), other, own, ALU.is_gt))
                link(v.tensor_tensor(eq[:, c].rearrange("p (a b) -> p a b", a=8), other, own, ALU.is_equal))
            link(v.tensor_tensor(eq.rearrange("p (m x) -> p m x", m=2), eq.rearrange("p (m x) -> p m x", m=2),
                                 pcol("lower").unsqueeze(1).broadcast_to([P, 2, 64]), ALU.mult))
            link(v.tensor_tensor(gt, gt, eq, ALU.add))
            link(v.tensor_reduce(rw[:, 24:40], gt.rearrange("p (a b) -> p a b", a=16), AX_X, ALU.add))
            link(v.tensor_scalar(chosen, rw[:, 24:40], 1.5, None, ALU.is_lt))
            v.tensor_tensor(rw[:, 0:16], rw[:, 0:16], chosen, ALU.mult).then_inc(*e.inc("chosen"))
            dve.wait_ge(*e.last("chosen"))
            link(v.tensor_reduce(rw[:, 40:42], r8, AX_X, ALU.add))
            link(v.reciprocal(rw[:, 42:44], rw[:, 40:42]))
            link(v.tensor_tensor(wcol[:, :, 1:NEXP + 1], r8, spread(42), ALU.mult))

            experts()

            e.enter("end")
            dve.wait_ge(*e.at("bank3", 0))
            for m in range(MT):
                tmp = hb[:].rearrange("p a b -> p (a b)")
                link(v.tensor_tensor(tmp, ysum[:, m, :], gate[2][:], ALU.mult))
                v.tensor_tensor(x[:, m, :], x[:, m, :], tmp, ALU.add).then_inc(*e.inc("x_last"))
                dve.wait_ge(*e.last("x_last"))
            dve.wait_ge(*e.at("rstd", 1))
            dve.wait_ge(*e.at("fnorm", 0, 16))
            for m in range(MT):
                v.scalar_tensor_tensor(out=xn_f[:, m, :], in0=x[:, m, :],
                                       scalar=st[:, s_rs + m:s_rs + m + 1], in1=fnorm[:],
                                       op0=ALU.mult, op1=ALU.mult).then_inc(*e.inc("final"))
                dve.wait_ge(*e.last("final"))
    return sg


def tables():
    f = np.float32
    p = np.arange(P)
    slopes = (2.0 ** (-8.0 * np.arange(1, 9) / 8)).astype(f)
    c = {}
    c["ident"] = np.eye(P, dtype=f)
    c["zeros"] = np.zeros((P, S), f)
    al = np.zeros((P, 8, 384), f)
    for m in range(MT):
        n = (m + 1) * P
        d = (m * P + p)[:, None] - np.arange(n)[None, :]
        b = slopes[None, :, None] * d[:, None, :]
        al[:, :, m * P:m * P + n] = np.where(d[:, None, :] >= 0, b, FAR)
    c["alibi"] = al.reshape(P, -1)
    ac = np.zeros((P, MT, 8, 16), f)
    ok = np.zeros((P, MT, 16), f)
    for m in range(MT):
        d = (m * P + p)[:, None] - (np.arange(16) * 16 + 31)[None, :]
        ac[:, m] = np.where(d[:, None, :] >= 0, slopes[None, :, None] * d[:, None, :], FAR)
        ok[:, m] = d >= 0
    c["alibi_c"] = ac.reshape(P, -1)
    c["ok_c"] = ok.reshape(P, -1)
    rs = np.zeros((P, 2, P), f)
    for g in range(2):
        for h in range(4 * g, 4 * g + 4):
            for t in range(T_CMP):
                rs[t, g, h * 16 + t] = 1.0
    c["rep_sel"] = rs.reshape(P, -1)
    c["mask8"] = (p[:, None] // 16 == np.arange(8)[None, :]).astype(f)
    col = p % 64
    first = np.clip(col - 8, 0, 48)[:, None]
    kc = np.arange(64)[None, :]
    c["namask"] = np.where((kc >= first) & (kc < first + 16), 0.0, FAR).astype(f)
    t = np.arange(S)
    inv = (10000.0 ** (-np.arange(8, dtype=f) / 8)).astype(f)
    ang = np.concatenate([(t // 64).astype(f)[:, None] * inv, (t % 64).astype(f)[:, None] * inv], axis=1)
    cos, sin = np.cos(ang).astype(f), np.sin(ang).astype(f)
    c["kcos"] = cos.reshape(MT, P, 16).transpose(1, 0, 2).reshape(P, 32)
    c["ksin"] = sin.reshape(MT, P, 16).transpose(1, 0, 2).reshape(P, 32)
    i = p % 32
    c["qcos"] = (-MS * cos[:, i % 16].T).astype(f)
    c["qsin"] = (np.where(i < 16, MS, -MS)[:, None] * sin[:, i % 16].T).astype(f)
    c["lower"] = np.broadcast_to(np.tril(np.ones((8, 8), f), -1).reshape(1, 64), (P, 64))
    return c


def kernel(**inputs):
    import concourse.bacc as bacc
    from concourse.bass_utils import run_bass_kernel_spmd

    a = {k: np.asarray(v) for k, v in inputs.items()}
    f = np.float32

    def cols(vec):
        return np.ascontiguousarray(vec.reshape(-1, P).T)

    def ktiles(w):
        n = w.shape[0] // P
        return w.reshape(n, P, -1).transpose(1, 0, 2).reshape(P, -1)

    ws = np.zeros((NSTEPS, P, STEP), f)
    pos = [0]

    def put(block):
        ws[pos[0], :, :block.shape[1]] = block
        pos[0] += 1

    def halves(w):
        return [ktiles(w[:512]), ktiles(w[512:])]

    def emit(phase, splits, ada, ck=None):
        for step in STEPS[phase]:
            if step[0] == "w":
                put(splits[step[1]])
            elif step[0] == "ada":
                u, j = divmod(step[1], 6)
                put(halves(ada[u][:, j * 512:(j + 1) * 512])[step[2]])
            else:
                put(ck)

    units = [a["w_ada"][0], a["w_ada"][1]]
    bias = [a["b_ada"][0], a["b_ada"][1]]
    for l in range(2):
        for h in range(2):
            units.append(a["w_ada_2"][l][:, h * 3072:(h + 1) * 3072])
            bias.append(a["b_ada_2"][l][h * 3072:(h + 1) * 3072])

    def mlp_blocks(gu, down, slots, lag):
        n = slots * 256
        ups = [np.concatenate([gu[:, s * 256:(s + 1) * 256], gu[:, n + s * 256:n + (s + 1) * 256]], axis=1)
               for s in range(slots)]
        out = list(halves(ups[0]))
        for s in range(1, slots):
            out += halves(ups[s])
            if s >= lag:
                out.append(ktiles(down[(s - lag) * 256:(s - lag + 1) * 256]))
        return out + [ktiles(down[s * 256:(s + 1) * 256]) for s in range(slots - lag, slots)]

    emit("pre", [], [units[0]])
    nsa = np.concatenate([np.arange(h * HD, (h + 1) * HD) for j in range(4) for h in (j, 4 + j)])
    for l in range(2):
        w = a["w_in"][l]
        q, kvo = w[:, 2048:2560][:, nsa], 2560
        part = lambda i: w[:, kvo + i * P:kvo + (i + 1) * P]
        slots = [w[:, 0:512], w[:, 512:1024], w[:, 1024:1536], w[:, 1536:2048], q,
                 np.concatenate([part(0), part(1), part(2), part(4)], axis=1),
                 np.concatenate([part(3), part(5), w[:, 3328:3352]], axis=1), w[:, 3352:3864],
                 a["w_out"][l][:, 0:512], a["w_out"][l][:, 512:1024]]
        ck = np.stack([ktiles(a[n][l]).reshape(P, 16, HD) for n in ("w_ck1", "w_cv1")], axis=2).reshape(P, -1)
        emit("lay", [b for s in slots for b in halves(s)], [units[l + 1]], ck)
    w, wo = a["na_w_qkv_2"][0], a["na_w_o_2"][0]
    slots = [w[:, s * 512:(s + 1) * 512] for s in range(6)] + [wo[:, 0:512], wo[:, 512:1024]]
    emit("na", [b for s in slots for b in halves(s)], [units[3]])
    emit("ffn", mlp_blocks(a["ffn_w_gu_2"][0], a["ffn_w_down_2"][0], FFN_SLOTS, 1), [units[4], units[5]])
    uq = a["mla_w_uq_2"][0].reshape(256, 16, 96)
    nope, r1, r2 = uq[:, :, :64], uq[:, :, 64::2], uq[:, :, 65::2]
    ukv = a["mla_w_ukv_2"][0].reshape(P, 16, 2, 64)
    down = a["mla_w_down_2"][0]
    down = np.concatenate([down[:, :384], down[:, 384::2], down[:, 385::2]], axis=1)
    wo = a["mla_w_o_2"][0]
    emit("mla", halves(down) + [
        ktiles(nope.reshape(256, 1024)),
        ktiles(np.concatenate([np.concatenate([r1, r2], axis=2).reshape(256, 512),
                               np.concatenate([r2, r1], axis=2).reshape(256, 512)], axis=1)),
        np.concatenate([ukv[:, :, 0].reshape(P, 1024), ukv[:, :, 1].reshape(P, 1024)], axis=1),
    ] + halves(wo[:, 0:512]) + halves(wo[:, 512:1024]), [])
    for x in range(NEXP):
        emit("moe", mlp_blocks(a["moe_w_gu_2"][0, x], a["moe_w_down_2"][0, x], MOE_SLOTS, 2), [])
    assert pos[0] == NSTEPS

    c = tables()

    def rows64(w, first):
        out = np.zeros((P, w.shape[1]), f)
        out[first:first + HD] = w
        return out

    lp = np.stack([np.concatenate([
        cols(a["g_pre"][l]), cols(bias[l][:2048]), ktiles(a["pe_k"][l].reshape(-1, 1)),
        ktiles(a["pe_v"][l].reshape(-1, 1)), rows64(a["w_ck2"][l], 0), rows64(a["w_cv2"][l], HD)], axis=1)
        for l in range(2)], axis=1)
    c["lpall"] = lp.reshape(P, -1)
    c["bcol"] = np.concatenate([cols(bias[u][:2048]) for u in range(2, 6)], axis=1)
    c["cc"] = np.concatenate([cols(a["c"][0]), cols(a["c_2"][0])], axis=1)
    c["lnorm"] = np.concatenate([cols(a["mla_q_norm_2"][0]), cols(a["mla_kv_norm_2"][0])], axis=1)
    c["router"] = ktiles(a["moe_w_router_2"][0])
    par_names = ["ident", "namask", "kcos", "ksin", "lower", "lpall", "bcol", "cc",
                 "lnorm", "router"]
    lc_names = ["alibi", "alibi_c", "ok_c", "rep_sel", "mask8"]
    dc = np.clip(np.arange(64)[None, :] - (np.arange(P) % 64)[:, None] + 15, 0, 30)
    dr = np.arange(6)[None, :] + 5 - (np.arange(P) // 64)[:, None]
    rp = a["na_rpb_2"][0][:, dr[:, :, None], dc[:, None, :]].transpose(1, 0, 2, 3).reshape(P, 96, 64)
    arrays = {
        "ws": ws,
        "x": a["x"][0].reshape(MT, P, D).transpose(1, 0, 2),
        "par": np.concatenate([c[n] for n in par_names], axis=1),
        "lc": np.concatenate([c[n] for n in lc_names], axis=1),
        "rp": rp,
        "brow": np.stack([b[2048:] for b in bias])[:, None, :],
        "gpost": np.ascontiguousarray(np.broadcast_to(a["g_post"][:, None, :], (2, P, D))),
        "mc": np.concatenate([c["zeros"], c["qcos"], c["qsin"]], axis=1),
        "rc": np.concatenate([np.broadcast_to(np.arange(S, dtype=f), (P, S)),
                              (np.arange(P)[:, None] < np.arange(P)[None, :]).astype(f)], axis=1),
        "fnorm": np.ascontiguousarray(np.broadcast_to(a["final_norm_2"][None, :], (P, D))),
    }
    arrays = {k: np.ascontiguousarray(v, dtype=f) for k, v in arrays.items()}

    nc = bacc.Bacc("TRN2", target_bir_lowering=False, num_devices=1)
    dram = {k: nc.dram_tensor(f"in_{k}", v.shape, F32, kind="ExternalInput").ap() for k, v in arrays.items()}
    dram["out"] = nc.dram_tensor("out_0", (P, MT, D), F32, kind="ExternalOutput").ap()
    dram["par_cols"] = [(n, c[n].shape[1]) for n in par_names]
    dram["lc_cols"] = [(n, c[n].shape[1]) for n in lc_names]
    build(nc, dram)
    r = run_bass_kernel_spmd(nc, [{f"in_{k}": v for k, v in arrays.items()}], core_ids=[0])
    return r.results[0]["out_0"].transpose(1, 0, 2).reshape(1, S, D)
```
